# Optimizing a Trainium2 kernel written in Bass

```python
import jax, jax.numpy as jnp
from jax import lax
import numpy as np

D_MODEL = 1024
BATCH = 1
SEQ = 1024
DEPTH = 1

CHUNK = 64
D_RNN = 1280
N_LRU_BLOCKS = 16
LRU_BLOCK = D_RNN // N_LRU_BLOCKS
CONV_WIDTH = 4
LRU_C = 8.0
N_HEADS = 16
N_KV_HEADS = 4
HEAD_DIM = 64
Q_GROUP = N_HEADS // N_KV_HEADS
WINDOW = 128
WINDOW_CHUNKS = WINDOW // CHUNK
D_ATTN = N_HEADS * HEAD_DIM
D_KV = N_KV_HEADS * HEAD_DIM
D_FF = ((-(-8 * D_MODEL // 3)) + 255) // 256 * 256
RMS_EPS = 1e-6
IN_SPLITS = [D_RNN, D_RNN, D_ATTN, D_KV, D_KV, D_MODEL, D_MODEL]
D_IN = sum(IN_SPLITS)

kernel_name = "hybrid_rglru_swa_sink_alibi_sandwich"

def rms_norm(x, g):
    xf = x.astype(jnp.float32)
    y = xf * lax.rsqrt(jnp.mean(xf * xf, axis=-1, keepdims=True) + RMS_EPS)
    return (y * g.astype(jnp.float32)).astype(x.dtype)

def _lru_combine(left, right):
    a_l, b_l = left
    a_r, b_r = right
    return a_l * a_r, a_r * b_l + b_r

def rg_lru_branch(u, conv_w, conv_b, w_rg, b_rg, w_ig, b_ig, lru_lambda):
    B, S, _ = u.shape
    u = lax.conv_general_dilated(
        u, conv_w[:, None, :].astype(u.dtype), window_strides=(1,),
        padding=[(CONV_WIDTH - 1, 0)], dimension_numbers=("NWC", "WIO", "NWC"),
        feature_group_count=D_RNN) + conv_b
    ub = u.reshape(B, S, N_LRU_BLOCKS, LRU_BLOCK)
    r = jax.nn.sigmoid(jnp.einsum("bsnc,ncd->bsnd", ub, w_rg).reshape(B, S, D_RNN) + b_rg)
    i = jax.nn.sigmoid(jnp.einsum("bsnc,ncd->bsnd", ub, w_ig).reshape(B, S, D_RNN) + b_ig)
    log_a = -LRU_C * r.astype(jnp.float32) * jax.nn.softplus(-lru_lambda.astype(jnp.float32))
    a = jnp.exp(log_a)
    b = jnp.sqrt(-jnp.expm1(2.0 * log_a)) * (i * u).astype(jnp.float32)
    _, h = lax.associative_scan(_lru_combine, (a, b), axis=1)
    return h.astype(u.dtype)

def _shift_chunks(t, s):
    if s == 0:
        return t
    pad = [(0, 0), (s, 0)] + [(0, 0)] * (t.ndim - 2)
    return jnp.pad(t, pad)[:, : t.shape[1]]

def sliding_window_sink_attention(q, k, v, attn_sinks):
    B, S, _ = q.shape
    NC = S // CHUNK
    KB = WINDOW_CHUNKS * CHUNK
    q = q.reshape(B, NC, CHUNK, N_KV_HEADS, Q_GROUP, HEAD_DIM)
    k = k.reshape(B, NC, CHUNK, N_KV_HEADS, HEAD_DIM)
    v = v.reshape(B, NC, CHUNK, N_KV_HEADS, HEAD_DIM)
    kb = jnp.concatenate([_shift_chunks(k, s) for s in reversed(range(WINDOW_CHUNKS))], axis=2)
    vb = jnp.concatenate([_shift_chunks(v, s) for s in reversed(range(WINDOW_CHUNKS))], axis=2)
    scale = HEAD_DIM ** -0.5
    scores = jnp.einsum("bcqkgd,bcskd->bckgqs", q, kb).astype(jnp.float32) * scale
    slopes = jnp.exp2(-8.0 * (jnp.arange(N_HEADS, dtype=jnp.float32) + 1.0) / N_HEADS)
    qi = jnp.arange(CHUNK)[:, None]
    kj = jnp.arange(KB)[None, :]
    dist = jnp.abs(qi + (WINDOW_CHUNKS - 1) * CHUNK - kj).astype(jnp.float32)
    alibi = (-slopes[:, None, None] * dist).reshape(N_KV_HEADS, Q_GROUP, CHUNK, KB)
    scores = scores + alibi
    src_chunk = jnp.arange(NC)[:, None] - (WINDOW_CHUNKS - 1) + kj // CHUNK
    valid = src_chunk >= 0
    scores = jnp.where(valid[None, :, None, None, None, :], scores, -jnp.inf)
    sink = jnp.broadcast_to(attn_sinks.astype(jnp.float32).reshape(1, 1, N_KV_HEADS, Q_GROUP, 1, 1),
                            scores.shape[:-1] + (1,))
    probs = jax.nn.softmax(jnp.concatenate([scores, sink], axis=-1), axis=-1)[..., :-1]
    out = jnp.einsum("bckgqs,bcskd->bcqkgd", probs.astype(v.dtype), vb)
    return out.reshape(B, S, D_ATTN)

def setup_inputs(seed: int = 0) -> dict:
    key = jax.random.key(seed)
    ks = jax.random.split(key, 24)
    f32 = jnp.float32
    L = DEPTH

    def nrm(k, shape, fan_in):
        return jax.random.normal(k, shape, f32) * (fan_in ** -0.5)

    def gain(k, shape):
        return 1.0 + 0.05 * jax.random.normal(k, shape, f32)

    u = jax.random.uniform(ks[9], (L, D_RNN), f32, 0.9, 0.999)
    a0 = u ** (1.0 / LRU_C)
    lru_lambda = jnp.log(a0) - jnp.log1p(-a0)
    return {
        "x": jax.random.normal(ks[0], (BATCH, SEQ, D_MODEL), f32),
        "norm_pre_mix": gain(ks[1], (L, D_MODEL)),
        "w_in": nrm(ks[2], (L, D_MODEL, D_IN), D_MODEL),
        "conv_w": nrm(ks[3], (L, CONV_WIDTH, D_RNN), CONV_WIDTH),
        "conv_b": 0.02 * jax.random.normal(ks[4], (L, D_RNN), f32),
        "w_rg": nrm(ks[5], (L, N_LRU_BLOCKS, LRU_BLOCK, LRU_BLOCK), LRU_BLOCK),
        "b_rg": 0.02 * jax.random.normal(ks[6], (L, D_RNN), f32),
        "w_ig": nrm(ks[7], (L, N_LRU_BLOCKS, LRU_BLOCK, LRU_BLOCK), LRU_BLOCK),
        "b_ig": 0.02 * jax.random.normal(ks[8], (L, D_RNN), f32),
        "lru_lambda": lru_lambda,
        "attn_sinks": 0.5 * jax.random.normal(ks[10], (L, N_HEADS), f32),
        "w_lru_br": nrm(ks[11], (L, D_RNN, D_MODEL), D_RNN),
        "w_attn_br": nrm(ks[12], (L, D_ATTN, D_MODEL), D_ATTN),
        "b_gate": 0.02 * jax.random.normal(ks[13], (L, 2 * D_MODEL), f32),
        "w_out": nrm(ks[14], (L, D_MODEL, D_MODEL), D_MODEL),
        "norm_post_mix": gain(ks[15], (L, D_MODEL)),
        "norm_pre_ffn": gain(ks[16], (L, D_MODEL)),
        "w_ffn_gate": nrm(ks[17], (L, D_MODEL, D_FF), D_MODEL),
        "w_ffn_up": nrm(ks[18], (L, D_MODEL, D_FF), D_MODEL),
        "w_ffn_down": nrm(ks[19], (L, D_FF, D_MODEL), D_FF),
        "norm_post_ffn": gain(ks[20], (L, D_MODEL)),
    }

def reference(x, norm_pre_mix, w_in, conv_w, conv_b, w_rg, b_rg, w_ig, b_ig, lru_lambda,
              attn_sinks, w_lru_br, w_attn_br, b_gate, w_out, norm_post_mix,
              norm_pre_ffn, w_ffn_gate, w_ffn_up, w_ffn_down, norm_post_ffn):
    bounds = [0] + [int(c) for c in np.cumsum(IN_SPLITS)]
    for l in range(DEPTH):
        h = rms_norm(x, norm_pre_mix[l])
        proj = h @ w_in[l]
        lru_u, lru_y, q, k, v, g_lru_pre, g_attn_pre = [
            proj[..., bounds[j]:bounds[j + 1]] for j in range(len(IN_SPLITS))]
        g_lru = jax.nn.sigmoid(g_lru_pre + b_gate[l, :D_MODEL])
        g_attn = jax.nn.sigmoid(g_attn_pre + b_gate[l, D_MODEL:])

        lru_h = rg_lru_branch(lru_u, conv_w[l], conv_b[l], w_rg[l], b_rg[l],
                              w_ig[l], b_ig[l], lru_lambda[l])
        lru_out = lru_h * jax.nn.gelu(lru_y)
        attn_out = sliding_window_sink_attention(q, k, v, attn_sinks[l])

        merged = g_lru * (lru_out @ w_lru_br[l]) + g_attn * (attn_out @ w_attn_br[l])
        mix = merged @ w_out[l]
        x = x + rms_norm(mix, norm_post_mix[l])

        h = rms_norm(x, norm_pre_ffn[l])
        f = (jax.nn.silu(h @ w_ffn_gate[l]) * (h @ w_ffn_up[l])) @ w_ffn_down[l]
        x = x + rms_norm(f, norm_post_ffn[l])
    return x


_drawn_inputs = setup_inputs


def setup_inputs(seed=0):
    import zlib

    import numpy as np

    out = dict(_drawn_inputs(seed))
    spreads = {}
    factors = {'b_rg': 8.0, 'b_ig': 8.0, 'b_gate': 8.0}
    for name, (base, spread) in spreads.items():
        noise = np.random.default_rng([zlib.crc32(name.encode()), seed]).standard_normal(out[name].shape)
        drawn = base * np.exp(spread * noise) if base else spread * noise
        out[name] = __import__('jax').numpy.asarray(drawn.astype(out[name].dtype))
    for name, factor in factors.items():
        out[name] = (out[name] * factor).astype(out[name].dtype)
    return out
```

```python
from contextlib import ExitStack

import numpy as np

import concourse.bass as bass
from concourse import mybir

F32 = mybir.dt.float32
F32R = mybir.dt.float32r
ACT = mybir.ActivationFunctionType
ALU = mybir.AluOpType
AX_X = mybir.AxisListType.X

P = 128
D = 1024
KD = D // P
SEQ = 1024
T = 512
HALVES = SEQ // T
D_RNN = 1280
KR = D_RNN // P
N_BLK = 16
BLK = D_RNN // N_BLK
TAPS = 4
HEADS, KV_HEADS, HD = 16, 4, 64
GRP = HEADS // KV_HEADS
D_KV = KV_HEADS * HD
PAIRS = KV_HEADS // 2
CH = 64
NCH = T // CH
D_FF = 2816
KF = D_FF // P
EPS = 1e-6
LRU_C = 8.0
MASKED = -1e30

RING = 4
CAP = 4 * P
UNIT = [4, 4]
GATE = [3, 3]
L_HEAD = UNIT + UNIT
L_STEP = UNIT + GATE + UNIT
L_TAIL = [3, 3, 2, 2]
V_BLOCKS = [4, 4, 4, 4]
KV = UNIT + UNIT + V_BLOCKS
A_STEP = [2, 2, 2, 2] + [3, 3, 2, 2]
B_STEP = UNIT + UNIT
F_STEP = UNIT + UNIT
DOWN = [4, 4, 4, 4, 3, 3]

MIX_STAGES = [("head", L_HEAD, 2), ("step", L_STEP, KR - 2), ("tail", L_TAIL, 1), ("kv", KV, 1),
              ("q", UNIT, KD), ("a", A_STEP, KD), ("b", B_STEP, KD), ("o", UNIT, KD)]
FFN_STAGES = [("f", F_STEP, KF), ("d", DOWN, KD)]


def stage_bases(stages, base):
    out = {}
    for name, sizes, groups in stages:
        out[name] = base
        base += len(sizes) * groups
    return out, base


BASE = []
_n = 0
for _h in range(HALVES):
    _b, _n = stage_bases(MIX_STAGES, _n)
    BASE.append(_b)
for _h in range(HALVES):
    _b, _n = stage_bases(FFN_STAGES, _n)
    BASE[_h].update(_b)
N_BLOCKS = _n

PARAMS = {}
_at = 0
for _name, _w in [("g_pre_mix", KD), ("g_post_mix", KD), ("g_pre_ffn", KD), ("g_post_ffn", KD),
                  ("conv_w", TAPS * KR), ("conv_b", KR), ("lam", KR), ("sink", 8),
                  ("b_rg", KR), ("b_ig", KR), ("b_gate_lru", KD), ("b_gate_attn", KD)]:
    PARAMS[_name] = _at
    _at += _w
N_PARAMS = _at
HALVED = PARAMS["b_rg"]


def build(nc, x_d, par_d, alibi_d, eye_d, w_d, x1_d, out_d):
    with ExitStack() as ctx:
        cursor = [0]

        def at(name, shape, dt, offset=None):
            size = 4 * int(np.prod(shape[1:]))
            size = (size + 31) // 32 * 32
            if offset is None:
                offset = cursor[0]
                cursor[0] += size
            return nc.alloc_sbuf_tensor_at(name, shape, dt, offset=offset + sbuf0)

        def sem(name):
            return ctx.enter_context(nc.semaphore(name))

        sbuf0 = (nc.sbuf_base + 31) // 32 * 32

        w_raw = at("w_raw", [P, RING, CAP], F32)
        w_hi = at("w_hi", [P, RING, CAP], F32R)
        w_lo = at("w_lo", [P, RING, CAP], F32R)
        par = at("par", [P, N_PARAMS], F32)
        half_b = at("half_b", [P, N_PARAMS - HALVED], F32)
        sp = at("sp", [P, 4, KR], F32)
        sp2 = at("sp2", [P, KR], F32)
        ones = at("ones", [P, P], F32)
        eye = at("eye", [P, P], F32)
        alibi = at("alibi", [P, 8, 2 * CH], F32)
        u_carry = at("u_carry", [P, KR, TAPS - 1], F32)
        h_carry = at("h_carry", [P, KR], F32)
        stat = at("stat", [P, 6, 8], F32)
        acc = at("acc", [P, T], F32)
        sq = at("sq", [P, T], F32)
        rstd_a = at("rstd_a", [P, T], F32)
        rstd_b = at("rstd_b", [P, T], F32)
        tmp = at("tmp", [P, 2, T], F32)
        xs = at("xs", [P, 2, T], F32)
        h_hi = at("h_hi", [P, KD, T], F32R)
        h_lo = at("h_lo", [P, KD, T], F32R)
        rows = at("rows", [P, KD, T], F32)
        reg_b = cursor[0]
        lru_hi = at("lru_hi", [P, KR, T], F32R)
        lru_lo = at("lru_lo", [P, KR, T], F32R)
        mg_hi = at("mg_hi", [P, KD, T], F32R, reg_b)
        mg_lo = at("mg_lo", [P, KD, T], F32R, reg_b + 4 * KD * T)
        reg_c = cursor[0]
        q_hi = at("q_hi", [P, KD // 2, 2 * T], F32R)
        q_lo = at("q_lo", [P, KD // 2, 2 * T], F32R)
        uc_hi = at("uc_hi", [P, 4, T], F32R, reg_c)
        uc_lo = at("uc_lo", [P, 4, T], F32R, reg_c + 16 * T)
        uc = at("uc", [P, 4, T], F32, reg_c + 32 * T)
        gy = at("gy", [P, 4, T], F32, reg_c + 48 * T)
        reg_p = cursor[0]
        prob = at("prob", [P, 8, 2 * CH], F32)
        pt_hi = at("pt_hi", [P, 8, 2 * CH], F32R)
        pt_lo = at("pt_lo", [P, 8, 2 * CH], F32R)
        g_r = at("g_r", [P, T], F32, reg_p)
        g_a = at("g_a", [P, T], F32, reg_p + 4 * T)
        g_i = at("g_i", [P, T], F32, reg_p + 8 * T)
        g_h = at("g_h", [P, T], F32, reg_p + 12 * T)
        u_raw = at("u_raw", [P, TAPS - 1 + T], F32, reg_p + 16 * T)
        k_hi = at("k_hi", [P, PAIRS, CH + T], F32R)
        k_lo = at("k_lo", [P, PAIRS, CH + T], F32R)
        v_hi = at("v_hi", [P, NCH + 1, D_KV], F32R)
        v_lo = at("v_lo", [P, NCH + 1, D_KV], F32R)
        f_hi = at("f_hi", [P, KF, T], F32R, reg_b)
        f_lo = at("f_lo", [P, KF, T], F32R, reg_b + 4 * KF * T)
        assert reg_b + 8 * KF * T <= cursor[0]
        assert sbuf0 + cursor[0] <= nc.sbuf_usable_end, (sbuf0 + cursor[0], nc.sbuf_usable_end)

        ps = ctx.enter_context(nc.psum_tensor("ps", [P, 8, 512], F32))
        BK_STAT = 3
        BK_S, BK_PT, BK_PV = 2, 4, 6

        w_loaded = [sem(f"w_loaded{i}") for i in range(RING)]
        par_loaded, x0_loaded = sem("par_loaded"), sem("x0_loaded")
        alibi_loaded = sem("alibi_loaded")
        xs_loaded = [sem(f"xs_loaded{i}") for i in range(2)]
        x1_stored, out_stored = sem("x1_stored"), sem("out_stored")
        w_hi_made, w_lo_made = sem("w_hi_made"), sem("w_lo_made")
        blocks_done = sem("blocks_done")
        prep_act, prep_dve, zeroed = sem("prep_act"), sem("prep_dve"), sem("zeroed")
        squared, summed, stat_mm, dev_made, rstd_made = (
            sem("squared"), sem("summed"), sem("stat_mm"), sem("dev_made"), sem("rstd_made"))
        normed, h_hi_made, h_lo_made = sem("normed"), sem("h_hi_made"), sem("h_lo_made")
        u_ctx, u_copied, tap0, taps, uc_hi_made, uc_lo_made, pad_zeroed = (
            sem("u_ctx"), sem("u_copied"), sem("tap0"), sem("taps"), sem("uc_hi_made"),
            sem("uc_lo_made"), sem("pad_zeroed"))
        r_made, i_made, th_made, th1_made, root_made, a_made, gelu_made, lru_hi_made = (
            sem("r_made"), sem("i_made"), sem("th_made"), sem("th1_made"), sem("root_made"),
            sem("a_made"), sem("gelu_made"), sem("lru_hi_made"))
        iu_made, recip_made, amp_made, b_made, scanned, h_kept, lru_made, lru_lo_made = (
            sem("iu_made"), sem("recip_made"), sem("amp_made"), sem("b_made"), sem("scanned"),
            sem("h_kept"), sem("lru_made"), sem("lru_lo_made"))
        kept_hi, kept_lo = sem("kept_hi"), sem("kept_lo")
        k_hi_made, k_lo_made, v_hi_made, v_lo_made = (
            sem("k_hi_made"), sem("k_lo_made"), sem("v_hi_made"), sem("v_lo_made"))
        q_hi_made, q_lo_made = sem("q_hi_made"), sem("q_lo_made")
        qk_done, biased, maxed, exped, probed, pt_done, pt_hi_made, pt_lo_made, pv_done = (
            sem("qk_done"), sem("biased"), sem("maxed"), sem("exped"), sem("probed"),
            sem("pt_done"), sem("pt_hi_made"), sem("pt_lo_made"), sem("pv_done"))
        ao_hi_made, ao_lo_made = sem("ao_hi_made"), sem("ao_lo_made")
        ga_made, lru_part = sem("ga_made"), sem("lru_part")
        gb_made, attn_part, merged, mg_hi_made, mg_lo_made = (
            sem("gb_made"), sem("attn_part"), sem("merged"), sem("mg_hi_made"), sem("mg_lo_made"))
        row_out = sem("row_out")
        silu_made, f_made, f_hi_made, f_lo_made = (
            sem("silu_made"), sem("f_made"), sem("f_hi_made"), sem("f_lo_made"))
        scaled, added = sem("scaled"), sem("added")
        waits_closed = sem("waits_closed")

        def wait_pos(eng, s, value):
            if not isinstance(value, int) or value > 0:
                eng.wait_ge(s, value)

        def own_wait(eng):
            eng.sem_inc(waits_closed, 1)

        def col(name, t, n=1):
            return par[:, bass.ds(t + PARAMS[name], n)]

        def half_col(name, t):
            return half_b[:, bass.ds(t + (PARAMS[name] - HALVED), 1)]

        def q_tile(q, pair, j):
            return q[:, bass.ds(pair, 1), :].rearrange("p o (c j t) -> p (o c) j t", j=2, t=CH)[:, :, j, :]

        def rd(ap):
            return ap.bitcast(F32)

        def rstd_of(n):
            return rstd_b if n in (1, 3, 5) else rstd_a

        block = ctx.enter_context(nc.Block())

        @block.sync
        def _(sp_eng):
            def load(dram, g, sizes, n, off0=0):
                off = 0
                for b, size in enumerate(sizes):
                    wait_pos(sp_eng, w_lo_made, n + b - RING + 1)
                    sp_eng.dma_start(w_raw[:, b % RING, 0:size * P],
                                     dram[g, :, off:off + size * P]).then_inc(w_loaded[b % RING], 16)
                    off += size * P

            def stream(stages, bases):
                for name, sizes, groups in stages:
                    per = 1 if len(sizes) % RING == 0 else 2
                    sizes2, dram, base = sizes * per, w_d[name], bases[name]
                    n_it = groups // per
                    first = 1 if base == 0 else 0
                    if first:
                        load(dram, 0, sizes2, 0)
                    if n_it - first == 1:
                        load(dram, first, sizes2, base + first * len(sizes2))
                    elif n_it > first:
                        with sp_eng.Fori(first, n_it) as g:
                            load(dram, g, sizes2, g * len(sizes2) + base)

            for h in range(HALVES):
                stream(MIX_STAGES, BASE[h])
            for h in range(HALVES):
                stream(FFN_STAGES, BASE[h])

        @block.gpsimd
        def _(pool):
            nc.gpsimd.memset(ones[:], 1.0).then_inc(zeroed, 1)
            nc.gpsimd.memset(u_carry[:], 0.0).then_inc(zeroed, 1)
            nc.gpsimd.memset(h_carry[:], 0.0).then_inc(zeroed, 1)
            nc.gpsimd.memset(rd(k_hi[:, :, 0:CH]), 0.0).then_inc(zeroed, 1)
            nc.gpsimd.memset(rd(k_lo[:, :, 0:CH]), 0.0).then_inc(zeroed, 1)
            nc.gpsimd.memset(rd(v_hi[0:CH, 0, :]), 0.0).then_inc(zeroed, 1)
            nc.gpsimd.memset(rd(v_lo[0:CH, 0, :]), 0.0).then_inc(zeroed, 1)

            def split(sizes, n, turn):
                for b, size in enumerate(sizes):
                    s, w = b % RING, slice(0, size * P)
                    pool.wait_ge(w_loaded[s], (turn + b // RING + 1) * 16)
                    wait_pos(pool, blocks_done, n + b - RING + 1)
                    own_wait(pool)
                    nc.gpsimd.tensor_scalar(w_hi[:, s, w], w_raw[:, s, w], 1.0, 0.0,
                                            ALU.mult, ALU.add).then_inc(w_hi_made, 1)
                    pool.wait_ge(w_hi_made, n + b + 1)
                    nc.gpsimd.tensor_tensor(w_lo[:, s, w], w_raw[:, s, w], rd(w_hi[:, s, w]),
                                            ALU.subtract).then_inc(w_lo_made, 1)

            def stream(stages, bases):
                for name, sizes, groups in stages:
                    per = 1 if len(sizes) % RING == 0 else 2
                    sizes2, base = sizes * per, bases[name]
                    n_it = groups // per
                    first = 1 if base == 0 else 0
                    assert base % RING == 0 and len(sizes2) % RING == 0
                    turns = len(sizes2) // RING
                    if first:
                        split(sizes2, 0, 0)
                    if n_it - first == 1:
                        split(sizes2, base + first * len(sizes2), base // RING + first * turns)
                    elif n_it > first:
                        with pool.Fori(first, n_it) as g:
                            split(sizes2, g * len(sizes2) + base, g * turns + base // RING)

            for h in range(HALVES):
                stream(MIX_STAGES, BASE[h])
            for h in range(HALVES):
                stream(FFN_STAGES, BASE[h])

        @block.tensor
        def _(pe):
            mm = nc.tensor.matmul

            def project(bank, n, slot, sizes, hi, lo, ready=None, tiles=None):
                total, k = sum(sizes), 0
                for b, size in enumerate(sizes):
                    pe.wait_ge(w_lo_made, n + b + 1)
                    s = (slot + b) % RING
                    for q in range(size):
                        if ready:
                            pe.wait_ge(ready[0], ready[1] + k + 1)
                        w = slice(q * P, (q + 1) * P)
                        kk = tiles[k] if tiles else k
                        if hi is q_hi:
                            x_hi, x_lo = q_tile(hi, kk // 2, kk % 2), q_tile(lo, kk // 2, kk % 2)
                        else:
                            x_hi, x_lo = hi[:, kk, :], lo[:, kk, :]
                        mm(ps[:, bank, :], w_hi[:, s, w], x_hi, start=(k == 0), stop=False)
                        mm(ps[:, bank, :], w_hi[:, s, w], x_lo, start=False, stop=False)
                        last = mm(ps[:, bank, :], w_lo[:, s, w], x_hi, start=False,
                                  stop=(k == total - 1))
                        k += 1
                    last.then_inc(blocks_done, 1)

            def stat_sum(n):
                pe.wait_ge(summed, 9 * (n + 1))
                wait_pos(pe, dev_made, n)
                wait_pos(pe, biased, {3: NCH, 2: NCH}.get(n, HALVES * NCH if n > 3 else 0))
                mm(ps[:, BK_STAT, :], ones[:], acc[:], start=True, stop=True).then_inc(stat_mm, 1)

            def gates(h, j, n, sizes, slot, q):
                J = j + KR * h
                last_tile = len(sizes) and sizes[0] == 2
                pe.wait_ge(uc_lo_made, J + (1 if last_tile else 2))
                if last_tile:
                    pe.wait_ge(r_made, J)
                    pe.wait_ge(i_made, J)
                tiles = [(q + d) % 4 for d in (-1, 0, 1)]
                for g in range(2):
                    project(4 + g, n + g, slot + g, sizes[g:g + 1], uc_hi, uc_lo, tiles=tiles)

            def u_unit(h, j, n, slot, ready=None):
                wait_pos(pe, u_copied, (j + KR * h) * 2)
                project(0, n, slot, UNIT, h_hi, h_lo, ready)

            def y_unit(h, j, n, slot):
                wait_pos(pe, gelu_made, j + KR * h)
                project(2, n, slot, UNIT, h_hi, h_lo)

            def recurrent(h):
                base = BASE[h]
                if h:
                    pe.wait_ge(row_out, 2 * (KD * h - 1))
                    pe.wait_ge(biased, NCH * h)
                for j in range(2):
                    n = base["head"] + 4 * j
                    u_unit(h, j, n, 0, (h_lo_made, KD * h) if j == 0 else None)
                    y_unit(h, j, n + 2, 2)
                if h:
                    stat_sum(2)
                else:
                    pass
                pe.wait_ge(pad_zeroed, 2 * (h + 1))
                with pe.Fori(0, 2) as it:
                    for q in range(4):
                        j = it * 4 + (2 + q)
                        n = (it * 4 + q) * 6 + base["step"]
                        slot = 6 * q
                        u_unit(h, j, n, slot)
                        gates(h, j - 2, n + 2, GATE, slot + 2, q)
                        y_unit(h, j, n + 4, slot + 4)
                stat_sum(3 if h else 1)
                gates(h, 8, base["tail"], [3, 3], 0, 0)
                gates(h, 9, base["tail"] + 2, [2, 2], 2, 1)

            def kvq(h):
                base = BASE[h]
                pe.wait_ge(u_copied, 2 * KR * (h + 1))
                project(0, base["kv"], 0, UNIT, h_hi, h_lo)
                if h == 0:
                    pass
                else:
                    pe.wait_ge(row_out, 2 * KD * h)
                project(1, base["kv"] + 2, 2, UNIT, h_hi, h_lo)
                pe.wait_ge(r_made, KR * (h + 1))
                pe.wait_ge(i_made, KR * (h + 1))
                wait_pos(pe, ao_lo_made, 2 * NCH * h)
                for b in range(4):
                    pe.wait_ge(w_lo_made, base["kv"] + 4 + b + 1)
                    for m in range(4):
                        out = ps[:, 4 + m, 0:D_KV]
                        for q in range(2):
                            k = 2 * b + q
                            w = slice(q * D_KV, (q + 1) * D_KV)
                            t = slice(m * P, (m + 1) * P)
                            mm(out, h_hi[:, k, t], w_hi[:, b, w], start=(k == 0), stop=False)
                            mm(out, h_lo[:, k, t], w_hi[:, b, w], start=False, stop=False)
                            last = mm(out, h_hi[:, k, t], w_lo[:, b, w], start=False, stop=(k == KD - 1))
                    last.then_inc(blocks_done, 1)
                pe.wait_ge(k_hi_made, PAIRS * (h + 1))
                pe.wait_ge(k_lo_made, PAIRS * (h + 1))
                for t in range(2):
                    project(t, base["q"] + 2 * t, 2 * t, UNIT, h_hi, h_lo)
                with pe.Fori(1, 4) as it:
                    for q in range(2):
                        t = it * 2 + q
                        pe.wait_ge(q_lo_made, t + (KD * h - 1))
                        project(q, t * 2 + base["q"], 2 * q, UNIT, h_hi, h_lo)

            def scores(h, c):
                C = NCH * h + c
                pe.wait_ge(biased, C) if C else None
                for p in range(PAIRS):
                    for b in range(2):
                        for half in range(2):
                            r = slice(64 * half, 64 * half + 64)
                            i = 2 * p + b
                            out = ps[:, BK_S + half, i * P:(i + 1) * P]
                            t = 2 * p + b
                            cq = slice(c * P, (c + 1) * P)
                            ck = slice(c * CH, (c + 2) * CH)
                            mm(out, q_hi[r, t, cq], k_hi[r, p, ck], start=True, stop=False)
                            mm(out, q_hi[r, t, cq], k_lo[r, p, ck], start=False, stop=False)
                            last = mm(out, q_lo[r, t, cq], k_hi[r, p, ck], start=False, stop=True)
                last.then_inc(qk_done, 1)

            def turn_probs(h, c):
                C = NCH * h + c
                pe.wait_ge(probed, 3 * (C + 1))
                wait_pos(pe, pt_lo_made, C)
                for i in range(8):
                    last = nc.tensor.transpose(ps[:, BK_PT + i // 4, (i % 4) * P:(i % 4 + 1) * P],
                                               prob[:, i, :], eye[:])
                last.then_inc(pt_done, 1)

            def weigh_values(h, c):
                C = NCH * h + c
                pe.wait_ge(pt_lo_made, C + 1)
                wait_pos(pe, ao_lo_made, 2 * C)
                for half in range(2):
                    for p in range(PAIRS):
                        out = ps[:, BK_PV + half, p * 256:(p + 1) * 256]
                        v = slice(p * P, (p + 1) * P)
                        t = slice(4 * half + 2 * p, 4 * half + 2 * p + 2)
                        mm(out, v_hi[:, c, v], pt_hi[:, t, :], start=True, stop=False)
                        mm(out, v_hi[:, c, v], pt_lo[:, t, :], start=False, stop=False)
                        last = mm(out, v_lo[:, c, v], pt_hi[:, t, :], start=False, stop=True)
                last.then_inc(pv_done, 1)

            def attention(h):
                pe.wait_ge(q_lo_made, KD * (h + 1))
                pe.wait_ge(gelu_made, KR * (h + 1))
                pe.wait_ge(dev_made, 4 if h else 2)
                for c in range(NCH):
                    n = BASE[h]["a"] + 8 * c
                    scores(h, c)
                    wait_pos(pe, ga_made, NCH * h + c) if c else None
                    project(0, n, 0, A_STEP[:4], h_hi, h_lo)
                    if c:
                        weigh_values(h, c - 1)
                    else:
                        pe.wait_ge(v_hi_made, 3 * (h + 1))
                        pe.wait_ge(v_lo_made, 3 * (h + 1))
                        pe.wait_ge(lru_lo_made, KR * (h + 1))
                    wait_pos(pe, lru_part, NCH * h + c) if c else None
                    project(1, n + 4, 0, A_STEP[4:], lru_hi, lru_lo)
                    turn_probs(h, c)
                weigh_values(h, NCH - 1)

            def attn_branch(h):
                base = BASE[h]["b"]

                def pair(c, wait0, wait1):
                    pe.wait_ge(*wait0)
                    project(0, c * 4 + base, 0, UNIT, h_hi, h_lo)
                    pe.wait_ge(*wait1)
                    if isinstance(c, int):
                        pe.wait_ge(ao_lo_made, 2 * NCH * (h + 1))
                    project(1, c * 4 + (base + 2), 2, UNIT, q_hi, q_lo)

                pair(0, (ga_made, NCH * (h + 1)), (lru_part, NCH * (h + 1)))
                with pe.Fori(1, KD) as c:
                    pair(c, (gb_made, c + KD * h), (attn_part, c + KD * h))

            def out_tiles(r0, base, sizes, hi, lo, first_waits, ready, between=None):
                for t in range(2):
                    pe.wait_ge(*first_waits[t])
                    project(t, base + len(sizes) * t, len(sizes) * t, sizes, hi, lo,
                            ready if t == 0 else None)
                with pe.Fori(1, KD // 2) as it:
                    for q in range(2):
                        t = it * 2 + q
                        pe.wait_ge(row_out, t * 2 + (2 * r0 - 2))
                        project(q, t * len(sizes) + base, len(sizes) * q, sizes, hi, lo)

            def ffn_up(h):
                base = BASE[h]["f"]

                def tile(t, n, ready=None):
                    project(0, n, 0, UNIT, h_hi, h_lo, ready)
                    return n

                for t in range(2):
                    if t == 0:
                        pe.wait_ge(row_out, 2 * (16 + KD * h - 1))
                    else:
                        pe.wait_ge(silu_made, KF * h + t)
                    project(0, base + 4 * t, 0, UNIT, h_hi, h_lo,
                            (h_lo_made, KD * (2 + h)) if t == 0 else None)
                    if t == 0:
                        pe.wait_ge(row_out, 2 * (16 + KD * h))
                    else:
                        pe.wait_ge(f_made, KF * h + t)
                    project(1, base + 4 * t + 2, 2, UNIT, h_hi, h_lo)
                stat_sum(6 if h else 4)
                with pe.Fori(2, KF) as t:
                    pe.wait_ge(silu_made, t + KF * h)
                    project(0, t * 4 + base, 0, UNIT, h_hi, h_lo)
                    pe.wait_ge(f_made, t + KF * h)
                    project(1, t * 4 + (base + 2), 2, UNIT, h_hi, h_lo)

            pe.wait_ge(zeroed, 7)
            stat_sum(0)
            for h in range(HALVES):
                recurrent(h)
                kvq(h)
                pe.wait_ge(par_loaded, 32)
                attention(h)
                attn_branch(h)
                out_tiles(KD * h, BASE[h]["o"], UNIT, mg_hi, mg_lo,
                          [(gb_made, KD * (h + 1)), (attn_part, KD * (h + 1))],
                          (mg_lo_made, KD * h))
            for h in range(HALVES):
                ffn_up(h)
                if h == 0:
                    stat_sum(5)
                out_tiles(16 + KD * h, BASE[h]["d"], DOWN, f_hi, f_lo,
                          [(silu_made, KF * (h + 1)), (f_made, KF * (h + 1))],
                          (f_lo_made, KF * h))
            stat_sum(7)

        @block.scalar
        def _(act):
            fn = nc.scalar.activation

            def load_xs(s, t, src):
                act.dma_start(xs[:, t % 2, :], src[t]).then_inc(xs_loaded[t % 2], 16)

            def deviation(n):
                act.wait_ge(stat_mm, n + 1)
                fn(rstd_of(n)[:], ps[:, BK_STAT, :], ACT.Sqrt, bias=eps_ap, scale=1.0 / D)\
                    .then_inc(dev_made, 1)

            def square(n, t, src):
                wait_pos(act, summed, n * 9 + t + 1)
                fn(sq[:], src, ACT.Square).then_inc(squared, 1)

            def norm_hi(k, t):
                act.wait_ge(normed, KD * k + t + 1)
                fn(h_hi[:, t, :], tmp[:, t % 2, :], ACT.Copy).then_inc(h_hi_made, 1)

            def conv_in(h, j, n, q):
                J = j + KR * h
                act.wait_ge(blocks_done, n + 2)
                wait_pos(act, taps, J * 3)
                own_wait(act)
                fn(u_raw[:, 0:TAPS - 1], u_carry[:, bass.ds(j, 1), :], ACT.Copy).then_inc(u_ctx, 1)
                fn(u_raw[:, TAPS - 1:], ps[:, 0, :], ACT.Copy).then_inc(u_copied, 1)
                act.wait_ge(u_ctx, J + 1)
                own_wait(act)
                fn(u_carry[:, bass.ds(j, 1), :], ps[:, 0, T - TAPS + 1:T], ACT.Copy)\
                    .then_inc(u_copied, 1)
                act.wait_ge(u_copied, J * 2 + 1)
                own_wait(act)
                fn(uc[:, q, :], u_raw[:, 0:T], ACT.Identity, bias=col("conv_b", j),
                   scale=col("conv_w", j)).then_inc(tap0, 1)

            def conv_hi(h, j, q):
                act.wait_ge(taps, (j + KR * h) * 3 + 3)
                fn(uc_hi[:, q, :], uc[:, q, :], ACT.Copy).then_inc(uc_hi_made, 1)

            def gate_fns(h, j, n):
                J = j + KR * h
                act.wait_ge(blocks_done, n + 2)
                own_wait(act)
                fn(g_r[:], ps[:, 4, :], ACT.Tanh, bias=half_col("b_rg", j), scale=0.5)\
                    .then_inc(r_made, 1)
                fn(g_i[:], ps[:, 5, :], ACT.Tanh, bias=half_col("b_ig", j), scale=0.5)\
                    .then_inc(i_made, 1)
                act.wait_ge(r_made, J + 1)
                own_wait(act)
                fn(g_r[:], g_r[:], ACT.Tanh, bias=sp2[:, bass.ds(j, 1)],
                   scale=sp2[:, bass.ds(j, 1)]).then_inc(th_made, 1)
                act.wait_ge(th_made, J + 1)
                fn(g_a[:], g_r[:], ACT.Identity, bias=one_ap).then_inc(th1_made, 1)

            def gate_root(h, j):
                J = j + KR * h
                act.wait_ge(th1_made, J + 1)
                fn(g_r[:], g_r[:], ACT.Sqrt).then_inc(root_made, 1)

            def gelu(h, j, n, q):
                J = j + KR * h
                act.wait_ge(blocks_done, n + 2)
                fn(gy[:, q, :], ps[:, 2, :], ACT.Gelu_apprx_tanh).then_inc(gelu_made, 1)

            def decay(h, j):
                act.wait_ge(amp_made, j + KR * h + 1)
                fn(g_a[:], g_a[:], ACT.Identity, bias=neg_ap, scale=2.0).then_inc(a_made, 1)

            def lru_out_hi(h, j):
                act.wait_ge(lru_made, j + KR * h + 1)
                own_wait(act)
                fn(lru_hi[:, bass.ds(j, 1), :], g_h[:], ACT.Copy).then_inc(lru_hi_made, 1)

            def recurrent(h):
                base = BASE[h]
                if h:
                    act.wait_ge(added, 0) if False else None
                for j in range(2):
                    n = base["head"] + 4 * j
                    conv_in(h, j, n, j)
                    conv_hi(h, j, j)
                    gelu(h, j, n + 2, j)
                if h:
                    residual(0)
                else:
                    for t in range(2):
                        load_xs(0, t, x_d[1])
                    for t in range(KD):
                        act.wait_ge(xs_loaded[t % 2], 16 * (t // 2 + 1))
                        square(1, t, xs[:, t % 2, :])
                        if t + 2 < KD:
                            act.wait_ge(squared, KD + t + 1)
                            load_xs(0, t + 2, x_d[1])
                with act.Fori(0, 2) as it:
                    for q in range(4):
                        j = it * 4 + (2 + q)
                        n = (it * 4 + q) * 6 + base["step"]
                        conv_in(h, j, n, (2 + q) % 4)
                        gate_fns(h, j - 2, n + 2)
                        conv_hi(h, j, (2 + q) % 4)
                        gate_root(h, j - 2)
                        gelu(h, j, n + 4, (2 + q) % 4)
                        decay(h, j - 2)
                        lru_out_hi(h, j - 2)
                deviation(3 if h else 1)
                for j in (8, 9):
                    gate_fns(h, j, base["tail"] + 2 * (j - 8))
                    gate_root(h, j)
                    decay(h, j)
                    lru_out_hi(h, j)

            def kvq(h):
                n = BASE[h]["kv"]
                if h:
                    act.wait_ge(blocks_done, n)
                    fn(k_hi[:, :, 0:CH], rd(k_hi[:, :, T:T + CH]), ACT.Copy).then_inc(kept_hi, 1)
                    fn(v_hi[0:CH, 0, :], rd(v_hi[0:CH, NCH, :]), ACT.Copy).then_inc(kept_hi, 1)
                    act.wait_ge(kept_hi, 2)
                else:
                    act.wait_ge(zeroed, 7)
                for p in range(PAIRS):
                    act.wait_ge(blocks_done, n + 2 * (p + 1))
                    fn(k_hi[:, p, CH:CH + T], ps[:, p, :], ACT.Copy).then_inc(k_hi_made, 1)
                act.wait_ge(blocks_done, n + 8)
                fn(v_hi[:, 1:NCH + 1:2, :], ps[:, 4:8, 0:D_KV], ACT.Copy).then_inc(v_hi_made, 1)
                act.wait_ge(v_hi_made, 3 * h + 1)
                fn(v_hi[CH:P, 0:NCH:2, :], rd(v_hi[0:CH, 1:NCH + 1:2, :]), ACT.Copy)\
                    .then_inc(v_hi_made, 1)
                fn(v_hi[0:CH, 2:NCH + 1:2, :], rd(v_hi[CH:P, 1:NCH + 1:2, :]), ACT.Copy)\
                    .then_inc(v_hi_made, 1)
                act.wait_ge(lru_lo_made, KR * (h + 1))
                with act.Fori(0, 4) as it:
                    for q in range(2):
                        t = it * 2 + q
                        act.wait_ge(blocks_done, t * 2 + (BASE[h]["q"] + 2))
                        own_wait(act)
                        fn(q_tile(q_hi, it, q), ps[:, q, :].rearrange("p (c t) -> p c t", t=CH),
                           ACT.Copy).then_inc(q_hi_made, 1)

            def attention(h):
                def exps(C):
                    act.wait_ge(maxed, C * 4 + 4)
                    for i in range(8):
                        fn(prob[:, i, :], prob[:, i, :], ACT.Exp, bias=stat[:, 2, i:i + 1],
                           accum_out=stat[:, 3, i:i + 1]).then_inc(exped, 1)
                    fn(stat[:, 4, :], stat[:, 1, :], ACT.Exp).then_inc(exped, 1)

                def gate(c, C):
                    act.wait_ge(blocks_done, c * 8 + (BASE[h]["a"] + 4))
                    wait_pos(act, lru_part, C)
                    own_wait(act)
                    fn(tmp[:, 0, :], ps[:, 0, :], ACT.Tanh, bias=half_col("b_gate_lru", c),
                       scale=0.5).then_inc(ga_made, 1)

                def out_hi(c, C):
                    act.wait_ge(pv_done, C + 1)
                    own_wait(act)
                    for half in range(2):
                        r = slice(64 * half, 64 * half + 64)
                        fn(q_hi[r, :, bass.ds(c * P, P)],
                           ps[r, BK_PV + half, :].rearrange("p (t q) -> p t q", q=P),
                           ACT.Copy).then_inc(ao_hi_made, 1)

                def turned_hi(C):
                    act.wait_ge(pt_done, C + 1)
                    fn(pt_hi[:, :, :], ps[:, BK_PT:BK_PT + 2, :].rearrange("p b (i k) -> p (b i) k", i=4),
                       ACT.Copy).then_inc(pt_hi_made, 1)

                def chunk(c, C):
                    exps(C)
                    gate(c, C)
                    if not isinstance(c, int):
                        out_hi(c - 1, C - 1)
                    turned_hi(C)

                chunk(0, NCH * h)
                if h == 0:
                    act.wait_ge(biased, 1)
                    act.dma_start(alibi[:], alibi_d[1]).then_inc(alibi_loaded, 16)
                with act.Fori(1, NCH) as c:
                    chunk(c, c + NCH * h)
                out_hi(NCH - 1, NCH * (h + 1) - 1)

            def attn_branch(h):
                def tile(c, C):
                    act.wait_ge(blocks_done, c * 4 + (BASE[h]["b"] + 2))
                    wait_pos(act, attn_part, C) if not isinstance(c, int) else \
                        act.wait_ge(lru_part, NCH * (h + 1))
                    own_wait(act)
                    fn(tmp[:, 0, :], ps[:, 0, :], ACT.Tanh, bias=half_col("b_gate_attn", c),
                       scale=0.5).then_inc(gb_made, 1)
                    act.wait_ge(merged, C + 1)
                    own_wait(act)
                    fn(mg_hi[:, bass.ds(c, 1), :], tmp[:, 1, :], ACT.Copy, scale=0.5)\
                        .then_inc(mg_hi_made, 1)

                tile(0, KD * h)
                with act.Fori(1, KD) as c:
                    tile(c, c + KD * h)

            def row_tile(n, r0, t, q, done_after):
                act.wait_ge(blocks_done, done_after)
                own_wait(act)
                fn(rows[:, bass.ds(t, 1), :], ps[:, q, :], ACT.Copy).then_inc(row_out, 1)
                act.wait_ge(summed, t + (9 * n + 1))
                fn(sq[:], ps[:, q, :], ACT.Square).then_inc(row_out, 1)

            def rows_out(n, r0, base, size, between):
                for t in range(2):
                    row_tile(n, r0, t, t, base + size * (t + 1))
                between()
                with act.Fori(1, KD // 2) as it:
                    for q in range(2):
                        t = it * 2 + q
                        row_tile(n, r0, t, q, t * size + (base + size))

            def normed_stream(k, s, src):
                for t in range(2):
                    load_xs(s, t, src)
                for t in range(KD):
                    norm_hi(k, t)
                    if t + 2 < KD:
                        load_xs(s, t + 2, src)

            def residual(h):
                s, n = 2 + 2 * h, 2 + 2 * h
                for t in range(2):
                    load_xs(s, t, x_d[h])
                deviation(n)
                for t in range(KD):
                    act.wait_ge(added, KD * h + t + 1)
                    if t + 2 < KD:
                        load_xs(s, t + 2, x_d[h])
                    act.dma_start(x1_d[h][t], rows[:, t, :]).then_inc(x1_stored, 16)
                    square(n + 1, t, rows[:, t, :])

            def final(h):
                for t in range(2):
                    load_xs(6 + h, t, x1_d[h])
                deviation(6 + h)
                for t in range(KD):
                    act.wait_ge(added, KD * (2 + h) + t + 1)
                    if t + 2 < KD:
                        load_xs(6 + h, t + 2, x1_d[h])
                    act.dma_start(out_d[h][t], rows[:, t, :]).then_inc(out_stored, 16)

            act.dma_start(par[:], par_d).then_inc(par_loaded, 16)
            for t in range(KD):
                act.dma_start(rows[:, t, :], x_d[0][t]).then_inc(x0_loaded, 16)
            act.dma_start(eye[:], eye_d).then_inc(par_loaded, 16)
            act.dma_start(alibi[:], alibi_d[0]).then_inc(alibi_loaded, 16)
            act.wait_ge(zeroed, 7)
            one_ap, neg_ap, eps_ap = 1.0, -1.0, EPS

            act.wait_ge(x0_loaded, 16 * KD)
            for t in range(KD):
                square(0, t, rows[:, t, :])
            deviation(0)
            act.wait_ge(par_loaded, 32)
            lam = par[:, PARAMS["lam"]:PARAMS["lam"] + KR]
            fn(sp[:, 0, :], lam, ACT.Abs).then_inc(prep_act, 1)
            act.wait_ge(prep_act, 1)
            fn(sp[:, 1, :], sp[:, 0, :], ACT.Exp, scale=-1.0).then_inc(prep_act, 1)
            for t in range(KD):
                norm_hi(0, t)
            act.wait_ge(prep_dve, 12)

            for h in range(HALVES):
                recurrent(h)
                kvq(h)
                attention(h)
                attn_branch(h)
                n, o = 2 + 2 * h, BASE[h]["o"]
                if h == 0:
                    rows_out(n, 0, o, 2, lambda: normed_stream(1, 1, x_d[1]))
                else:
                    act.wait_ge(x1_stored, 16 * KD)
                    rows_out(n, KD, o, 2, lambda: normed_stream(2, 3, x1_d[0]))
            for h in range(HALVES):
                def tile(t, F):
                    act.wait_ge(blocks_done, t * 4 + (BASE[h]["f"] + 2))
                    if isinstance(t, int) and t == 0:
                        act.wait_ge(h_lo_made, KD * (3 + h))
                    else:
                        act.wait_ge(f_made, F)
                    fn(tmp[:, 0, :], ps[:, 0, :], ACT.Silu).then_inc(silu_made, 1)
                    act.wait_ge(f_made, F + 1)
                    own_wait(act)
                    fn(f_hi[:, bass.ds(t, 1), :], tmp[:, 1, :], ACT.Copy).then_inc(f_hi_made, 1)

                for t in range(2):
                    tile(t, KF * h + t)
                if h == 0:
                    residual(1)
                else:
                    final(0)
                with act.Fori(2, KF) as t:
                    tile(t, t + KF * h)
                if h == 0:
                    deviation(5)
                    act.wait_ge(x1_stored, 2 * 16 * KD)
                    act.wait_ge(f_lo_made, KF)
                    act.wait_ge(blocks_done, BASE[0]["d"])
                    normed_stream(3, 5, x1_d[1])
                else:
                    act.wait_ge(out_stored, 16 * KD)
                rows_out(6 + h, 16 + KD * h, BASE[h]["d"], len(DOWN), lambda: None)
            final(1)
            act.wait_ge(out_stored, HALVES * 16 * KD)

        @block.vector
        def _(dve):
            tt, ts, stt = nc.vector.tensor_tensor, nc.vector.tensor_scalar, nc.vector.scalar_tensor_tensor

            def open_sum(n):
                wait_pos(dve, stat_mm, n)
                wait_pos(dve, summed, 9 * n)
                nc.vector.memset(acc[:], 0.0).then_inc(summed, 1)

            def add_square(n, t, sem_value):
                dve.wait_ge(*sem_value)
                dve.wait_ge(summed, t + (9 * n + 1))
                tt(acc[:], acc[:], sq[:], ALU.add).then_inc(summed, 1)

            def invert(n):
                dve.wait_ge(dev_made, n + 1)
                nc.vector.reciprocal(rstd_of(n)[:], rstd_of(n)[:]).then_inc(rstd_made, 1)

            def normalise(k, gain, rstd, src, loaded):
                for t in range(KD):
                    dve.wait_ge(*loaded(t))
                    if t >= 2:
                        dve.wait_ge(h_lo_made, KD * k + t - 1)
                    stt(tmp[:, t % 2, :], src(t), col(gain, t), rstd[:], ALU.mult, ALU.mult)\
                        .then_inc(normed, 1)
                    if t >= 1:
                        norm_lo(k, t - 1)
                norm_lo(k, KD - 1)

            def norm_lo(k, t):
                dve.wait_ge(normed, KD * k + t + 1)
                dve.wait_ge(h_hi_made, KD * k + t + 1)
                tt(h_lo[:, t, :], tmp[:, t % 2, :], rd(h_hi[:, t, :]), ALU.subtract)\
                    .then_inc(h_lo_made, 1)

            def xs_at(s):
                return lambda t: (xs_loaded[t % 2], 16 * (4 * s + t // 2 + 1))

            def conv(h, j, q):
                J = j + KR * h
                dve.wait_ge(tap0, J + 1)
                for k in range(1, TAPS):
                    if k > 1:
                        dve.wait_ge(taps, J * 3 + (k - 1))
                    stt(uc[:, q, :], u_raw[:, k:k + T], col("conv_w", j + KR * k), uc[:, q, :],
                        ALU.mult, ALU.add).then_inc(taps, 1)

            def conv_lo(h, j, q):
                J = j + KR * h
                dve.wait_ge(uc_hi_made, J + 1)
                tt(uc_lo[:, q, :], uc[:, q, :], rd(uc_hi[:, q, :]), ALU.subtract)\
                    .then_inc(uc_lo_made, 1)

            def recurrence(h, j, q):
                J = j + KR * h
                dve.wait_ge(i_made, J + 1)
                stt(g_i[:], g_i[:], 1.0, uc[:, q, :], ALU.add, ALU.mult).then_inc(iu_made, 1)
                dve.wait_ge(th1_made, J + 1)
                nc.vector.reciprocal(g_a[:], g_a[:]).then_inc(recip_made, 1)
                dve.wait_ge(root_made, J + 1)
                dve.wait_ge(recip_made, J + 1)
                tt(g_r[:], g_r[:], g_a[:], ALU.mult).then_inc(amp_made, 1)
                dve.wait_ge(amp_made, J + 1)
                dve.wait_ge(iu_made, J + 1)
                tt(g_i[:], g_i[:], g_r[:], ALU.mult).then_inc(b_made, 1)
                dve.wait_ge(b_made, J + 1)
                dve.wait_ge(a_made, J + 1)
                nc.vector.tensor_tensor_scan(g_h[:], g_a[:], g_i[:], h_carry[:, bass.ds(j, 1)],
                                             ALU.mult, ALU.add).then_inc(scanned, 1)
                dve.wait_ge(scanned, J + 1)
                own_wait(dve)
                nc.vector.tensor_copy(h_carry[:, bass.ds(j, 1)], g_h[:, T - 1:T]).then_inc(h_kept, 1)
                dve.wait_ge(gelu_made, J + 1)
                dve.wait_ge(h_kept, J + 1)
                tt(g_h[:], g_h[:], gy[:, q, :], ALU.mult).then_inc(lru_made, 1)
                dve.wait_ge(lru_hi_made, J + 1)
                dve.wait_ge(lru_made, J + 1)
                tt(lru_lo[:, bass.ds(j, 1), :], g_h[:], rd(lru_hi[:, bass.ds(j, 1), :]), ALU.subtract)\
                    .then_inc(lru_lo_made, 1)

            def recurrent(h):
                dve.wait_ge(tap0, KR * h + 1)
                nc.vector.memset(rd(uc_hi[:, 3, :]), 0.0).then_inc(pad_zeroed, 1)
                nc.vector.memset(rd(uc_lo[:, 3, :]), 0.0).then_inc(pad_zeroed, 1)
                for j in range(2):
                    conv(h, j, j)
                    conv_lo(h, j, j)
                if h:
                    residual(0)
                else:
                    open_sum(1)
                    for t in range(KD):
                        add_square(1, t, (squared, KD + t + 1))
                dve.wait_ge(pad_zeroed, 2 * (h + 1))
                with dve.Fori(0, 2) as it:
                    for q in range(4):
                        j = it * 4 + (2 + q)
                        conv(h, j, (2 + q) % 4)
                        conv_lo(h, j, (2 + q) % 4)
                        recurrence(h, j - 2, q)
                invert(3 if h else 1)
                for j in (8, 9):
                    recurrence(h, j, j % 4)

            def kvq(h):
                n = BASE[h]["kv"]
                if h:
                    dve.wait_ge(blocks_done, n)
                    nc.vector.tensor_copy(k_lo[:, :, 0:CH], rd(k_lo[:, :, T:T + CH])).then_inc(kept_lo, 1)
                    nc.vector.tensor_copy(v_lo[0:CH, 0, :], rd(v_lo[0:CH, NCH, :])).then_inc(kept_lo, 1)
                    dve.wait_ge(kept_lo, 2)
                else:
                    dve.wait_ge(zeroed, 7)
                for p in range(PAIRS):
                    dve.wait_ge(k_hi_made, PAIRS * h + p + 1)
                    tt(k_lo[:, p, CH:CH + T], ps[:, p, :], rd(k_hi[:, p, CH:CH + T]), ALU.subtract)\
                        .then_inc(k_lo_made, 1)
                dve.wait_ge(v_hi_made, 3 * h + 1)
                tt(v_lo[:, 1:NCH + 1:2, :], ps[:, 4:8, 0:D_KV], rd(v_hi[:, 1:NCH + 1:2, :]),
                   ALU.subtract).then_inc(v_lo_made, 1)
                dve.wait_ge(v_lo_made, 3 * h + 1)
                nc.vector.tensor_copy(v_lo[CH:P, 0:NCH:2, :], rd(v_lo[0:CH, 1:NCH + 1:2, :]))\
                    .then_inc(v_lo_made, 1)
                nc.vector.tensor_copy(v_lo[0:CH, 2:NCH + 1:2, :], rd(v_lo[CH:P, 1:NCH + 1:2, :]))\
                    .then_inc(v_lo_made, 1)
                with dve.Fori(0, 4) as it:
                    for q in range(2):
                        t = it * 2 + q
                        dve.wait_ge(q_hi_made, t + (KD * h + 1))
                        tt(q_tile(q_lo, it, q), ps[:, q, :].rearrange("p (c t) -> p c t", t=CH),
                           rd(q_tile(q_hi, it, q)), ALU.subtract).then_inc(q_lo_made, 1)

            def attention(h):
                sink = par[:, PARAMS["sink"]:PARAMS["sink"] + 8]
                S = ps[:, BK_S:BK_S + 2, :].rearrange("p b (i k) -> p (b i) k", i=4)
                PT = ps[:, BK_PT:BK_PT + 2, :].rearrange("p b (i k) -> p (b i) k", i=4)

                def softmax_in(C):
                    dve.wait_ge(qk_done, C + 1)
                    wait_pos(dve, pt_done, C)
                    stt(prob[:], S, HD ** -0.5, alibi[:], ALU.mult, ALU.add).then_inc(biased, 1)
                    dve.wait_ge(biased, C + 1)
                    nc.vector.tensor_reduce(stat[:, 0, :], prob[:], AX_X, ALU.max).then_inc(maxed, 1)
                    dve.wait_ge(maxed, C * 4 + 1)
                    tt(stat[:, 0, :], stat[:, 0, :], sink, ALU.max).then_inc(maxed, 1)
                    dve.wait_ge(maxed, C * 4 + 2)
                    tt(stat[:, 1, :], sink, stat[:, 0, :], ALU.subtract).then_inc(maxed, 1)
                    ts(stat[:, 2, :], stat[:, 0, :], -1.0, None, ALU.mult).then_inc(maxed, 1)

                def softmax_out(C):
                    dve.wait_ge(exped, C * 9 + 9)
                    tt(stat[:, 3, :], stat[:, 3, :], stat[:, 4, :], ALU.add).then_inc(probed, 1)
                    dve.wait_ge(probed, C * 3 + 1)
                    nc.vector.reciprocal(stat[:, 5, :], stat[:, 3, :]).then_inc(probed, 1)
                    dve.wait_ge(probed, C * 3 + 2)
                    tt(prob[:], prob[:], stat[:, 5, :].rearrange("p (i o) -> p i o", o=1)
                       .broadcast_to([P, 8, 2 * CH]), ALU.mult).then_inc(probed, 1)

                def out_lo(c, C):
                    for half in range(2):
                        r = slice(64 * half, 64 * half + 64)
                        dve.wait_ge(ao_hi_made, C * 2 + (half + 1))
                        q = (r, slice(None), bass.ds(c * P, P))
                        tt(q_lo[q], ps[r, BK_PV + half, :].rearrange("p (t q) -> p t q", q=P),
                           rd(q_hi[q]), ALU.subtract).then_inc(ao_lo_made, 1)

                def chunk(c, C):
                    softmax_in(C)
                    softmax_out(C)
                    if not isinstance(c, int):
                        out_lo(c - 1, C - 1)
                    dve.wait_ge(ga_made, C + 1)
                    dve.wait_ge(blocks_done, c * 8 + (BASE[h]["a"] + 8))
                    stt(rows[:, bass.ds(c, 1), :], tmp[:, 0, :], 1.0, ps[:, 1, :], ALU.add, ALU.mult)\
                        .then_inc(lru_part, 1)
                    dve.wait_ge(pt_hi_made, C + 1)
                    tt(pt_lo[:], PT, rd(pt_hi[:]), ALU.subtract).then_inc(pt_lo_made, 1)

                dve.wait_ge(alibi_loaded, 16)
                if h:
                    dve.wait_ge(x1_stored, 16 * KD)
                chunk(0, NCH * h)
                dve.wait_ge(alibi_loaded, 32)
                with dve.Fori(1, NCH) as c:
                    chunk(c, c + NCH * h)
                out_lo(NCH - 1, NCH * (h + 1) - 1)

            def attn_branch(h):
                def tile(c, C):
                    dve.wait_ge(gb_made, C + 1)
                    dve.wait_ge(blocks_done, c * 4 + (BASE[h]["b"] + 4))
                    stt(tmp[:, 1, :], tmp[:, 0, :], 1.0, ps[:, 1, :], ALU.add, ALU.mult)\
                        .then_inc(attn_part, 1)
                    dve.wait_ge(attn_part, C + 1)
                    tt(tmp[:, 1, :], tmp[:, 1, :], rows[:, bass.ds(c, 1), :], ALU.add).then_inc(merged, 1)
                    dve.wait_ge(mg_hi_made, C + 1)
                    stt(mg_lo[:, bass.ds(c, 1), :], tmp[:, 1, :], 0.5, rd(mg_hi[:, bass.ds(c, 1), :]),
                        ALU.mult, ALU.subtract).then_inc(mg_lo_made, 1)

                tile(0, KD * h)
                with dve.Fori(1, KD) as c:
                    dve.wait_ge(mg_lo_made, c + KD * h)
                    tile(c, c + KD * h)

            def rows_in(n, r0, between):
                open_sum(n)
                for t in range(2):
                    add_square(n, t, (row_out, 2 * (r0 + t + 1)))
                between()
                with dve.Fori(2, KD) as t:
                    add_square(n, t, (row_out, t * 2 + 2 * (r0 + 1)))

            def residual(h):
                n = 2 + 2 * h
                invert(n)
                open_sum(n + 1)
                add_norm(n, "g_post_mix", KD * h, 2 + 2 * h, n + 1)

            def add_norm(n, gain, a0, s, nn):
                dve.wait_ge(rstd_made, n + 1)
                for t in range(KD):
                    stt(rows[:, t, :], rows[:, t, :], col(gain, t), rstd_of(n)[:], ALU.mult, ALU.mult)\
                        .then_inc(scaled, 1)
                    dve.wait_ge(scaled, a0 + t + 1)
                    dve.wait_ge(*xs_at(s)(t))
                    tt(rows[:, t, :], rows[:, t, :], xs[:, t % 2, :], ALU.add).then_inc(added, 1)
                    if nn is not None and t:
                        add_square(nn, t - 1, (squared, sq_base(nn) + t))
                if nn is not None:
                    add_square(nn, KD - 1, (squared, sq_base(nn) + KD))

            def sq_base(n):
                return KD * {0: 0, 1: 1, 3: 2, 5: 3}[n]

            open_sum(0)
            for t in range(KD):
                add_square(0, t, (squared, t + 1))
            dve.wait_ge(par_loaded, 32)
            done = [0]

            def step(ins):
                done[0] += 1
                ins.then_inc(prep_dve, 1)
                dve.wait_ge(prep_dve, done[0])

            step(ts(half_b[:], par[:, HALVED:N_PARAMS], 0.5, None, ALU.mult))
            invert(0)
            dve.wait_ge(rstd_made, 1)
            dve.wait_ge(prep_act, 2)
            e, s, s2, poly = sp[:, 1, :], sp[:, 0, :], sp[:, 2, :], sp[:, 3, :]
            step(ts(s, e, 2.0, None, ALU.add))
            step(nc.vector.reciprocal(s2, s))
            step(tt(s, e, s2, ALU.mult))
            step(tt(s2, s, s, ALU.mult))
            step(ts(poly, s2, 1.0 / 17, None, ALU.mult))
            for m in (15, 13, 11, 9, 7, 5, 3):
                step(stt(poly, poly, 1.0 / m, s2, ALU.add, ALU.mult))
            step(stt(poly, poly, 1.0, s, ALU.add, ALU.mult))
            step(ts(s2, par[:, PARAMS["lam"]:PARAMS["lam"] + KR], -2.0, 0.0, ALU.mult, ALU.max))
            step(stt(sp2[:], poly, 4.0, s2, ALU.mult, ALU.add))
            normalise(0, "g_pre_mix", rstd_a, lambda t: rows[:, t, :], lambda t: (x0_loaded, 16 * KD))

            for h in range(HALVES):
                recurrent(h)
                kvq(h)
                attention(h)
                attn_branch(h)
                dve.wait_ge(mg_lo_made, KD * (h + 1))
                if h == 0:
                    rows_in(2, 0, lambda: normalise(1, "g_pre_mix", rstd_b,
                                                    lambda t: xs[:, t % 2, :], xs_at(1)))
                else:
                    rows_in(4, KD, lambda: normalise(2, "g_pre_ffn", rstd_b,
                                                     lambda t: xs[:, t % 2, :], xs_at(3)))
            for h in range(HALVES):
                def tile(t, F):
                    dve.wait_ge(silu_made, F + 1)
                    dve.wait_ge(blocks_done, t * 4 + (BASE[h]["f"] + 4))
                    if not isinstance(F, int) or F:
                        dve.wait_ge(f_lo_made, F)
                    tt(tmp[:, 1, :], ps[:, 1, :], tmp[:, 0, :], ALU.mult).then_inc(f_made, 1)
                    dve.wait_ge(f_hi_made, F + 1)
                    dve.wait_ge(f_made, F + 1)
                    tt(f_lo[:, bass.ds(t, 1), :], tmp[:, 1, :], rd(f_hi[:, bass.ds(t, 1), :]),
                       ALU.subtract).then_inc(f_lo_made, 1)

                for t in range(2):
                    tile(t, KF * h + t)
                if h == 0:
                    residual(1)
                else:
                    invert(6)
                    add_norm(6, "g_post_ffn", 2 * KD, 6, None)
                with dve.Fori(2, KF) as t:
                    tile(t, t + KF * h)
                if h == 0:
                    dve.wait_ge(f_lo_made, KF)
                    invert(5)
                    dve.wait_ge(rstd_made, 6)
                    normalise(3, "g_pre_ffn", rstd_b, lambda t: xs[:, t % 2, :], xs_at(5))
                rows_in(6 + h, 16 + KD * h, lambda: None)
            invert(7)
            add_norm(7, "g_post_ffn", 3 * KD, 7, None)


def k_tiles(w):
    return w.reshape(-1, P, w.shape[1]).transpose(1, 0, 2)


def cols(w, c):
    return k_tiles(w[:, c * P:(c + 1) * P]).reshape(P, -1)


def weight_streams(w_in, w_rg, w_ig, w_lru_br, w_attn_br, w_out, w_gate, w_up, w_down):
    bounds = np.cumsum([0, D_RNN, D_RNN, HEADS * HD, D_KV, D_KV, D, D])
    u, y, q, k, v, gl, ga = [w_in[:, bounds[i]:bounds[i + 1]] for i in range(7)]
    order = [(2 * p + half) * GRP + a for p in range(PAIRS) for a in range(GRP) for half in range(2)]
    q = q.reshape(D, HEADS, HD)[:, order].reshape(D, -1)
    w_attn_br = w_attn_br.reshape(HEADS, HD, D)[order].reshape(-1, D)

    def gate(w, j, last=False):
        full = np.zeros((D_RNN + 2 * P, D_RNN), w.dtype)
        for b in range(N_BLK):
            full[P + b * BLK:P + (b + 1) * BLK, b * BLK:(b + 1) * BLK] = w[b]
        part = full[j * P:(j + (2 if last else 3)) * P, j * P:(j + 1) * P]
        return k_tiles(part).reshape(P, -1)

    def cat(*parts):
        return np.concatenate(parts, axis=1)

    return {
        "head": np.stack([cat(cols(u, j), cols(y, j)) for j in range(2)]),
        "step": np.stack([cat(*[x for jj in (j, j + 1)
                                for x in (cols(u, jj), gate(w_rg, jj - 2), gate(w_ig, jj - 2), cols(y, jj))])
                          for j in range(2, KR, 2)]),
        "tail": cat(gate(w_rg, 8), gate(w_ig, 8), gate(w_rg, 9, True), gate(w_ig, 9, True))[None],
        "kv": cat(cols(k, 0), cols(k, 1), k_tiles(v).reshape(P, -1))[None],
        "q": np.stack([cat(cols(q, t), cols(q, t + 1)) for t in range(0, KD, 2)]),
        "a": np.stack([cat(cols(gl, c), cols(w_lru_br, c)) for c in range(KD)]),
        "b": np.stack([cat(cols(ga, c), cols(w_attn_br, c)) for c in range(KD)]),
        "o": np.stack([cat(cols(w_out, t), cols(w_out, t + 1)) for t in range(0, KD, 2)]),
        "f": np.stack([cat(cols(w_gate, t), cols(w_up, t)) for t in range(KF)]),
        "d": np.stack([cat(cols(w_down, t), cols(w_down, t + 1)) for t in range(0, KD, 2)]),
    }


def by_tile(v):
    return v.reshape(-1, P).T


def score_heads():
    p = np.arange(P)[:, None]
    i = np.arange(8)[None, :]
    half, pair, b = i // 4, i // 2 % 2, i % 2
    return (2 * pair + half) * GRP + 2 * b + p // CH


def alibi_tables():
    slope = np.exp2(-8.0 * (np.arange(HEADS, dtype=np.float32) + 1) / HEADS).astype(np.float32)
    qi = np.arange(P)[:, None] % CH
    dist = np.abs(qi + CH - np.arange(2 * CH)[None, :]).astype(np.float32)
    table = -slope[score_heads()][:, :, None] * dist[:, None, :]
    masked = table.copy()
    masked[:, :, :CH] = MASKED
    return np.stack([masked, table]).astype(np.float32)


def kernel(**inputs):
    import concourse.bacc as bacc
    from concourse.bass_utils import run_bass_kernel_spmd as run

    a = {k: np.asarray(v) for k, v in inputs.items()}
    one = {k: v[0] for k, v in a.items()}
    table = [by_tile(one["norm_pre_mix"]), by_tile(one["norm_post_mix"]),
             by_tile(one["norm_pre_ffn"]), by_tile(one["norm_post_ffn"]),
             np.concatenate([by_tile(one["conv_w"][k]) for k in range(TAPS)], axis=1),
             by_tile(one["conv_b"]), by_tile(one["lru_lambda"]), one["attn_sinks"][score_heads()],
             by_tile(one["b_rg"]), by_tile(one["b_ig"]),
             by_tile(one["b_gate"][:D]), by_tile(one["b_gate"][D:])]
    arrays = {
        "x_t": one["x"].T.reshape(KD, P, HALVES, T).transpose(2, 0, 1, 3),
        "params": np.concatenate(table, axis=1),
        "alibi_in": alibi_tables(),
        "eye_in": np.eye(P, dtype=np.float32),
    }
    streams = weight_streams(one["w_in"], one["w_rg"], one["w_ig"], one["w_lru_br"],
                             one["w_attn_br"], one["w_out"], one["w_ffn_gate"], one["w_ffn_up"],
                             one["w_ffn_down"])
    arrays.update({f"w_{name}": w for name, w in streams.items()})
    arrays = {k: np.ascontiguousarray(v) for k, v in arrays.items()}

    nc = bacc.Bacc("TRN2", target_bir_lowering=False, num_devices=1)
    dram = {k: nc.dram_tensor(k, v.shape, F32, kind="ExternalInput").ap() for k, v in arrays.items()}
    x1 = nc.dram_tensor("x1_scratch", (HALVES, KD, P, T), F32).ap()
    out = nc.dram_tensor("out_t", (HALVES, KD, P, T), F32, kind="ExternalOutput").ap()
    build(nc, dram["x_t"], dram["params"], dram["alibi_in"], dram["eye_in"],
          {name: dram[f"w_{name}"] for name in streams}, x1, out)
    r = run(nc, [arrays], core_ids=[0])
    got = r.results[0]["out_t"]
    return np.ascontiguousarray(got.transpose(0, 3, 1, 2).reshape(1, SEQ, D))
```

```python
from contextlib import ExitStack

import numpy as np

import concourse.bass as bass
from concourse import mybir

F32 = mybir.dt.float32
F32R = mybir.dt.float32r
ACT = mybir.ActivationFunctionType
ALU = mybir.AluOpType
AX_X = mybir.AxisListType.X

P = 128
D = 1024
KD = D // P
SEQ = 1024
T = 512
HALVES = SEQ // T
D_RNN = 1280
KR = D_RNN // P
N_BLK = 16
BLK = D_RNN // N_BLK
TAPS = 4
HEADS, KV_HEADS, HD = 16, 4, 64
GRP = HEADS // KV_HEADS
D_KV = KV_HEADS * HD
PAIRS = KV_HEADS // 2
CH = 64
NCH = T // CH
D_FF = 2816
KF = D_FF // P
EPS = 1e-6
LRU_C = 8.0
MASKED = -1e30

RING = 4
CAP = 4 * P
UNIT = [4, 4]
GATE = [3, 3]
L_HEAD = UNIT + UNIT
L_STEP = UNIT + GATE + UNIT
L_TAIL = UNIT + [3, 3] + UNIT + [2, 2]
V_BLOCKS = [4, 4, 4, 4]
A_STEP = [2, 2, 2, 2] + [3, 3, 2, 2]
B_STEP = UNIT + UNIT
F_STEP = UNIT + UNIT
DOWN = [4, 4, 4, 4, 3, 3]

MIX_STAGES = [("head", L_HEAD, 2), ("step", L_STEP, KR - 2), ("tail", L_TAIL, 1), ("v", V_BLOCKS, 1),
              ("q", UNIT, KD), ("a", A_STEP, KD), ("b", B_STEP, KD), ("o", UNIT, KD)]
FFN_STAGES = [("f", F_STEP, KF), ("d", DOWN, KD)]


def stage_bases(stages, base):
    out = {}
    for name, sizes, groups in stages:
        out[name] = base
        base += len(sizes) * groups
    return out, base


BASE = []
_n = 0
for _h in range(HALVES):
    _b, _n = stage_bases(MIX_STAGES, _n)
    BASE.append(_b)
for _h in range(HALVES):
    _b, _n = stage_bases(FFN_STAGES, _n)
    BASE[_h].update(_b)
N_BLOCKS = _n

PARAMS = {}
_at = 0
for _name, _w in [("g_pre_mix", KD), ("g_post_mix", KD), ("g_pre_ffn", KD), ("g_post_ffn", KD),
                  ("conv_w", TAPS * KR), ("conv_b", KR), ("lam", KR), ("sink", 8),
                  ("b_rg", KR), ("b_ig", KR), ("b_gate_lru", KD), ("b_gate_attn", KD)]:
    PARAMS[_name] = _at
    _at += _w
N_PARAMS = _at
PREP_STEPS = 16
DVE_LAST = 5
HALVED = PARAMS["b_rg"]


def build(nc, x_d, par_d, alibi_d, eye_d, w_d, x1_d, out_d):
    with ExitStack() as ctx:
        cursor = [0]

        def at(name, shape, dt, offset=None):
            size = 4 * int(np.prod(shape[1:]))
            size = (size + 31) // 32 * 32
            if offset is None:
                offset = cursor[0]
                cursor[0] += size
            return nc.alloc_sbuf_tensor_at(name, shape, dt, offset=offset + sbuf0)

        def sem(name):
            return ctx.enter_context(nc.semaphore(name))

        sbuf0 = (nc.sbuf_base + 31) // 32 * 32

        w_raw = at("w_raw", [P, RING, CAP], F32)
        w_hi = at("w_hi", [P, RING, CAP], F32R)
        w_lo = at("w_lo", [P, RING, CAP], F32R)
        par = at("par", [P, N_PARAMS], F32)
        half_b = at("half_b", [P, N_PARAMS - HALVED], F32)
        sp = at("sp", [P, 4, KR], F32)
        sp2 = at("sp2", [P, KR], F32)
        ones = at("ones", [P, P], F32)
        eye = at("eye", [P, P], F32)
        alibi = at("alibi", [P, 8, 2 * CH], F32)
        u_carry = at("u_carry", [P, KR, TAPS - 1], F32)
        h_carry = at("h_carry", [P, KR], F32)
        stat = at("stat", [P, 6, 8], F32)
        acc = at("acc", [P, T], F32)
        sq = at("sq", [P, T], F32)
        rstd_a = at("rstd_a", [P, T], F32)
        rstd_b = at("rstd_b", [P, T], F32)
        tmp = at("tmp", [P, 2, T], F32)
        xs = at("xs", [P, 2, T], F32)
        reg_h = cursor[0]
        h_hi = at("h_hi", [P, KD, T], F32R)
        x1_all = at("x1_all", [P, KD, T], F32, reg_h)
        h_lo = at("h_lo", [P, KD, T], F32R)
        rows = at("rows", [P, KD, T], F32)
        reg_b = cursor[0]
        lru_hi = at("lru_hi", [P, KR, T], F32R)
        lru_lo = at("lru_lo", [P, KR, T], F32R)
        mg_hi = at("mg_hi", [P, KD, T], F32R, reg_b)
        mg_lo = at("mg_lo", [P, KD, T], F32R, reg_b + 4 * KD * T)
        reg_c = cursor[0]
        q_hi = at("q_hi", [P, KD // 2, 2 * T], F32R)
        q_lo = at("q_lo", [P, KD // 2, 2 * T], F32R)
        uc_hi = at("uc_hi", [P, 4, T], F32R, reg_c)
        uc_lo = at("uc_lo", [P, 4, T], F32R, reg_c + 16 * T)
        uc = at("uc", [P, 4, T], F32, reg_c + 32 * T)
        gy = at("gy", [P, 4, T], F32, reg_c + 48 * T)
        reg_p = cursor[0]
        prob = at("prob", [P, 8, 2 * CH], F32)
        pt_hi = at("pt_hi", [P, 8, 2 * CH], F32R)
        pt_lo = at("pt_lo", [P, 8, 2 * CH], F32R)
        g_r = at("g_r", [P, T], F32, reg_p)
        g_a = at("g_a", [P, T], F32, reg_p + 4 * T)
        g_i = at("g_i", [P, T], F32, reg_p + 8 * T)
        g_h = at("g_h", [P, T], F32, reg_p + 12 * T)
        u_raw = at("u_raw", [P, TAPS - 1 + T], F32, reg_p + 16 * T)
        k_hi = at("k_hi", [P, PAIRS, CH + T], F32R)
        k_lo = at("k_lo", [P, PAIRS, CH + T], F32R)
        v_hi = at("v_hi", [P, NCH + 1, D_KV], F32R)
        v_lo = at("v_lo", [P, NCH + 1, D_KV], F32R)
        f_hi = at("f_hi", [P, KF, T], F32R, reg_b)
        f_lo = at("f_lo", [P, KF, T], F32R, reg_b + 4 * KF * T)
        assert reg_b + 8 * KF * T <= cursor[0]
        assert sbuf0 + cursor[0] <= nc.sbuf_usable_end, (sbuf0 + cursor[0], nc.sbuf_usable_end)

        ps = ctx.enter_context(nc.psum_tensor("ps", [P, 8, 512], F32))
        BK_STAT = 3
        BK_K = (1, 0)
        BK_V = (2, 3, 6, 7)
        v_out = ps.rearrange("p (a b) n -> p a b n", b=4)[:, :, 2:4, 0:D_KV]
        BK_S, BK_PT, BK_PV = 2, 4, 6

        w_loaded = [sem(f"w_loaded{i}") for i in range(RING)]
        par_loaded = sem("par_loaded")
        x0_loaded = [sem(f"x0_loaded{t}") for t in range(KD)]
        x1_all_loaded = sem("x1_all_loaded")
        alibi_loaded = sem("alibi_loaded")
        xs_loaded = [sem(f"xs_loaded{i}") for i in range(2)]
        x1_stored, out_stored = sem("x1_stored"), sem("out_stored")
        w_hi_made, w_lo_made = sem("w_hi_made"), sem("w_lo_made")
        blocks_done = sem("blocks_done")
        prep_act, prep_dve, zeroed = sem("prep_act"), sem("prep_dve"), sem("zeroed")
        squared, summed, stat_mm, dev_made, rstd_made = (
            sem("squared"), sem("summed"), sem("stat_mm"), sem("dev_made"), sem("rstd_made"))
        normed, h_hi_made, h_lo_made = sem("normed"), sem("h_hi_made"), sem("h_lo_made")
        u_ctx, u_copied, tap0, taps, uc_hi_made, uc_lo_made, pad_zeroed = (
            sem("u_ctx"), sem("u_copied"), sem("tap0"), sem("taps"), sem("uc_hi_made"),
            sem("uc_lo_made"), sem("pad_zeroed"))
        r_made, i_made, th_made, th1_made, root_made, a_made, gelu_made, lru_hi_made = (
            sem("r_made"), sem("i_made"), sem("th_made"), sem("th1_made"), sem("root_made"),
            sem("a_made"), sem("gelu_made"), sem("lru_hi_made"))
        iu_made, recip_made, amp_made, b_made, scanned, h_kept, lru_made, lru_lo_made = (
            sem("iu_made"), sem("recip_made"), sem("amp_made"), sem("b_made"), sem("scanned"),
            sem("h_kept"), sem("lru_made"), sem("lru_lo_made"))
        kept_hi, kept_lo = sem("kept_hi"), sem("kept_lo")
        k_hi_made, k_lo_made, v_hi_made, v_lo_made = (
            sem("k_hi_made"), sem("k_lo_made"), sem("v_hi_made"), sem("v_lo_made"))
        q_hi_made, q_lo_made = sem("q_hi_made"), sem("q_lo_made")
        qk_done, biased, maxed, exped, probed, pt_done, pt_hi_made, pt_lo_made, pv_done = (
            sem("qk_done"), sem("biased"), sem("maxed"), sem("exped"), sem("probed"),
            sem("pt_done"), sem("pt_hi_made"), sem("pt_lo_made"), sem("pv_done"))
        ao_hi_made, ao_lo_made = sem("ao_hi_made"), sem("ao_lo_made")
        ga_made, lru_part = sem("ga_made"), sem("lru_part")
        gb_made, attn_part, merged, mg_hi_made, mg_lo_made = (
            sem("gb_made"), sem("attn_part"), sem("merged"), sem("mg_hi_made"), sem("mg_lo_made"))
        row_out = sem("row_out")
        silu_made, f_made, f_hi_made, f_lo_made = (
            sem("silu_made"), sem("f_made"), sem("f_hi_made"), sem("f_lo_made"))
        scaled, added = sem("scaled"), sem("added")
        pool_scaled, pool_added = sem("pool_scaled"), sem("pool_added")
        waits_closed = sem("waits_closed")

        def wait_pos(eng, s, value):
            if not isinstance(value, int) or value > 0:
                eng.wait_ge(s, value)

        def own_wait(eng):
            eng.sem_inc(waits_closed, 1)

        def col(name, t, n=1):
            return par[:, bass.ds(t + PARAMS[name], n)]

        def half_col(name, t):
            return half_b[:, bass.ds(t + (PARAMS[name] - HALVED), 1)]

        def q_tile(q, pair, j):
            return q[:, bass.ds(pair, 1), :].rearrange("p o (c j t) -> p (o c) j t", j=2, t=CH)[:, :, j, :]

        def v_whole(v):
            return v[:, 1:NCH + 1:2, :].rearrange("p (a b) n -> p a b n", b=2)

        def rd(ap):
            return ap.bitcast(F32)

        def rstd_of(n):
            return rstd_b if n in (1, 3, 5) else rstd_a

        block = ctx.enter_context(nc.Block())

        @block.sync
        def _(sp_eng):
            def load(dram, g, sizes, n, off0=0):
                off = 0
                for b, size in enumerate(sizes):
                    wait_pos(sp_eng, w_lo_made, n + b - RING + 1)
                    sp_eng.dma_start(w_raw[:, b % RING, 0:size * P],
                                     dram[g, :, off:off + size * P]).then_inc(w_loaded[b % RING], 16)
                    off += size * P

            def stream(stages, bases):
                for name, sizes, groups in stages:
                    per = 1 if len(sizes) % RING == 0 else 2
                    sizes2, dram, base = sizes * per, w_d[name], bases[name]
                    n_it = groups // per
                    first = 1 if base == 0 else 0
                    if first:
                        load(dram, 0, sizes2, 0)
                    if n_it - first == 1:
                        load(dram, first, sizes2, base + first * len(sizes2))
                    elif n_it > first:
                        with sp_eng.Fori(first, n_it) as g:
                            load(dram, g, sizes2, g * len(sizes2) + base)

            for t in range(0, KD, 2):
                sp_eng.dma_start(rows[:, t, :], x_d[0][t]).then_inc(x0_loaded[t], 16)
            for h in range(HALVES):
                stream(MIX_STAGES, BASE[h])
            for h in range(HALVES):
                stream(FFN_STAGES, BASE[h])

        @block.gpsimd
        def _(pool):
            nc.gpsimd.memset(ones[:], 1.0).then_inc(zeroed, 1)
            nc.gpsimd.memset(u_carry[:], 0.0).then_inc(zeroed, 1)
            nc.gpsimd.memset(h_carry[:], 0.0).then_inc(zeroed, 1)
            nc.gpsimd.memset(rd(k_hi[:, :, 0:CH]), 0.0).then_inc(zeroed, 1)
            nc.gpsimd.memset(rd(k_lo[:, :, 0:CH]), 0.0).then_inc(zeroed, 1)
            nc.gpsimd.memset(rd(v_hi[0:CH, 0, :]), 0.0).then_inc(zeroed, 1)
            nc.gpsimd.memset(rd(v_lo[0:CH, 0, :]), 0.0).then_inc(zeroed, 1)

            def split(sizes, n, turn):
                for b, size in enumerate(sizes):
                    s, w = b % RING, slice(0, size * P)
                    pool.wait_ge(w_loaded[s], (turn + b // RING + 1) * 16)
                    wait_pos(pool, blocks_done, n + b - RING + 1)
                    own_wait(pool)
                    nc.gpsimd.tensor_scalar(w_hi[:, s, w], w_raw[:, s, w], 1.0, 0.0,
                                            ALU.mult, ALU.add).then_inc(w_hi_made, 1)
                    pool.wait_ge(w_hi_made, n + b + 1)
                    nc.gpsimd.tensor_tensor(w_lo[:, s, w], w_raw[:, s, w], rd(w_hi[:, s, w]),
                                            ALU.subtract).then_inc(w_lo_made, 1)

            def stream(stages, bases):
                for name, sizes, groups in stages:
                    per = 1 if len(sizes) % RING == 0 else 2
                    sizes2, base = sizes * per, bases[name]
                    n_it = groups // per
                    first = 1 if base == 0 else 0
                    assert base % RING == 0 and len(sizes2) % RING == 0
                    turns = len(sizes2) // RING
                    if first:
                        split(sizes2, 0, 0)
                    if n_it - first == 1:
                        split(sizes2, base + first * len(sizes2), base // RING + first * turns)
                    elif n_it > first:
                        with pool.Fori(first, n_it) as g:
                            split(sizes2, g * len(sizes2) + base, g * turns + base // RING)

            for h in range(HALVES):
                stream(MIX_STAGES, BASE[h])
            for h in range(HALVES):
                stream(FFN_STAGES, BASE[h])

            pool.wait_ge(rstd_made, 8)
            pool.wait_ge(row_out, 2 * KD * 4)
            for i, t in enumerate(range(DVE_LAST, KD)):
                nc.gpsimd.tensor_tensor(rows[:, t, :], rows[:, t, :], rstd_a[:], ALU.mult)\
                    .then_inc(pool_scaled, 1)
                pool.wait_ge(x1_all_loaded, 16 * KD)
                pool.wait_ge(pool_scaled, i + 1)
                nc.gpsimd.tensor_tensor(rows[:, t, :], rows[:, t, :], x1_all[:, t, :], ALU.add)\
                    .then_inc(pool_added, 1)

        @block.tensor
        def _(pe):
            mm = nc.tensor.matmul

            def project(bank, n, slot, sizes, hi, lo, ready=None, tiles=None, inner=None):
                total, k = sum(sizes), 0
                out = ps[:, bank, :] if isinstance(bank, int) else ps[:, bass.ds(bank, 1), :]
                for b, size in enumerate(sizes):
                    pe.wait_ge(w_lo_made, n + b + 1)
                    s = (slot + b) % RING
                    for q in range(size):
                        if ready:
                            pe.wait_ge(ready[0], ready[1] + k + 1)
                        w = slice(q * P, (q + 1) * P)
                        kk = tiles[k] if tiles else k
                        if hi is q_hi:
                            x_hi, x_lo = q_tile(hi, kk // 2, kk % 2), q_tile(lo, kk // 2, kk % 2)
                        else:
                            x_hi, x_lo = hi[:, kk, :], lo[:, kk, :]
                        mm(out, w_hi[:, s, w], x_hi, start=(k == 0), stop=False)
                        mm(out, w_hi[:, s, w], x_lo, start=False, stop=False)
                        last = mm(out, w_lo[:, s, w], x_hi, start=False,
                                  stop=(k == total - 1))
                        k += 1
                    last.then_inc(blocks_done, 1)
                    if inner and b == 0:
                        inner()

            def stat_sum(n):
                pe.wait_ge(summed, 9 * (n + 1))
                wait_pos(pe, dev_made, n)
                wait_pos(pe, biased, NCH * min((n + 1) // 2, HALVES))
                mm(ps[:, BK_STAT, :], ones[:], acc[:], start=True, stop=True).then_inc(stat_mm, 1)

            def gates(h, j, n, size, slot, q, first=None):
                J = j + KR * h
                last_tile = size == 2 and first is None
                pe.wait_ge(uc_lo_made, J + (1 if last_tile else 2))
                if last_tile:
                    pe.wait_ge(r_made, J)
                    pe.wait_ge(i_made, J)
                tiles = first or [(q + d) % 4 for d in (-1, 0, 1)][:size]
                for g in range(2):
                    project(4 + g, n + g, slot + g, [size], uc_hi, uc_lo, tiles=tiles)

            def head(h, j, ready):
                n = BASE[h]["head"] + 4 * j
                wait_pos(pe, u_copied, (j + KR * h) * 2)
                wait_pos(pe, gelu_made, j + KR * h)
                for b in range(2):
                    for u, bank in enumerate((0, 2)):
                        pe.wait_ge(w_lo_made, n + 2 * b + u + 1)
                        for q in range(4):
                            k, w = 4 * b + q, slice(q * P, (q + 1) * P)
                            if ready:
                                pe.wait_ge(h_lo_made, KD * h + k + 1)
                            s = 2 * b + u
                            mm(ps[:, bank, :], w_hi[:, s, w], h_hi[:, k, :], start=(k == 0), stop=False)
                            mm(ps[:, bank, :], w_hi[:, s, w], h_lo[:, k, :], start=False, stop=False)
                            last = mm(ps[:, bank, :], w_lo[:, s, w], h_hi[:, k, :], start=False,
                                      stop=(k == KD - 1))
                        last.then_inc(blocks_done, 1)

            def recurrent(h):
                if h:
                    pe.wait_ge(row_out, 2 * 3)
                for j in range(2):
                    head(h, j, j == 0)
                if h:
                    stat_sum(2)
                pe.wait_ge(pad_zeroed, 2 * (h + 1))
                with pe.Fori(0, 2) as it:
                    for q in range(4):
                        j = it * 4 + (2 + q)
                        n = (it * 4 + q) * 6 + BASE[h]["step"]
                        slot = 6 * q
                        wait_pos(pe, u_copied, (j + KR * h) * 2)
                        project(0, n, slot, UNIT, h_hi, h_lo)
                        gates(h, j - 2, n + 2, 3, slot + 2, q)
                        wait_pos(pe, gelu_made, j + KR * h)
                        project(2, n + 4, slot + 4, UNIT, h_hi, h_lo)

            def kvq(h):
                n, n_v, n_q = BASE[h]["tail"], BASE[h]["v"], BASE[h]["q"]
                wait_pos(pe, row_out, 2 * KD * h)
                project(BK_K[0], n, 0, UNIT, h_hi, h_lo)
                gates(h, 8, n + 2, 3, 2, 0)
                pe.wait_ge(u_copied, 2 * KR * (h + 1))
                project(BK_K[1], n + 4, 0, UNIT, h_hi, h_lo)
                gates(h, 9, n + 6, 2, 2, 1)
                pe.wait_ge(gelu_made, KR * (h + 1))
                pe.wait_ge(dev_made, 3 if h else 1)
                for b in range(4):
                    pe.wait_ge(w_lo_made, n_v + b + 1)
                    for m in range(4):
                        out = ps[:, BK_V[m], 0:D_KV]
                        for q in range(2):
                            k = 2 * b + q
                            w = slice(q * D_KV, (q + 1) * D_KV)
                            t = slice(m * P, (m + 1) * P)
                            mm(out, h_hi[:, k, t], w_hi[:, b, w], start=(k == 0), stop=False)
                            mm(out, h_lo[:, k, t], w_hi[:, b, w], start=False, stop=False)
                            last = mm(out, h_hi[:, k, t], w_lo[:, b, w], start=False, stop=(k == KD - 1))
                    last.then_inc(blocks_done, 1)
                pe.wait_ge(k_hi_made, PAIRS * (h + 1))
                pe.wait_ge(k_lo_made, PAIRS * (h + 1))
                for t in range(2):
                    project(t, n_q + 2 * t, 2 * t, UNIT, h_hi, h_lo)
                with pe.Fori(1, 4) as it:
                    for q in range(2):
                        t = it * 2 + q
                        pe.wait_ge(q_lo_made, t + (KD * h - 1))
                        project(q, t * 2 + n_q, 2 * q, UNIT, h_hi, h_lo)

            def scores(h, c):
                C = NCH * h + c
                pe.wait_ge(biased, C) if C else None
                for p in range(PAIRS):
                    for b in range(2):
                        for half in range(2):
                            r = slice(64 * half, 64 * half + 64)
                            i = 2 * p + b
                            out = ps[:, BK_S + half, i * P:(i + 1) * P]
                            t = 2 * p + b
                            cq = slice(c * P, (c + 1) * P)
                            ck = slice(c * CH, (c + 2) * CH)
                            mm(out, q_hi[r, t, cq], k_hi[r, p, ck], start=True, stop=False)
                            mm(out, q_hi[r, t, cq], k_lo[r, p, ck], start=False, stop=False)
                            last = mm(out, q_lo[r, t, cq], k_hi[r, p, ck], start=False, stop=True)
                last.then_inc(qk_done, 1)

            def turn_probs(h, c):
                C = NCH * h + c
                pe.wait_ge(probed, 3 * (C + 1))
                wait_pos(pe, pt_lo_made, C)
                for i in range(8):
                    last = nc.tensor.transpose(ps[:, BK_PT + i // 4, (i % 4) * P:(i % 4 + 1) * P],
                                               prob[:, i, :], eye[:])
                last.then_inc(pt_done, 1)

            def weigh_values(h, c):
                C = NCH * h + c
                pe.wait_ge(pt_lo_made, C + 1)
                wait_pos(pe, ao_lo_made, 2 * C)
                for half in range(2):
                    for p in range(PAIRS):
                        out = ps[:, BK_PV + half, p * 256:(p + 1) * 256]
                        v = slice(p * P, (p + 1) * P)
                        t = slice(4 * half + 2 * p, 4 * half + 2 * p + 2)
                        mm(out, v_hi[:, c, v], pt_hi[:, t, :], start=True, stop=False)
                        mm(out, v_hi[:, c, v], pt_lo[:, t, :], start=False, stop=False)
                        last = mm(out, v_lo[:, c, v], pt_hi[:, t, :], start=False, stop=True)
                last.then_inc(pv_done, 1)

            def attention(h):
                pe.wait_ge(q_lo_made, KD * (h + 1))
                for c in range(NCH):
                    n = BASE[h]["a"] + 8 * c
                    if c == 0:
                        def begin():
                            pe.wait_ge(v_hi_made, 3 * (h + 1))
                            pe.wait_ge(v_lo_made, 3 * (h + 1))
                            scores(h, 0)

                        project(0, n, 0, A_STEP[:4], h_hi, h_lo, inner=begin)
                        pe.wait_ge(lru_lo_made, KR * (h + 1))
                    else:
                        scores(h, c)
                        pe.wait_ge(ga_made, NCH * h + c)
                        project(0, n, 0, A_STEP[:4], h_hi, h_lo)
                        weigh_values(h, c - 1)
                        pe.wait_ge(lru_part, NCH * h + c)
                    project(1, n + 4, 0, A_STEP[4:], lru_hi, lru_lo)
                    if c == 0:
                        pe.wait_ge(r_made, KR * (h + 1))
                        pe.wait_ge(i_made, KR * (h + 1))
                    turn_probs(h, c)

            def attn_branch(h):
                base = BASE[h]["b"]
                pe.wait_ge(ga_made, NCH * (h + 1))
                project(0, base, 0, UNIT, h_hi, h_lo, inner=lambda: weigh_values(h, NCH - 1))
                pe.wait_ge(lru_part, NCH * (h + 1))
                pe.wait_ge(ao_lo_made, 2 * NCH * (h + 1))
                project(1, base + 2, 2, UNIT, q_hi, q_lo)
                stat_sum(1 + 2 * h)
                with pe.Fori(1, KD) as c:
                    pe.wait_ge(gb_made, c + KD * h)
                    project(0, c * 4 + base, 0, UNIT, h_hi, h_lo)
                    pe.wait_ge(attn_part, c + KD * h)
                    project(1, c * 4 + (base + 2), 2, UNIT, q_hi, q_lo)

            def out_tiles(base, sizes, hi, lo, bank0, bank1, ready):
                for t in range(2):
                    pe.wait_ge(*(bank1 if t else bank0))
                    project(t, base + len(sizes) * t, len(sizes) * t, sizes, hi, lo,
                            None if t else ready[:2])
                pe.wait_ge(dev_made, ready[2])
                with pe.Fori(1, KD // 2) as it:
                    for q in range(2):
                        t = it * 2 + q
                        project(t, t * len(sizes) + base, len(sizes) * q, sizes, hi, lo)

            def ffn_up(h):
                base = BASE[h]["f"]

                for t in range(2):
                    if t == 0:
                        pe.wait_ge(row_out, 2 * (KD * (1 + h) + 1))
                    else:
                        pe.wait_ge(silu_made, KF * h + t)
                    project(0, base + 4 * t, 0, UNIT, h_hi, h_lo,
                            (h_lo_made, KD * (2 + h)) if t == 0 else None)
                    if t == 0:
                        pe.wait_ge(row_out, 2 * (KD * (1 + h) + 2))
                    else:
                        pe.wait_ge(f_made, KF * h + t)
                    project(1, base + 4 * t + 2, 2, UNIT, h_hi, h_lo)
                stat_sum(6 if h else 4)
                with pe.Fori(2, KF) as t:
                    pe.wait_ge(silu_made, t + KF * h)
                    project(0, t * 4 + base, 0, UNIT, h_hi, h_lo)
                    pe.wait_ge(f_made, t + KF * h)
                    project(1, t * 4 + (base + 2), 2, UNIT, h_hi, h_lo)

            pe.wait_ge(zeroed, 7)
            stat_sum(0)
            for h in range(HALVES):
                recurrent(h)
                kvq(h)
                pe.wait_ge(par_loaded, 32)
                attention(h)
                attn_branch(h)
                out_tiles(BASE[h]["o"], UNIT, mg_hi, mg_lo, (gb_made, KD * (h + 1)),
                          (attn_part, KD * (h + 1)), (mg_lo_made, KD * h, 2 + 2 * h))
            for h in range(HALVES):
                ffn_up(h)
                if h == 0:
                    stat_sum(5)
                out_tiles(BASE[h]["d"], DOWN, f_hi, f_lo, (silu_made, KF * (h + 1)),
                          (f_made, KF * (h + 1)), (f_lo_made, KF * h, 6 + h))
            stat_sum(7)

        @block.scalar
        def _(act):
            fn = nc.scalar.activation

            def load_xs(s, t, src):
                act.dma_start(xs[:, t % 2, :], src[t]).then_inc(xs_loaded[t % 2], 16)

            def deviation(n):
                act.wait_ge(stat_mm, n + 1)
                fn(rstd_of(n)[:], ps[:, BK_STAT, :], ACT.Sqrt, bias=eps_ap, scale=1.0 / D)\
                    .then_inc(dev_made, 1)

            def square(n, t, src):
                wait_pos(act, summed, n * 9 + t + 1)
                fn(sq[:], src, ACT.Square).then_inc(squared, 1)

            def norm_hi(k, t):
                act.wait_ge(normed, KD * k + t + 1)
                fn(h_hi[:, t, :], tmp[:, t % 2, :], ACT.Copy).then_inc(h_hi_made, 1)

            def conv_in(h, j, done, q):
                J = j + KR * h
                act.wait_ge(blocks_done, done)
                wait_pos(act, taps, J * 3)
                own_wait(act)
                fn(u_raw[:, 0:TAPS - 1], u_carry[:, bass.ds(j, 1), :], ACT.Copy).then_inc(u_ctx, 1)
                fn(u_raw[:, TAPS - 1:], ps[:, 0, :], ACT.Copy).then_inc(u_copied, 1)
                act.wait_ge(u_ctx, J + 1)
                own_wait(act)
                fn(u_carry[:, bass.ds(j, 1), :], ps[:, 0, T - TAPS + 1:T], ACT.Copy)\
                    .then_inc(u_copied, 1)
                act.wait_ge(u_copied, J * 2 + 1)
                own_wait(act)
                fn(uc[:, q, :], u_raw[:, 0:T], ACT.Identity, bias=col("conv_b", j),
                   scale=col("conv_w", j)).then_inc(tap0, 1)

            def conv_hi(h, j, q):
                act.wait_ge(taps, (j + KR * h) * 3 + 3)
                fn(uc_hi[:, q, :], uc[:, q, :], ACT.Copy).then_inc(uc_hi_made, 1)

            def gate_fns(h, j, n):
                J = j + KR * h
                act.wait_ge(blocks_done, n + 2)
                own_wait(act)
                fn(g_r[:], ps[:, 4, :], ACT.Tanh, bias=half_col("b_rg", j), scale=0.5)\
                    .then_inc(r_made, 1)
                fn(g_i[:], ps[:, 5, :], ACT.Tanh, bias=half_col("b_ig", j), scale=0.5)\
                    .then_inc(i_made, 1)
                act.wait_ge(r_made, J + 1)
                own_wait(act)
                fn(g_r[:], g_r[:], ACT.Tanh, bias=sp2[:, bass.ds(j, 1)],
                   scale=sp2[:, bass.ds(j, 1)]).then_inc(th_made, 1)
                act.wait_ge(th_made, J + 1)
                fn(g_a[:], g_r[:], ACT.Identity, bias=one_ap).then_inc(th1_made, 1)

            def gate_root(h, j):
                J = j + KR * h
                act.wait_ge(th1_made, J + 1)
                fn(g_r[:], g_r[:], ACT.Sqrt).then_inc(root_made, 1)

            def gelu(h, j, done, q):
                J = j + KR * h
                act.wait_ge(blocks_done, done)
                fn(gy[:, q, :], ps[:, 2, :], ACT.Gelu_apprx_tanh).then_inc(gelu_made, 1)

            def decay(h, j):
                act.wait_ge(amp_made, j + KR * h + 1)
                fn(g_a[:], g_a[:], ACT.Identity, bias=neg_ap, scale=2.0).then_inc(a_made, 1)

            def lru_out_hi(h, j):
                act.wait_ge(lru_made, j + KR * h + 1)
                own_wait(act)
                fn(lru_hi[:, bass.ds(j, 1), :], g_h[:], ACT.Copy).then_inc(lru_hi_made, 1)

            def recurrent(h):
                for j in range(2):
                    done = BASE[h]["head"] + 4 * j
                    conv_in(h, j, done + 3, j)
                    conv_hi(h, j, j)
                    gelu(h, j, done + 4, j)
                if h:
                    deviation(2)
                else:
                    lam = par[:, PARAMS["lam"]:PARAMS["lam"] + KR]
                    fn(sp[:, 0, :], lam, ACT.Abs).then_inc(prep_act, 1)
                    act.wait_ge(prep_act, 1)
                    fn(sp[:, 1, :], sp[:, 0, :], ACT.Exp, scale=-1.0).then_inc(prep_act, 1)
                    act.wait_ge(prep_dve, PREP_STEPS)
                with act.Fori(0, 2) as it:
                    for q in range(4):
                        j = it * 4 + (2 + q)
                        n = (it * 4 + q) * 6 + BASE[h]["step"]
                        conv_in(h, j, n + 2, (2 + q) % 4)
                        gate_fns(h, j - 2, n + 2)
                        conv_hi(h, j, (2 + q) % 4)
                        gate_root(h, j - 2)
                        gelu(h, j, n + 6, (2 + q) % 4)
                        decay(h, j - 2)
                        lru_out_hi(h, j - 2)

            def kvq(h):
                n, n_q = BASE[h]["tail"], BASE[h]["q"]
                if h:
                    act.wait_ge(pv_done, NCH)
                    fn(k_hi[:, :, 0:CH], rd(k_hi[:, :, T:T + CH]), ACT.Copy).then_inc(kept_hi, 1)
                    fn(v_hi[0:CH, 0, :], rd(v_hi[0:CH, NCH, :]), ACT.Copy).then_inc(kept_hi, 1)
                    act.wait_ge(kept_hi, 2)
                else:
                    act.wait_ge(zeroed, 7)
                for p in range(PAIRS):
                    act.wait_ge(blocks_done, n + 4 * p + 2)
                    fn(k_hi[:, p, CH:CH + T], ps[:, BK_K[p], :], ACT.Copy).then_inc(k_hi_made, 1)
                    gate_fns(h, 8 + p, n + 4 * p + 2)
                    gate_root(h, 8 + p)
                    decay(h, 8 + p)
                    lru_out_hi(h, 8 + p)
                act.wait_ge(blocks_done, BASE[h]["v"] + 4)
                fn(v_whole(v_hi), v_out, ACT.Copy).then_inc(v_hi_made, 1)
                act.wait_ge(v_hi_made, 3 * h + 1)
                fn(v_hi[CH:P, 0:NCH:2, :], rd(v_hi[0:CH, 1:NCH + 1:2, :]), ACT.Copy)\
                    .then_inc(v_hi_made, 1)
                fn(v_hi[0:CH, 2:NCH + 1:2, :], rd(v_hi[CH:P, 1:NCH + 1:2, :]), ACT.Copy)\
                    .then_inc(v_hi_made, 1)
                act.wait_ge(lru_lo_made, KR * (h + 1))
                with act.Fori(0, KD // 2) as it:
                    if h == 0:
                        act.wait_ge(squared, it * 2 + KD)
                    load_pair(x_d[1 - h], it)
                    for q in range(2):
                        t = it * 2 + q
                        act.wait_ge(blocks_done, t * 2 + (n_q + 2))
                        own_wait(act)
                        fn(q_tile(q_hi, it, q), ps[:, q, :].rearrange("p (c t) -> p c t", t=CH),
                           ACT.Copy).then_inc(q_hi_made, 1)
                        if h:
                            x1_out(0, t)
                        else:
                            act.wait_ge(xs_loaded[q], it * 16 + 16)
                            square(1, t, xs[:, q, :])
                if h == 0:
                    act.wait_ge(squared, 2 * KD)

            def attention(h):
                def exps(C):
                    act.wait_ge(maxed, C * 4 + 4)
                    for i in range(8):
                        fn(prob[:, i, :], prob[:, i, :], ACT.Exp, bias=stat[:, 2, i:i + 1],
                           accum_out=stat[:, 3, i:i + 1]).then_inc(exped, 1)
                    fn(stat[:, 4, :], stat[:, 1, :], ACT.Exp).then_inc(exped, 1)

                def gate(c, C):
                    act.wait_ge(blocks_done, c * 8 + (BASE[h]["a"] + 4))
                    wait_pos(act, lru_part, C)
                    own_wait(act)
                    fn(tmp[:, 0, :], ps[:, 0, :], ACT.Tanh, bias=half_col("b_gate_lru", c),
                       scale=0.5).then_inc(ga_made, 1)

                def out_hi(c, C):
                    act.wait_ge(pv_done, C + 1)
                    own_wait(act)
                    for half in range(2):
                        r = slice(64 * half, 64 * half + 64)
                        fn(q_hi[r, :, bass.ds(c * P, P)],
                           ps[r, BK_PV + half, :].rearrange("p (t q) -> p t q", q=P),
                           ACT.Copy).then_inc(ao_hi_made, 1)

                def turned_hi(C):
                    act.wait_ge(pt_done, C + 1)
                    fn(pt_hi[:, :, :], ps[:, BK_PT:BK_PT + 2, :].rearrange("p b (i k) -> p (b i) k", i=4),
                       ACT.Copy).then_inc(pt_hi_made, 1)

                def chunk(c, C):
                    exps(C)
                    gate(c, C)
                    if not isinstance(c, int):
                        out_hi(c - 1, C - 1)
                    turned_hi(C)

                chunk(0, NCH * h)
                if h == 0:
                    act.wait_ge(biased, 1)
                    act.dma_start(alibi[:], alibi_d[1]).then_inc(alibi_loaded, 16)
                with act.Fori(1, NCH) as c:
                    chunk(c, c + NCH * h)
                out_hi(NCH - 1, NCH * (h + 1) - 1)

            def attn_branch(h):
                def tile(c, C):
                    act.wait_ge(blocks_done, c * 4 + (BASE[h]["b"] + 2))
                    wait_pos(act, attn_part, C) if not isinstance(c, int) else \
                        act.wait_ge(lru_part, NCH * (h + 1))
                    own_wait(act)
                    fn(tmp[:, 0, :], ps[:, 0, :], ACT.Tanh, bias=half_col("b_gate_attn", c),
                       scale=0.5).then_inc(gb_made, 1)
                    act.wait_ge(merged, C + 1)
                    own_wait(act)
                    fn(mg_hi[:, bass.ds(c, 1), :], tmp[:, 1, :], ACT.Copy, scale=0.5)\
                        .then_inc(mg_hi_made, 1)

                tile(0, KD * h)
                deviation(1 + 2 * h)
                with act.Fori(1, KD) as c:
                    tile(c, c + KD * h)

            def row_tile(n, t, done):
                act.wait_ge(blocks_done, done)
                own_wait(act)
                bank = ps[:, bass.ds(t, 1), :]
                if n == 7:
                    fn(rows[:, bass.ds(t, 1), :], bank, ACT.Copy, scale=col("g_post_ffn", t))\
                        .then_inc(row_out, 1)
                else:
                    fn(rows[:, bass.ds(t, 1), :], bank, ACT.Copy).then_inc(row_out, 1)
                act.wait_ge(summed, t + (9 * n + 1))
                own_wait(act)
                fn(sq[:], bank, ACT.Square).then_inc(row_out, 1)

            def rows_out(n, base, size, between):
                for t in range(2):
                    row_tile(n, t, base + size * (t + 1))
                between()
                with act.Fori(2, KD) as t:
                    row_tile(n, t, t * size + (base + size))

            def normed_stream(k, s, src):
                for t in range(2):
                    load_xs(s, t, src)
                for t in range(KD):
                    norm_hi(k, t)
                    if t + 2 < KD:
                        load_xs(s, t + 2, src)

            def load_pair(src, it):
                own_wait(act)
                for q in range(2):
                    act.dma_start(xs[:, q, :], src[bass.ds(it * 2 + q, 1), :, :]
                                  .rearrange("o p t -> (o p) t")).then_inc(xs_loaded[q], 16)

            def x1_out(h, t):
                act.wait_ge(added, t + (KD * h + 1))
                own_wait(act)
                act.dma_start(x1_d[h][bass.ds(t, 1), :, :].rearrange("o p t -> (o p) t"),
                              rows[:, bass.ds(t, 1), :].rearrange("p o t -> p (o t)"))\
                    .then_inc(x1_stored, 16)
                act.wait_ge(summed, t + (9 * (3 + 2 * h) + 1))
                own_wait(act)
                fn(sq[:], rows[:, bass.ds(t, 1), :], ACT.Square).then_inc(squared, 1)

            for t in range(1, KD, 2):
                act.dma_start(rows[:, t, :], x_d[0][t]).then_inc(x0_loaded[t], 16)
            act.dma_start(par[:], par_d).then_inc(par_loaded, 16)
            act.dma_start(eye[:], eye_d).then_inc(par_loaded, 16)
            act.dma_start(alibi[:], alibi_d[0]).then_inc(alibi_loaded, 16)
            act.wait_ge(zeroed, 7)
            one_ap, neg_ap, eps_ap = 1.0, -1.0, EPS

            for t in range(KD):
                act.wait_ge(x0_loaded[t], 16)
                if t >= 2:
                    act.wait_ge(summed, t)
                fn(tmp[:, t % 2, :], rows[:, t, :], ACT.Square).then_inc(squared, 1)
            deviation(0)
            for t in range(KD):
                norm_hi(0, t)

            for h in range(HALVES):
                recurrent(h)
                kvq(h)
                attention(h)
                attn_branch(h)
                n, o = 2 + 2 * h, BASE[h]["o"]
                if h == 0:
                    rows_out(n, o, 2, lambda: normed_stream(1, 1, x_d[1]))
                else:
                    act.wait_ge(x1_stored, 16 * KD)
                    rows_out(n, o, 2, lambda: normed_stream(2, 3, x1_d[0]))
            for h in range(HALVES):
                def tile(t, F):
                    act.wait_ge(blocks_done, t * 4 + (BASE[h]["f"] + 2))
                    if isinstance(t, int) and t == 0:
                        act.wait_ge(h_lo_made, KD * (3 + h))
                    else:
                        act.wait_ge(f_made, F)
                    fn(tmp[:, 0, :], ps[:, 0, :], ACT.Silu).then_inc(silu_made, 1)
                    act.wait_ge(f_made, F + 1)
                    own_wait(act)
                    fn(f_hi[:, bass.ds(t, 1), :], tmp[:, 1, :], ACT.Copy).then_inc(f_hi_made, 1)

                for t in range(2):
                    tile(t, KF * h + t)
                deviation(4 + 2 * h)
                with act.Fori(0, KD // 2) as it:
                    load_pair(x1_d[0] if h else x_d[1], it)
                    for q in range(2):
                        t = it * 2 + (2 + q)
                        tile(t, t + KF * h)
                        c = it * 2 + q
                        if h == 0:
                            x1_out(1, c)
                        else:
                            act.wait_ge(added, c + (2 * KD + 1))
                            own_wait(act)
                            act.dma_start(out_d[0][bass.ds(c, 1), :, :].rearrange("o p t -> (o p) t"),
                                          rows[:, bass.ds(c, 1), :].rearrange("p o t -> p (o t)"))\
                                .then_inc(out_stored, 16)
                with act.Fori(KD + 2, KF) as t:
                    tile(t, t + KF * h)
                if h == 0:
                    deviation(5)
                    act.wait_ge(x1_stored, 2 * 16 * KD)
                    act.wait_ge(f_lo_made, KF)
                    act.wait_ge(blocks_done, BASE[0]["d"])
                    normed_stream(3, 5, x1_d[1])
                else:
                    act.wait_ge(out_stored, 16 * KD)
                    act.wait_ge(blocks_done, BASE[1]["d"])
                    for t in range(KD):
                        act.dma_start(x1_all[:, t, :], x1_d[1][t]).then_inc(x1_all_loaded, 16)
                rows_out(6 + h, BASE[h]["d"], len(DOWN), lambda: None)

            deviation(7)
            for t in range(KD):
                if t < DVE_LAST:
                    act.wait_ge(added, 3 * KD + t + 1)
                else:
                    act.wait_ge(pool_added, t - DVE_LAST + 1)
                act.dma_start(out_d[1][t], rows[:, t, :]).then_inc(out_stored, 16)
            act.wait_ge(out_stored, HALVES * 16 * KD)

        @block.vector
        def _(dve):
            tt, ts, stt = nc.vector.tensor_tensor, nc.vector.tensor_scalar, nc.vector.scalar_tensor_tensor

            def open_sum(n):
                wait_pos(dve, stat_mm, n)
                wait_pos(dve, summed, 9 * n)
                nc.vector.memset(acc[:], 0.0).then_inc(summed, 1)

            def add_square(n, t, sem_value):
                dve.wait_ge(*sem_value)
                dve.wait_ge(summed, t + (9 * n + 1))
                tt(acc[:], acc[:], sq[:], ALU.add).then_inc(summed, 1)

            def invert(n):
                dve.wait_ge(dev_made, n + 1)
                nc.vector.reciprocal(rstd_of(n)[:], rstd_of(n)[:]).then_inc(rstd_made, 1)

            def normalise(k, gain, rstd, src, loaded):
                for t in range(KD):
                    dve.wait_ge(*loaded(t))
                    if t >= 2:
                        dve.wait_ge(h_lo_made, KD * k + t - 1)
                    stt(tmp[:, t % 2, :], src(t), col(gain, t), rstd[:], ALU.mult, ALU.mult)\
                        .then_inc(normed, 1)
                    if t >= 1:
                        norm_lo(k, t - 1)
                norm_lo(k, KD - 1)

            def norm_lo(k, t):
                dve.wait_ge(normed, KD * k + t + 1)
                dve.wait_ge(h_hi_made, KD * k + t + 1)
                tt(h_lo[:, t, :], tmp[:, t % 2, :], rd(h_hi[:, t, :]), ALU.subtract)\
                    .then_inc(h_lo_made, 1)

            def xs_at(s):
                return lambda t: (xs_loaded[t % 2], 16 * (4 * s + t // 2 + 1))

            def conv(h, j, q):
                J = j + KR * h
                dve.wait_ge(tap0, J + 1)
                for k in range(1, TAPS):
                    if k > 1:
                        dve.wait_ge(taps, J * 3 + (k - 1))
                    stt(uc[:, q, :], u_raw[:, k:k + T], col("conv_w", j + KR * k), uc[:, q, :],
                        ALU.mult, ALU.add).then_inc(taps, 1)

            def conv_lo(h, j, q):
                J = j + KR * h
                dve.wait_ge(uc_hi_made, J + 1)
                tt(uc_lo[:, q, :], uc[:, q, :], rd(uc_hi[:, q, :]), ALU.subtract)\
                    .then_inc(uc_lo_made, 1)

            def recurrence(h, j, q):
                J = j + KR * h
                dve.wait_ge(i_made, J + 1)
                stt(g_i[:], g_i[:], 1.0, uc[:, q, :], ALU.add, ALU.mult).then_inc(iu_made, 1)
                dve.wait_ge(th1_made, J + 1)
                nc.vector.reciprocal(g_a[:], g_a[:]).then_inc(recip_made, 1)
                dve.wait_ge(root_made, J + 1)
                dve.wait_ge(recip_made, J + 1)
                tt(g_r[:], g_r[:], g_a[:], ALU.mult).then_inc(amp_made, 1)
                dve.wait_ge(amp_made, J + 1)
                dve.wait_ge(iu_made, J + 1)
                tt(g_i[:], g_i[:], g_r[:], ALU.mult).then_inc(b_made, 1)
                dve.wait_ge(b_made, J + 1)
                dve.wait_ge(a_made, J + 1)
                nc.vector.tensor_tensor_scan(g_h[:], g_a[:], g_i[:], h_carry[:, bass.ds(j, 1)],
                                             ALU.mult, ALU.add).then_inc(scanned, 1)
                dve.wait_ge(scanned, J + 1)
                own_wait(dve)
                nc.vector.tensor_copy(h_carry[:, bass.ds(j, 1)], g_h[:, T - 1:T]).then_inc(h_kept, 1)
                dve.wait_ge(gelu_made, J + 1)
                dve.wait_ge(h_kept, J + 1)
                tt(g_h[:], g_h[:], gy[:, q, :], ALU.mult).then_inc(lru_made, 1)
                dve.wait_ge(lru_hi_made, J + 1)
                dve.wait_ge(lru_made, J + 1)
                tt(lru_lo[:, bass.ds(j, 1), :], g_h[:], rd(lru_hi[:, bass.ds(j, 1), :]), ALU.subtract)\
                    .then_inc(lru_lo_made, 1)

            def recurrent(h):
                dve.wait_ge(tap0, KR * h + 1)
                nc.vector.memset(rd(uc_hi[:, 3, :]), 0.0).then_inc(pad_zeroed, 1)
                nc.vector.memset(rd(uc_lo[:, 3, :]), 0.0).then_inc(pad_zeroed, 1)
                for j in range(2):
                    conv(h, j, j)
                    conv_lo(h, j, j)
                if h:
                    invert(2)
                    dve.wait_ge(rstd_made, 3)
                else:
                    prepare()
                dve.wait_ge(pad_zeroed, 2 * (h + 1))
                with dve.Fori(0, 2) as it:
                    for q in range(4):
                        j = it * 4 + (2 + q)
                        conv(h, j, (2 + q) % 4)
                        conv_lo(h, j, (2 + q) % 4)
                        recurrence(h, j - 2, q)

            def kvq(h):
                if h:
                    dve.wait_ge(pv_done, NCH)
                    nc.vector.tensor_copy(k_lo[:, :, 0:CH], rd(k_lo[:, :, T:T + CH])).then_inc(kept_lo, 1)
                    nc.vector.tensor_copy(v_lo[0:CH, 0, :], rd(v_lo[0:CH, NCH, :])).then_inc(kept_lo, 1)
                    dve.wait_ge(kept_lo, 2)
                else:
                    dve.wait_ge(zeroed, 7)
                for p in range(PAIRS):
                    dve.wait_ge(k_hi_made, PAIRS * h + p + 1)
                    tt(k_lo[:, p, CH:CH + T], ps[:, BK_K[p], :], rd(k_hi[:, p, CH:CH + T]),
                       ALU.subtract).then_inc(k_lo_made, 1)
                    recurrence(h, 8 + p, p)
                dve.wait_ge(v_hi_made, 3 * h + 1)
                tt(v_whole(v_lo), v_out, rd(v_whole(v_hi)), ALU.subtract).then_inc(v_lo_made, 1)
                dve.wait_ge(v_lo_made, 3 * h + 1)
                nc.vector.tensor_copy(v_lo[CH:P, 0:NCH:2, :], rd(v_lo[0:CH, 1:NCH + 1:2, :]))\
                    .then_inc(v_lo_made, 1)
                nc.vector.tensor_copy(v_lo[0:CH, 2:NCH + 1:2, :], rd(v_lo[CH:P, 1:NCH + 1:2, :]))\
                    .then_inc(v_lo_made, 1)
                open_sum(1 + 2 * h)
                with dve.Fori(0, KD // 2) as it:
                    for q in range(2):
                        t = it * 2 + q
                        dve.wait_ge(q_hi_made, t + (KD * h + 1))
                        tt(q_tile(q_lo, it, q), ps[:, q, :].rearrange("p (c t) -> p c t", t=CH),
                           rd(q_tile(q_hi, it, q)), ALU.subtract).then_inc(q_lo_made, 1)
                        if h:
                            add_norm(2, "g_post_mix", 0, 2, it, q)
                        add_square(1 + 2 * h, t, (squared, t + (sq_base(1 + 2 * h) + 1)))

            def attention(h):
                sink = par[:, PARAMS["sink"]:PARAMS["sink"] + 8]
                S = ps[:, BK_S:BK_S + 2, :].rearrange("p b (i k) -> p (b i) k", i=4)
                PT = ps[:, BK_PT:BK_PT + 2, :].rearrange("p b (i k) -> p (b i) k", i=4)

                def softmax_in(C):
                    dve.wait_ge(qk_done, C + 1)
                    wait_pos(dve, pt_done, C)
                    stt(prob[:], S, HD ** -0.5, alibi[:], ALU.mult, ALU.add).then_inc(biased, 1)
                    dve.wait_ge(biased, C + 1)
                    nc.vector.tensor_reduce(stat[:, 0, :], prob[:], AX_X, ALU.max).then_inc(maxed, 1)
                    dve.wait_ge(maxed, C * 4 + 1)
                    tt(stat[:, 0, :], stat[:, 0, :], sink, ALU.max).then_inc(maxed, 1)
                    dve.wait_ge(maxed, C * 4 + 2)
                    tt(stat[:, 1, :], sink, stat[:, 0, :], ALU.subtract).then_inc(maxed, 1)
                    ts(stat[:, 2, :], stat[:, 0, :], -1.0, None, ALU.mult).then_inc(maxed, 1)

                def softmax_out(C):
                    dve.wait_ge(exped, C * 9 + 9)
                    tt(stat[:, 3, :], stat[:, 3, :], stat[:, 4, :], ALU.add).then_inc(probed, 1)
                    dve.wait_ge(probed, C * 3 + 1)
                    nc.vector.reciprocal(stat[:, 5, :], stat[:, 3, :]).then_inc(probed, 1)
                    dve.wait_ge(probed, C * 3 + 2)
                    tt(prob[:], prob[:], stat[:, 5, :].rearrange("p (i o) -> p i o", o=1)
                       .broadcast_to([P, 8, 2 * CH]), ALU.mult).then_inc(probed, 1)

                def out_lo(c, C):
                    for half in range(2):
                        r = slice(64 * half, 64 * half + 64)
                        dve.wait_ge(ao_hi_made, C * 2 + (half + 1))
                        q = (r, slice(None), bass.ds(c * P, P))
                        tt(q_lo[q], ps[r, BK_PV + half, :].rearrange("p (t q) -> p t q", q=P),
                           rd(q_hi[q]), ALU.subtract).then_inc(ao_lo_made, 1)

                def chunk(c, C):
                    softmax_in(C)
                    softmax_out(C)
                    if not isinstance(c, int):
                        out_lo(c - 1, C - 1)
                    dve.wait_ge(ga_made, C + 1)
                    dve.wait_ge(blocks_done, c * 8 + (BASE[h]["a"] + 8))
                    stt(rows[:, bass.ds(c, 1), :], tmp[:, 0, :], 1.0, ps[:, 1, :], ALU.add, ALU.mult)\
                        .then_inc(lru_part, 1)
                    dve.wait_ge(pt_hi_made, C + 1)
                    tt(pt_lo[:], PT, rd(pt_hi[:]), ALU.subtract).then_inc(pt_lo_made, 1)

                dve.wait_ge(alibi_loaded, 16)
                if h:
                    dve.wait_ge(x1_stored, 16 * KD)
                chunk(0, NCH * h)
                dve.wait_ge(alibi_loaded, 32)
                with dve.Fori(1, NCH) as c:
                    chunk(c, c + NCH * h)
                out_lo(NCH - 1, NCH * (h + 1) - 1)

            def attn_branch(h):
                def tile(c, C):
                    dve.wait_ge(gb_made, C + 1)
                    dve.wait_ge(blocks_done, c * 4 + (BASE[h]["b"] + 4))
                    stt(tmp[:, 1, :], tmp[:, 0, :], 1.0, ps[:, 1, :], ALU.add, ALU.mult)\
                        .then_inc(attn_part, 1)
                    dve.wait_ge(attn_part, C + 1)
                    tt(tmp[:, 1, :], tmp[:, 1, :], rows[:, bass.ds(c, 1), :], ALU.add).then_inc(merged, 1)
                    dve.wait_ge(mg_hi_made, C + 1)
                    stt(mg_lo[:, bass.ds(c, 1), :], tmp[:, 1, :], 0.5, rd(mg_hi[:, bass.ds(c, 1), :]),
                        ALU.mult, ALU.subtract).then_inc(mg_lo_made, 1)

                tile(0, KD * h)
                invert(1 + 2 * h)
                with dve.Fori(1, KD) as c:
                    dve.wait_ge(mg_lo_made, c + KD * h)
                    tile(c, c + KD * h)

            def rows_in(n, r0, between):
                open_sum(n)
                for t in range(2):
                    add_square(n, t, (row_out, 2 * (r0 + t + 1)))
                between()
                with dve.Fori(2, KD) as t:
                    add_square(n, t, (row_out, t * 2 + 2 * (r0 + 1)))

            def add_norm(n, gain, a0, s, it, q):
                c = it * 2 + q
                stt(rows[:, bass.ds(c, 1), :], rows[:, bass.ds(c, 1), :], col(gain, c), rstd_of(n)[:],
                    ALU.mult, ALU.mult).then_inc(scaled, 1)
                dve.wait_ge(scaled, c + (a0 + 1))
                dve.wait_ge(xs_loaded[q], it * 16 + (64 * s + 16))
                tt(rows[:, bass.ds(c, 1), :], rows[:, bass.ds(c, 1), :], xs[:, q, :], ALU.add)\
                    .then_inc(added, 1)

            def sq_base(n):
                return KD * {0: 0, 1: 1, 3: 2, 5: 3}[n]

            def prepare():
                dve.wait_ge(par_loaded, 32)
                done = [0]

                def step(ins):
                    done[0] += 1
                    ins.then_inc(prep_dve, 1)
                    dve.wait_ge(prep_dve, done[0])

                step(ts(half_b[:], par[:, HALVED:N_PARAMS], 0.5, None, ALU.mult))
                dve.wait_ge(prep_act, 2)
                e, s, s2, poly = sp[:, 1, :], sp[:, 0, :], sp[:, 2, :], sp[:, 3, :]
                step(ts(s, e, 2.0, None, ALU.add))
                step(nc.vector.reciprocal(s2, s))
                step(tt(s, e, s2, ALU.mult))
                step(tt(s2, s, s, ALU.mult))
                step(ts(poly, s2, 1.0 / 17, None, ALU.mult))
                for m in (15, 13, 11, 9, 7, 5, 3):
                    step(stt(poly, poly, 1.0 / m, s2, ALU.add, ALU.mult))
                step(stt(poly, poly, 1.0, s, ALU.add, ALU.mult))
                step(ts(s2, par[:, PARAMS["lam"]:PARAMS["lam"] + KR], -2.0, 0.0, ALU.mult, ALU.max))
                step(stt(sp2[:], poly, 4.0, s2, ALU.mult, ALU.add))
                assert done[0] == PREP_STEPS

            open_sum(0)
            for t in range(KD):
                dve.wait_ge(squared, t + 1)
                dve.wait_ge(summed, t + 1)
                tt(acc[:], acc[:], tmp[:, t % 2, :], ALU.add).then_inc(summed, 1)
            invert(0)
            dve.wait_ge(rstd_made, 1)
            dve.wait_ge(par_loaded, 32)
            normalise(0, "g_pre_mix", rstd_a, lambda t: rows[:, t, :], lambda t: (x0_loaded[t], 16))

            for h in range(HALVES):
                recurrent(h)
                kvq(h)
                attention(h)
                attn_branch(h)
                dve.wait_ge(mg_lo_made, KD * (h + 1))
                if h == 0:
                    rows_in(2, 0, lambda: normalise(1, "g_pre_mix", rstd_b,
                                                    lambda t: xs[:, t % 2, :], xs_at(1)))
                else:
                    rows_in(4, KD, lambda: normalise(2, "g_pre_ffn", rstd_b,
                                                     lambda t: xs[:, t % 2, :], xs_at(3)))
            for h in range(HALVES):
                def tile(t, F):
                    dve.wait_ge(silu_made, F + 1)
                    dve.wait_ge(blocks_done, t * 4 + (BASE[h]["f"] + 4))
                    if not isinstance(F, int) or F:
                        dve.wait_ge(f_lo_made, F)
                    tt(tmp[:, 1, :], ps[:, 1, :], tmp[:, 0, :], ALU.mult).then_inc(f_made, 1)
                    dve.wait_ge(f_hi_made, F + 1)
                    dve.wait_ge(f_made, F + 1)
                    tt(f_lo[:, bass.ds(t, 1), :], tmp[:, 1, :], rd(f_hi[:, bass.ds(t, 1), :]),
                       ALU.subtract).then_inc(f_lo_made, 1)

                for t in range(2):
                    tile(t, KF * h + t)
                invert(4 + 2 * h)
                if h == 0:
                    open_sum(5)
                dve.wait_ge(rstd_made, 5 + 2 * h)
                with dve.Fori(0, KD // 2) as it:
                    for q in range(2):
                        t, c = it * 2 + (2 + q), it * 2 + q
                        tile(t, t + KF * h)
                        if h == 0:
                            add_norm(4, "g_post_mix", KD, 4, it, q)
                            add_square(5, c, (squared, c + (sq_base(5) + 1)))
                        else:
                            add_norm(6, "g_post_ffn", 2 * KD, 6, it, q)
                with dve.Fori(KD + 2, KF) as t:
                    tile(t, t + KF * h)
                if h == 0:
                    dve.wait_ge(f_lo_made, KF)
                    invert(5)
                    dve.wait_ge(rstd_made, 6)
                    normalise(3, "g_pre_ffn", rstd_b, lambda t: xs[:, t % 2, :], xs_at(5))
                rows_in(6 + h, 16 + KD * h, lambda: None)
            invert(7)
            dve.wait_ge(rstd_made, 8)
            for t in range(DVE_LAST):
                tt(rows[:, t, :], rows[:, t, :], rstd_a[:], ALU.mult).then_inc(scaled, 1)
                dve.wait_ge(x1_all_loaded, 16 * KD)
                dve.wait_ge(scaled, 3 * KD + t + 1)
                tt(rows[:, t, :], rows[:, t, :], x1_all[:, t, :], ALU.add).then_inc(added, 1)


def k_tiles(w):
    return w.reshape(-1, P, w.shape[1]).transpose(1, 0, 2)


def cols(w, c):
    return k_tiles(w[:, c * P:(c + 1) * P]).reshape(P, -1)


def weight_streams(w_in, w_rg, w_ig, w_lru_br, w_attn_br, w_out, w_gate, w_up, w_down):
    bounds = np.cumsum([0, D_RNN, D_RNN, HEADS * HD, D_KV, D_KV, D, D])
    u, y, q, k, v, gl, ga = [w_in[:, bounds[i]:bounds[i + 1]] for i in range(7)]
    order = [(2 * p + half) * GRP + a for p in range(PAIRS) for a in range(GRP) for half in range(2)]
    q = q.reshape(D, HEADS, HD)[:, order].reshape(D, -1)
    w_attn_br = w_attn_br.reshape(HEADS, HD, D)[order].reshape(-1, D)

    def gate(w, j, last=False):
        full = np.zeros((D_RNN + 2 * P, D_RNN), w.dtype)
        for b in range(N_BLK):
            full[P + b * BLK:P + (b + 1) * BLK, b * BLK:(b + 1) * BLK] = w[b]
        part = full[j * P:(j + (2 if last else 3)) * P, j * P:(j + 1) * P]
        return k_tiles(part).reshape(P, -1)

    def cat(*parts):
        return np.concatenate(parts, axis=1)

    return {
        "head": np.stack([cat(*[cols(m, j)[:, b * CAP:(b + 1) * CAP] for b in range(2) for m in (u, y)])
                          for j in range(2)]),
        "step": np.stack([cat(*[x for jj in (j, j + 1)
                                for x in (cols(u, jj), gate(w_rg, jj - 2), gate(w_ig, jj - 2), cols(y, jj))])
                          for j in range(2, KR, 2)]),
        "tail": cat(cols(k, 0), gate(w_rg, 8), gate(w_ig, 8),
                    cols(k, 1), gate(w_rg, 9, True), gate(w_ig, 9, True))[None],
        "v": k_tiles(v).reshape(P, -1)[None],
        "q": np.stack([cat(cols(q, t), cols(q, t + 1)) for t in range(0, KD, 2)]),
        "a": np.stack([cat(cols(gl, c), cols(w_lru_br, c)) for c in range(KD)]),
        "b": np.stack([cat(cols(ga, c), cols(w_attn_br, c)) for c in range(KD)]),
        "o": np.stack([cat(cols(w_out, t), cols(w_out, t + 1)) for t in range(0, KD, 2)]),
        "f": np.stack([cat(cols(w_gate, t), cols(w_up, t)) for t in range(KF)]),
        "d": np.stack([cat(cols(w_down, t), cols(w_down, t + 1)) for t in range(0, KD, 2)]),
    }


def by_tile(v):
    return v.reshape(-1, P).T


def score_heads():
    p = np.arange(P)[:, None]
    i = np.arange(8)[None, :]
    half, pair, b = i // 4, i // 2 % 2, i % 2
    return (2 * pair + half) * GRP + 2 * b + p // CH


def alibi_tables():
    slope = np.exp2(-8.0 * (np.arange(HEADS, dtype=np.float32) + 1) / HEADS).astype(np.float32)
    qi = np.arange(P)[:, None] % CH
    dist = np.abs(qi + CH - np.arange(2 * CH)[None, :]).astype(np.float32)
    table = -slope[score_heads()][:, :, None] * dist[:, None, :]
    masked = table.copy()
    masked[:, :, :CH] = MASKED
    return np.stack([masked, table]).astype(np.float32)


def kernel(**inputs):
    import concourse.bacc as bacc
    from concourse.bass_utils import run_bass_kernel_spmd as run

    a = {k: np.asarray(v) for k, v in inputs.items()}
    one = {k: v[0] for k, v in a.items()}
    table = [by_tile(one["norm_pre_mix"]), by_tile(one["norm_post_mix"]),
             by_tile(one["norm_pre_ffn"]), by_tile(one["norm_post_ffn"]),
             np.concatenate([by_tile(one["conv_w"][k]) for k in range(TAPS)], axis=1),
             by_tile(one["conv_b"]), by_tile(one["lru_lambda"]), one["attn_sinks"][score_heads()],
             by_tile(one["b_rg"]), by_tile(one["b_ig"]),
             by_tile(one["b_gate"][:D]), by_tile(one["b_gate"][D:])]
    arrays = {
        "x_t": one["x"].T.reshape(KD, P, HALVES, T).transpose(2, 0, 1, 3),
        "params": np.concatenate(table, axis=1),
        "alibi_in": alibi_tables(),
        "eye_in": np.eye(P, dtype=np.float32),
    }
    streams = weight_streams(one["w_in"], one["w_rg"], one["w_ig"], one["w_lru_br"],
                             one["w_attn_br"], one["w_out"], one["w_ffn_gate"], one["w_ffn_up"],
                             one["w_ffn_down"])
    arrays.update({f"w_{name}": w for name, w in streams.items()})
    arrays = {k: np.ascontiguousarray(v) for k, v in arrays.items()}

    nc = bacc.Bacc("TRN2", target_bir_lowering=False, num_devices=1)
    dram = {k: nc.dram_tensor(k, v.shape, F32, kind="ExternalInput").ap() for k, v in arrays.items()}
    x1 = nc.dram_tensor("x1_scratch", (HALVES, KD, P, T), F32).ap()
    out = nc.dram_tensor("out_t", (HALVES, KD, P, T), F32, kind="ExternalOutput").ap()
    build(nc, dram["x_t"], dram["params"], dram["alibi_in"], dram["eye_in"],
          {name: dram[f"w_{name}"] for name in streams}, x1, out)
    r = run(nc, [arrays], core_ids=[0])
    got = r.results[0]["out_t"]
    return np.ascontiguousarray(got.transpose(0, 3, 1, 2).reshape(1, SEQ, D))
```

```python
from contextlib import ExitStack

import numpy as np

import concourse.bass as bass
from concourse import mybir

F32 = mybir.dt.float32
F32R = mybir.dt.float32r
ACT = mybir.ActivationFunctionType
ALU = mybir.AluOpType
AX_X = mybir.AxisListType.X

P = 128
D = 1024
KD = D // P
SEQ = 1024
T = 512
HALVES = SEQ // T
D_RNN = 1280
KR = D_RNN // P
N_BLK = 16
BLK = D_RNN // N_BLK
TAPS = 4
HEADS, KV_HEADS, HD = 16, 4, 64
GRP = HEADS // KV_HEADS
D_KV = KV_HEADS * HD
PAIRS = KV_HEADS // 2
CH = 64
NCH = T // CH
D_FF = 2816
KF = D_FF // P
EPS = 1e-6
LRU_C = 8.0
MASKED = -1e30

RING = 4
CAP = 4 * P
UNIT = [4, 4]
GATE = [3, 3]
L_HEAD = UNIT + UNIT
L_STEP = UNIT + [2, 2] + UNIT + (UNIT + GATE + UNIT) * 3
L_TAIL = UNIT + [3, 3] + UNIT + [2, 2]
V_BLOCKS = [4, 4, 4, 4]
A_STEP = [2, 2, 2, 2] + [3, 3, 2, 2]
B_STEP = UNIT + UNIT
F_STEP = UNIT + UNIT
DOWN = [4, 4, 4, 4, 3, 3]

MIX_STAGES = [("head", L_HEAD, 2), ("step", L_STEP, 2), ("tail", L_TAIL, 1), ("v", V_BLOCKS, 1),
              ("q", UNIT, KD), ("a", A_STEP, KD), ("b", B_STEP, KD), ("o", UNIT, KD)]
FFN_STAGES = [("f", F_STEP, KF), ("d", DOWN, KD)]


def stage_bases(stages, base):
    out = {}
    for name, sizes, groups in stages:
        out[name] = base
        base += len(sizes) * groups
    return out, base


BASE = []
_n = 0
for _h in range(HALVES):
    _b, _n = stage_bases(MIX_STAGES, _n)
    BASE.append(_b)
for _h in range(HALVES):
    _b, _n = stage_bases(FFN_STAGES, _n)
    BASE[_h].update(_b)
N_BLOCKS = _n

PARAMS = {}
_at = 0
for _name, _w in [("g_pre_mix", KD), ("g_post_mix", KD), ("g_pre_ffn", KD), ("g_post_ffn", KD),
                  ("conv_w", TAPS * KR), ("conv_b", KR), ("lam", KR), ("sink", 8),
                  ("b_rg", KR), ("b_ig", KR), ("b_gate_lru", KD), ("b_gate_attn", KD)]:
    PARAMS[_name] = _at
    _at += _w
N_PARAMS = _at
WARM_UP = 24
PREP_STEPS = 16
DVE_LAST = 5
HALVED = PARAMS["b_rg"]


def build(nc, x_d, par_d, alibi_d, eye_d, w_d, x1_d, out_d):
    with ExitStack() as ctx:
        cursor = [0]

        def at(name, shape, dt, offset=None):
            size = 4 * int(np.prod(shape[1:]))
            size = (size + 31) // 32 * 32
            if offset is None:
                offset = cursor[0]
                cursor[0] += size
            return nc.alloc_sbuf_tensor_at(name, shape, dt, offset=offset + sbuf0)

        def sem(name):
            return ctx.enter_context(nc.semaphore(name))

        sbuf0 = (nc.sbuf_base + 31) // 32 * 32

        w_raw = at("w_raw", [P, RING, CAP], F32)
        w_hi = at("w_hi", [P, RING, CAP], F32R)
        w_lo = at("w_lo", [P, RING, CAP], F32R)
        par = at("par", [P, N_PARAMS], F32)
        half_b = at("half_b", [P, N_PARAMS - HALVED], F32)
        sp = at("sp", [P, 4, KR], F32)
        sp2 = at("sp2", [P, KR], F32)
        ones = at("ones", [P, P], F32)
        ones_r = at("ones_r", [P, P], F32R)
        eye = at("eye", [P, P], F32)
        alibi = at("alibi", [P, 8, 2 * CH], F32)
        u_carry = at("u_carry", [P, KR, TAPS - 1], F32)
        h_carry = at("h_carry", [P, KR], F32)
        dev = at("dev", [P, T // P], F32)
        stat = at("stat", [P, 6, 8], F32)
        acc = at("acc", [P, T], F32)
        acc_lo = at("acc_lo", [P, T], F32R, cursor[0])
        sq = at("sq", [P, T], F32)
        acc_hi_a = at("acc_hi_a", [P, T], F32R, cursor[0])
        rstd_a = at("rstd_a", [P, T], F32)
        acc_hi_b = at("acc_hi_b", [P, T], F32R, cursor[0])
        rstd_b = at("rstd_b", [P, T], F32)
        reg_t = cursor[0]
        tmp = at("tmp", [P, 2, T], F32)
        kd_hi = at("kd_hi", [P, PAIRS, 2, 2 * CH], F32R, reg_t)
        kd_lo = at("kd_lo", [P, PAIRS, 2, 2 * CH], F32R, reg_t + 4 * T)
        xs = at("xs", [P, 2, T], F32)
        pv_part, pv_sum = xs[:, 1, :], rstd_a[:]
        reg_h = cursor[0]
        h_hi = at("h_hi", [P, KD, T], F32R)
        x1_all = at("x1_all", [P, KD, T], F32, reg_h)
        h_lo = at("h_lo", [P, KD, T], F32R)
        rows = at("rows", [P, KD, T], F32)
        reg_b = cursor[0]
        lru_hi = at("lru_hi", [P, KR, T], F32R)
        lru_lo = at("lru_lo", [P, KR, T], F32R)
        mg_hi = at("mg_hi", [P, KD, T], F32R, reg_b)
        mg_lo = at("mg_lo", [P, KD, T], F32R, reg_b + 4 * KD * T)
        reg_c = cursor[0]
        q_hi = at("q_hi", [P, KD // 2, 2 * T], F32R)
        q_lo = at("q_lo", [P, KD // 2, 2 * T], F32R)
        uc_hi = at("uc_hi", [P, 4, T], F32R, reg_c)
        uc_lo = at("uc_lo", [P, 4, T], F32R, reg_c + 16 * T)
        uc = at("uc", [P, 4, T], F32, reg_c + 32 * T)
        gy = at("gy", [P, 4, T], F32, reg_c + 48 * T)
        reg_p = cursor[0]
        prob = at("prob", [P, 8, 2 * CH], F32)
        pt_hi = at("pt_hi", [P, 8, 2 * CH], F32R)
        pt_lo = at("pt_lo", [P, 8, 2 * CH], F32R)
        g_r = at("g_r", [P, T], F32, reg_p)
        g_a = at("g_a", [P, T], F32, reg_p + 4 * T)
        g_i = at("g_i", [P, T], F32, reg_p + 8 * T)
        g_h = at("g_h", [P, T], F32, reg_p + 12 * T)
        u_raw = at("u_raw", [P, TAPS - 1 + T], F32, reg_p + 16 * T)
        k_hi = at("k_hi", [P, PAIRS, CH + T], F32R)
        k_lo = at("k_lo", [P, PAIRS, CH + T], F32R)
        v_hl = at("v_hl", [P, NCH + 1, KV_HEADS, 2 * HD], F32R)
        v_hi, v_lo = v_hl[:, :, :, 0:HD], v_hl[:, :, :, HD:2 * HD]
        f_hi = at("f_hi", [P, KF, T], F32R, reg_b)
        f_lo = at("f_lo", [P, KF, T], F32R, reg_b + 4 * KF * T)
        assert reg_b + 8 * KF * T <= cursor[0]
        assert sbuf0 + cursor[0] <= nc.sbuf_usable_end, (sbuf0 + cursor[0], nc.sbuf_usable_end)

        ps = ctx.enter_context(nc.psum_tensor("ps", [P, 8, 512], F32))
        BK_STAT = 3
        BK_RSTD = 4
        BK_U, BK_Y = (0, 1), (2, 6)
        BK_K = (1, 0)
        BK_V = (2, 3, 6, 7)
        BK_S, BK_PT, BK_PV = 2, 4, 6

        w_loaded = [sem(f"w_loaded{i}") for i in range(RING)]
        par_loaded = sem("par_loaded")
        x0_loaded = [sem(f"x0_loaded{t}") for t in range(KD)]
        x1_all_loaded = sem("x1_all_loaded")
        alibi_loaded = sem("alibi_loaded")
        xs_loaded = [sem(f"xs_loaded{i}") for i in range(2)]
        x1_stored, out_stored = sem("x1_stored"), sem("out_stored")
        w_hi_made, w_lo_made = sem("w_hi_made"), sem("w_lo_made")
        blocks_done = sem("blocks_done")
        prep_act, prep_dve, zeroed = sem("prep_act"), sem("prep_dve"), sem("zeroed")
        squared, summed, stat_mm, dev_made, rstd_made = (
            sem("squared"), sem("summed"), sem("stat_mm"), sem("dev_made"), sem("rstd_made"))
        acc_hi_made, acc_lo_made = sem("acc_hi_made"), sem("acc_lo_made")
        table_in = sem("table_in")
        summed_0 = sem("summed_0")
        diag_made, spread, rstd_copied = sem("diag_made"), sem("spread"), sem("rstd_copied")
        normed, h_hi_made, h_lo_made = sem("normed"), sem("h_hi_made"), sem("h_lo_made")
        u_ctx, u_copied, tap0, taps, uc_hi_made, uc_lo_made = (
            sem("u_ctx"), sem("u_copied"), sem("tap0"), sem("taps"), sem("uc_hi_made"),
            sem("uc_lo_made"))
        r_made, i_made, th_made, th1_made, root_made, a_made, gelu_made, lru_hi_made = (
            sem("r_made"), sem("i_made"), sem("th_made"), sem("th1_made"), sem("root_made"),
            sem("a_made"), sem("gelu_made"), sem("lru_hi_made"))
        iu_made, recip_made, amp_made, b_made, scanned, h_kept, lru_made, lru_lo_made = (
            sem("iu_made"), sem("recip_made"), sem("amp_made"), sem("b_made"), sem("scanned"),
            sem("h_kept"), sem("lru_made"), sem("lru_lo_made"))
        kept_hi, kept_lo = sem("kept_hi"), sem("kept_lo")
        kd_zeroed, kd_hi_made, kd_lo_made = sem("kd_zeroed"), sem("kd_hi_made"), sem("kd_lo_made")
        k_hi_made, k_lo_made, v_hi_made, v_lo_made = (
            sem("k_hi_made"), sem("k_lo_made"), sem("v_hi_made"), sem("v_lo_made"))
        q_hi_made, q_lo_made = sem("q_hi_made"), sem("q_lo_made")
        qk_done, biased, maxed, exped, probed, pt_done, pt_hi_made, pt_lo_made, pv_done = (
            sem("qk_done"), sem("biased"), sem("maxed"), sem("exped"), sem("probed"),
            sem("pt_done"), sem("pt_hi_made"), sem("pt_lo_made"), sem("pv_done"))
        pv_parted, pv_summed = sem("pv_parted"), sem("pv_summed")
        ao_hi_made, ao_lo_made = sem("ao_hi_made"), sem("ao_lo_made")
        ga_made, lru_part = sem("ga_made"), sem("lru_part")
        gb_made, attn_part, merged, mg_hi_made, mg_lo_made = (
            sem("gb_made"), sem("attn_part"), sem("merged"), sem("mg_hi_made"), sem("mg_lo_made"))
        row_out = sem("row_out")
        silu_made, f_made, f_hi_made, f_lo_made = (
            sem("silu_made"), sem("f_made"), sem("f_hi_made"), sem("f_lo_made"))
        scaled, added = sem("scaled"), sem("added")
        pool_scaled, pool_added = sem("pool_scaled"), sem("pool_added")
        waits_closed = sem("waits_closed")

        def wait_pos(eng, s, value):
            if not isinstance(value, int) or value > 0:
                eng.wait_ge(s, value)

        def own_wait(eng):
            eng.sem_inc(waits_closed, 1)

        def col(name, t, n=1):
            return par[:, bass.ds(t + PARAMS[name], n)]

        def half_col(name, t):
            return half_b[:, bass.ds(t + (PARAMS[name] - HALVED), 1)]

        def q_tile(q, pair, j):
            return q[:, bass.ds(pair, 1), :].rearrange("p o (c j t) -> p (o c) j t", j=2, t=CH)[:, :, j, :]

        def v_whole(v, a):
            return v[:, 4 * a + 1:4 * a + 4:2]

        def v_out(a):
            return ps[:, BK_V[2 * a]:BK_V[2 * a] + 2, 0:D_KV].rearrange("p b (g d) -> p b g d", d=HD)

        def rd(ap):
            return ap.bitcast(F32)

        def sum_base(n):
            return (KD + 1) * (n - 1)

        def acc_hi_of(n):
            return acc_hi_b if n in (1, 3, 5) else acc_hi_a

        def rstd_of(n):
            return rstd_b if n in (1, 3, 5) else rstd_a

        block = ctx.enter_context(nc.Block())

        @block.sync
        def _(sp_eng):
            def load(dram, g, sizes, n):
                off = 0
                for b, size in enumerate(sizes):
                    wait_pos(sp_eng, w_lo_made, n + b - RING + 1)
                    sp_eng.dma_start(w_raw[:, b % RING, 0:size * P],
                                     dram[g, :, off:off + size * P]).then_inc(w_loaded[b % RING], 16)
                    off += size * P

            def stream(stages, bases):
                for name, sizes, groups in stages:
                    per = 1 if len(sizes) % RING == 0 else 2
                    sizes2, dram, base = sizes * per, w_d[name], bases[name]
                    n_it = groups // per
                    first = 1 if base == 0 else 0
                    if first:
                        load(dram, 0, sizes2, 0)
                    if n_it - first == 1:
                        load(dram, first, sizes2, base + first * len(sizes2))
                    elif n_it > first:
                        with sp_eng.Fori(first, n_it) as g:
                            load(dram, g, sizes2, g * len(sizes2) + base)

            for t in range(KD):
                sp_eng.dma_start(rows[:, t, :], x_d[0][t]).then_inc(x0_loaded[t], 16)
            sp_eng.dma_start(par[:], par_d).then_inc(par_loaded, 16)
            sp_eng.dma_start(eye[:], eye_d).then_inc(par_loaded, 16)
            for h in range(HALVES):
                stream(MIX_STAGES, BASE[h])
            for h in range(HALVES):
                stream(FFN_STAGES, BASE[h])

        @block.gpsimd
        def _(pool):
            nc.gpsimd.memset(ones[:], 1.0).then_inc(zeroed, 1)
            nc.gpsimd.memset(u_carry[:], 0.0).then_inc(zeroed, 1)
            nc.gpsimd.memset(h_carry[:], 0.0).then_inc(zeroed, 1)
            nc.gpsimd.memset(rd(k_hi[:, :, 0:CH]), 0.0).then_inc(zeroed, 1)
            nc.gpsimd.memset(rd(k_lo[:, :, 0:CH]), 0.0).then_inc(zeroed, 1)
            nc.gpsimd.memset(rd(v_hl[0:CH, 0, :, :]), 0.0).then_inc(zeroed, 1)

            def split(sizes, n, turn):
                for b, size in enumerate(sizes):
                    s, w = b % RING, slice(0, size * P)
                    pool.wait_ge(w_loaded[s], (turn + b // RING + 1) * 16)
                    wait_pos(pool, blocks_done, n + b - RING + 1)
                    own_wait(pool)
                    nc.gpsimd.tensor_scalar(w_hi[:, s, w], w_raw[:, s, w], 1.0, 0.0,
                                            ALU.mult, ALU.add).then_inc(w_hi_made, 1)
                    pool.wait_ge(w_hi_made, n + b + 1)
                    nc.gpsimd.tensor_tensor(w_lo[:, s, w], w_raw[:, s, w], rd(w_hi[:, s, w]),
                                            ALU.subtract).then_inc(w_lo_made, 1)

            def stream(stages, bases):
                for name, sizes, groups in stages:
                    per = 1 if len(sizes) % RING == 0 else 2
                    sizes2, base = sizes * per, bases[name]
                    n_it = groups // per
                    first = 1 if base == 0 else 0
                    assert base % RING == 0 and len(sizes2) % RING == 0
                    turns = len(sizes2) // RING
                    if first:
                        split(sizes2, 0, 0)
                    if n_it - first == 1:
                        split(sizes2, base + first * len(sizes2), base // RING + first * turns)
                    elif n_it > first:
                        with pool.Fori(first, n_it) as g:
                            split(sizes2, g * len(sizes2) + base, g * turns + base // RING)

            for h in range(HALVES):
                stream(MIX_STAGES, BASE[h])
            for h in range(HALVES):
                stream(FFN_STAGES, BASE[h])

            pool.wait_ge(rstd_copied, 1)
            pool.wait_ge(row_out, 2 * KD * 4)
            for i, t in enumerate(range(DVE_LAST, KD)):
                nc.gpsimd.tensor_tensor(rows[:, t, :], rows[:, t, :], rstd_b[:], ALU.mult)\
                    .then_inc(pool_scaled, 1)
                pool.wait_ge(x1_all_loaded, 16 * KD)
                pool.wait_ge(pool_scaled, i + 1)
                nc.gpsimd.tensor_tensor(rows[:, t, :], rows[:, t, :], x1_all[:, t, :], ALU.add)\
                    .then_inc(pool_added, 1)

        @block.tensor
        def _(pe):
            mm = nc.tensor.matmul

            def project(bank, n, slot, sizes, hi, lo, ready=None, tiles=None, inner=None,
                        inner_at=0):
                total, k = sum(sizes), 0
                out = ps[:, bank, :] if isinstance(bank, int) else ps[:, bass.ds(bank, 1), :]
                for b, size in enumerate(sizes):
                    pe.wait_ge(w_lo_made, n + b + 1)
                    s = (slot + b) % RING
                    for q in range(size):
                        if ready:
                            pe.wait_ge(ready[0], ready[1] + k + 1)
                        w = slice(q * P, (q + 1) * P)
                        kk = tiles[k] if tiles else k
                        if hi is q_hi:
                            x_hi, x_lo = q_tile(hi, kk // 2, kk % 2), q_tile(lo, kk // 2, kk % 2)
                        elif isinstance(kk, int):
                            x_hi, x_lo = hi[:, kk, :], lo[:, kk, :]
                        else:
                            x_hi, x_lo = hi[:, bass.ds(kk, 1), :], lo[:, bass.ds(kk, 1), :]
                        mm(out, w_hi[:, s, w], x_hi, start=(k == 0), stop=False)
                        mm(out, w_hi[:, s, w], x_lo, start=False, stop=False)
                        last = mm(out, w_lo[:, s, w], x_hi, start=False,
                                  stop=(k == total - 1))
                        k += 1
                    last.then_inc(blocks_done, 1)
                    if inner and b == inner_at:
                        inner()

            def narrow_sum(part, start, stop):
                for m in range(T // P):
                    last = mm(ps[:, m, 0:2], part[:, m * P:(m + 1) * P], ones[:, 0:2],
                              start=start, stop=stop)
                if stop:
                    last.then_inc(stat_mm, 1)

            def spread_rstd(done):
                pe.wait_ge(diag_made, done)
                mm(ps[:, BK_RSTD, :], ones[:], rstd_a[:], start=True, stop=True).then_inc(spread, 1)

            def stat_sum(n):
                pe.wait_ge(acc_hi_made, n + 1)
                pe.wait_ge(acc_lo_made, n)
                wait_pos(pe, dev_made, n)
                wait_pos(pe, biased, NCH * min((n + 1) // 2, HALVES))
                mm(ps[:, BK_STAT, :], ones_r[:], acc_hi_of(n)[:], start=True, stop=False)
                mm(ps[:, BK_STAT, :], ones_r[:], acc_lo[:], start=False, stop=True).then_inc(stat_mm, 1)

            def gates(h, j, n, size, slot, q, first=None):
                J = j + KR * h
                last_tile = size == 2 and first is None
                pe.wait_ge(uc_lo_made, J + (1 if last_tile else 2))
                if last_tile:
                    pe.wait_ge(r_made, J)
                    pe.wait_ge(i_made, J)
                tiles = first or [(q + d) % 4 for d in (-1, 0, 1)][:size]
                for g in range(2):
                    project(4 + g, n + g, slot + g, [size], uc_hi, uc_lo, tiles=tiles)

            def head(h, j, ready):
                n = BASE[h]["head"] + 4 * j
                wait_pos(pe, row_out, 2 * (BK_Y[j] + 1) * h)
                for b in range(2):
                    for u, bank in enumerate((BK_U[j], BK_Y[j])):
                        pe.wait_ge(w_lo_made, n + 2 * b + u + 1)
                        for q in range(4):
                            k, w = 4 * b + q, slice(q * P, (q + 1) * P)
                            if ready:
                                pe.wait_ge(h_lo_made, KD * h + k + 1)
                            s = 2 * b + u
                            mm(ps[:, bank, :], w_hi[:, s, w], h_hi[:, k, :], start=(k == 0), stop=False)
                            mm(ps[:, bank, :], w_hi[:, s, w], h_lo[:, k, :], start=False, stop=False)
                            last = mm(ps[:, bank, :], w_lo[:, s, w], h_hi[:, k, :], start=False,
                                      stop=(k == KD - 1))
                        last.then_inc(blocks_done, 1)

            def recurrent(h):
                for j in range(2):
                    head(h, j, j == 0)
                if h:
                    stat_sum(2)
                with pe.Fori(0, 2) as it:
                    for q in range(4):
                        j = it * 4 + (2 + q)
                        n = (it * 4 + q) * 6 + BASE[h]["step"]
                        slot = 6 * q
                        wait_pos(pe, u_copied, (j + KR * h) * 2)
                        project(0, n, slot, UNIT, h_hi, h_lo)
                        if q:
                            gates(h, j - 2, n + 2, 3, slot + 2, q)
                        else:
                            gates(h, j - 2, n + 2, 2, slot + 2, q, [it * 3, it * -1 + 1])
                        wait_pos(pe, gelu_made, j + KR * h)
                        project(2, n + 4, slot + 4, UNIT, h_hi, h_lo)

            def kvq(h):
                n, n_v, n_q = BASE[h]["tail"], BASE[h]["v"], BASE[h]["q"]
                wait_pos(pe, row_out, 2 * KD * h)
                project(BK_K[0], n, 0, UNIT, h_hi, h_lo)
                gates(h, 8, n + 2, 3, 2, 0)
                pe.wait_ge(u_copied, 2 * KR * (h + 1))
                project(BK_K[1], n + 4, 0, UNIT, h_hi, h_lo)
                gates(h, 9, n + 6, 2, 2, 1)
                pe.wait_ge(gelu_made, KR * (h + 1))
                pe.wait_ge(dev_made, 3 if h else 1)
                for b in range(4):
                    pe.wait_ge(w_lo_made, n_v + b + 1)
                    for m in range(4):
                        out = ps[:, BK_V[m], 0:D_KV]
                        for q in range(2):
                            k = 2 * b + q
                            w = slice(q * D_KV, (q + 1) * D_KV)
                            t = slice(m * P, (m + 1) * P)
                            mm(out, h_hi[:, k, t], w_hi[:, b, w], start=(k == 0), stop=False)
                            mm(out, h_lo[:, k, t], w_hi[:, b, w], start=False, stop=False)
                            last = mm(out, h_hi[:, k, t], w_lo[:, b, w], start=False, stop=(k == KD - 1))
                    last.then_inc(blocks_done, 1)
                pe.wait_ge(k_hi_made, PAIRS * (h + 1))
                pe.wait_ge(k_lo_made, PAIRS * (h + 1))
                for t in range(2):
                    project(t, n_q + 2 * t, 2 * t, UNIT, h_hi, h_lo)
                with pe.Fori(1, 4) as it:
                    for q in range(2):
                        t = it * 2 + q
                        pe.wait_ge(q_lo_made, t + (KD * h - 1))
                        project(q, t * 2 + n_q, 2 * q, UNIT, h_hi, h_lo)

            def scores(h, c):
                C = NCH * h + c
                pe.wait_ge(biased, C) if C else None
                pe.wait_ge(kd_hi_made, 2 * (C + 1))
                pe.wait_ge(kd_lo_made, 2 * (C + 1))
                cq = slice(c * P, (c + 1) * P)
                for p in range(PAIRS):
                    for b in range(2):
                        out = ps[:, BK_S + p, b * 4 * CH:(b + 1) * 4 * CH]
                        t = 2 * p + b
                        mm(out, q_hi[:, t, cq], kd_hi[:, p, :, :], start=True, stop=False)
                        mm(out, q_hi[:, t, cq], kd_lo[:, p, :, :], start=False, stop=False)
                        last = mm(out, q_lo[:, t, cq], kd_hi[:, p, :, :], start=False, stop=True)
                last.then_inc(qk_done, 1)

            def turn_probs(h, c):
                C = NCH * h + c
                pe.wait_ge(probed, 3 * (C + 1))
                wait_pos(pe, pt_lo_made, C)
                for i in range(8):
                    last = nc.tensor.transpose(ps[:, BK_PT + i // 4, (i % 4) * P:(i % 4 + 1) * P],
                                               prob[:, i, :], eye[:])
                last.then_inc(pt_done, 1)

            def weigh_values(h, c):
                C = NCH * h + c
                pe.wait_ge(pt_lo_made, C + 1)
                wait_pos(pe, pv_summed, 2 * C)
                for half in range(2):
                    for p in range(PAIRS):
                        out = ps[:, BK_PV + half, p * 256:(p + 1) * 256]
                        v = v_hl[:, c, 2 * p + half, :]
                        t = slice(4 * p + half, 4 * p + half + 3, 2)
                        mm(out, v, pt_hi[:, t, :], start=True, stop=False)
                        last = mm(out, v, pt_lo[:, t, :], start=False, stop=True)
                last.then_inc(pv_done, 1)

            def attention(h):
                pe.wait_ge(q_lo_made, KD * (h + 1) - 1)
                for c in range(NCH):
                    n = BASE[h]["a"] + 8 * c
                    if c == 0:
                        def begin():
                            pe.wait_ge(q_lo_made, KD * (h + 1))
                            pe.wait_ge(v_hi_made, 4 * h + 2)
                            pe.wait_ge(v_lo_made, 4 * h + 2)
                            scores(h, 0)

                        project(0, n, 0, A_STEP[:4], h_hi, h_lo, inner=begin, inner_at=2)
                        pe.wait_ge(lru_lo_made, KR * (h + 1))
                    else:
                        scores(h, c)
                        pe.wait_ge(ga_made, NCH * h + c)
                        if c == 1:
                            pe.wait_ge(r_made, KR * (h + 1))
                            pe.wait_ge(i_made, KR * (h + 1))
                            project(0, n, 0, A_STEP[:4], h_hi, h_lo, inner=lambda: turn_probs(h, 0),
                                    inner_at=0)
                            pe.wait_ge(v_hi_made, 4 * (h + 1))
                            pe.wait_ge(v_lo_made, 4 * (h + 1))
                        else:
                            project(0, n, 0, A_STEP[:4], h_hi, h_lo)
                        weigh_values(h, c - 1)
                        pe.wait_ge(lru_part, NCH * h + c)
                    project(1, n + 4, 0, A_STEP[4:], lru_hi, lru_lo)
                    if c:
                        turn_probs(h, c)

            def attn_branch(h):
                base = BASE[h]["b"]
                pe.wait_ge(ga_made, NCH * (h + 1))
                project(0, base, 0, UNIT, h_hi, h_lo, inner=lambda: weigh_values(h, NCH - 1),
                        inner_at=0)
                stat_sum(1 + 2 * h)
                pe.wait_ge(lru_part, NCH * (h + 1))
                pe.wait_ge(ao_lo_made, NCH * (h + 1))
                project(1, base + 2, 2, UNIT, q_hi, q_lo)
                with pe.Fori(1, KD) as c:
                    pe.wait_ge(gb_made, c + KD * h)
                    project(0, c * 4 + base, 0, UNIT, h_hi, h_lo)
                    pe.wait_ge(attn_part, c + KD * h)
                    project(1, c * 4 + (base + 2), 2, UNIT, q_hi, q_lo)

            def out_tiles(base, sizes, hi, lo, bank0, bank1, ready):
                for t in range(2):
                    pe.wait_ge(*(bank1 if t else bank0))
                    project(t, base + len(sizes) * t, len(sizes) * t, sizes, hi, lo,
                            None if t else ready[:2])
                pe.wait_ge(dev_made, ready[2])
                with pe.Fori(1, KD // 2) as it:
                    for q in range(2):
                        t = it * 2 + q
                        project(t, t * len(sizes) + base, len(sizes) * q, sizes, hi, lo)

            def ffn_up(h):
                base = BASE[h]["f"]

                for t in range(2):
                    if t == 0:
                        pe.wait_ge(row_out, 2 * (KD * (1 + h) + 1))
                    else:
                        pe.wait_ge(silu_made, KF * h + t)
                    project(0, base + 4 * t, 0, UNIT, h_hi, h_lo,
                            (h_lo_made, KD * (2 + h)) if t == 0 else None)
                    if t == 0:
                        pe.wait_ge(row_out, 2 * (KD * (1 + h) + 2))
                    else:
                        pe.wait_ge(f_made, KF * h + t)
                    project(1, base + 4 * t + 2, 2, UNIT, h_hi, h_lo)
                stat_sum(6 if h else 4)
                with pe.Fori(2, KF) as t:
                    pe.wait_ge(silu_made, t + KF * h)
                    project(0, t * 4 + base, 0, UNIT, h_hi, h_lo)
                    pe.wait_ge(f_made, t + KF * h)
                    project(1, t * 4 + (base + 2), 2, UNIT, h_hi, h_lo)

            pe.wait_ge(zeroed, 6)
            with pe.Fori(0, WARM_UP) as _:
                mm(ps[:, 7, 0:P], ones[:], ones[:], start=True, stop=True)
            pe.wait_ge(summed_0, KD - 1)
            narrow_sum(acc, True, True)
            spread_rstd(1)
            for h in range(HALVES):
                recurrent(h)
                kvq(h)
                pe.wait_ge(par_loaded, 32)
                attention(h)
                attn_branch(h)
                out_tiles(BASE[h]["o"], UNIT, mg_hi, mg_lo, (gb_made, KD * (h + 1)),
                          (attn_part, KD * (h + 1)), (mg_lo_made, KD * h, 2 + 2 * h))
            for h in range(HALVES):
                ffn_up(h)
                if h == 0:
                    stat_sum(5)
                out_tiles(BASE[h]["d"], DOWN, f_hi, f_lo, (silu_made, KF * (h + 1)),
                          (f_made, KF * (h + 1)), (f_lo_made, KF * h, 6 + h))
            pe.wait_ge(summed, sum_base(8) - 1)
            pe.wait_ge(row_out, 2 * KD * 4 - 2)
            narrow_sum(acc, True, False)
            pe.wait_ge(row_out, 2 * KD * 4 - 1)
            narrow_sum(sq, False, True)
            spread_rstd(2)

        @block.scalar
        def _(act):
            fn = nc.scalar.activation

            def load_xs(s, t, src):
                act.dma_start(xs[:, t % 2, :], src[t]).then_inc(xs_loaded[t % 2], 16)

            def deviation(n):
                act.wait_ge(stat_mm, n + 1)
                fn(rstd_of(n)[:], ps[:, BK_STAT, :], ACT.Sqrt, bias=eps_ap, scale=1.0 / D)\
                    .then_inc(dev_made, 1)

            def acc_hi(n):
                act.wait_ge(summed, sum_base(n + 1))
                fn(acc_hi_of(n)[:], acc[:], ACT.Copy).then_inc(acc_hi_made, 1)

            def narrow_deviation(n):
                act.wait_ge(stat_mm, n + 1)
                fn(dev.rearrange("p (m o) -> p m o", o=1), ps[:, 0:4, 0:1], ACT.Sqrt, bias=eps_ap,
                   scale=1.0 / D).then_inc(dev_made, 1)

            def square(n, t, src):
                wait_pos(act, summed, t + (sum_base(n) + 1))
                fn(sq[:], src, ACT.Square).then_inc(squared, 1)

            def norm_hi(k, t):
                act.wait_ge(normed, KD * k + t + 1)
                fn(h_hi[:, t, :], tmp[:, t % 2, :], ACT.Copy).then_inc(h_hi_made, 1)

            def conv_in(h, j, done, q, bank=0):
                J = j + KR * h
                act.wait_ge(blocks_done, done)
                wait_pos(act, taps, J * 3)
                own_wait(act)
                fn(u_raw[:, 0:TAPS - 1], u_carry[:, bass.ds(j, 1), :], ACT.Copy).then_inc(u_ctx, 1)
                fn(u_raw[:, TAPS - 1:], ps[:, bank, :], ACT.Copy).then_inc(u_copied, 1)
                act.wait_ge(u_ctx, J + 1)
                own_wait(act)
                fn(u_carry[:, bass.ds(j, 1), :], ps[:, bank, T - TAPS + 1:T], ACT.Copy)\
                    .then_inc(u_copied, 1)
                act.wait_ge(u_copied, J * 2 + 1)
                own_wait(act)
                fn(uc[:, q, :], u_raw[:, 0:T], ACT.Identity, bias=col("conv_b", j),
                   scale=col("conv_w", j)).then_inc(tap0, 1)

            def conv_hi(h, j, q):
                act.wait_ge(taps, (j + KR * h) * 3 + 3)
                fn(uc_hi[:, q, :], uc[:, q, :], ACT.Copy).then_inc(uc_hi_made, 1)

            def gate_fns(h, j, n):
                J = j + KR * h
                act.wait_ge(blocks_done, n + 2)
                own_wait(act)
                fn(g_r[:], ps[:, 4, :], ACT.Tanh, bias=half_col("b_rg", j), scale=0.5)\
                    .then_inc(r_made, 1)
                fn(g_i[:], ps[:, 5, :], ACT.Tanh, bias=half_col("b_ig", j), scale=0.5)\
                    .then_inc(i_made, 1)
                act.wait_ge(r_made, J + 1)
                own_wait(act)
                fn(g_r[:], g_r[:], ACT.Tanh, bias=sp2[:, bass.ds(j, 1)],
                   scale=sp2[:, bass.ds(j, 1)]).then_inc(th_made, 1)
                act.wait_ge(th_made, J + 1)
                fn(g_a[:], g_r[:], ACT.Identity, bias=one_ap).then_inc(th1_made, 1)

            def gate_root(h, j):
                J = j + KR * h
                act.wait_ge(th1_made, J + 1)
                fn(g_r[:], g_r[:], ACT.Sqrt).then_inc(root_made, 1)

            def gelu(h, j, done, q, bank=2):
                J = j + KR * h
                act.wait_ge(blocks_done, done)
                fn(gy[:, q, :], ps[:, bank, :], ACT.Gelu_apprx_tanh).then_inc(gelu_made, 1)

            def decay(h, j):
                act.wait_ge(amp_made, j + KR * h + 1)
                fn(g_a[:], g_a[:], ACT.Identity, bias=neg_ap, scale=2.0).then_inc(a_made, 1)

            def lru_out_hi(h, j):
                act.wait_ge(lru_made, j + KR * h + 1)
                own_wait(act)
                fn(lru_hi[:, bass.ds(j, 1), :], g_h[:], ACT.Copy).then_inc(lru_hi_made, 1)

            def recurrent(h):
                for j in range(2):
                    done = BASE[h]["head"] + 4 * j
                    conv_in(h, j, done + 3, j, BK_U[j])
                    conv_hi(h, j, j)
                    gelu(h, j, done + 4, j, BK_Y[j])
                if h:
                    deviation(2)
                else:
                    lam = par[:, PARAMS["lam"]:PARAMS["lam"] + KR]
                    fn(sp[:, 0, :], lam, ACT.Abs).then_inc(prep_act, 1)
                    act.wait_ge(prep_act, 1)
                    fn(sp[:, 1, :], sp[:, 0, :], ACT.Exp, scale=-1.0).then_inc(prep_act, 1)
                    act.wait_ge(prep_dve, PREP_STEPS)
                for q in range(2):
                    load_xs(2 * h, q, x_d[1 - h])
                with act.Fori(0, 2) as it:
                    for q in range(4):
                        j = it * 4 + (2 + q)
                        n = (it * 4 + q) * 6 + BASE[h]["step"]
                        conv_in(h, j, n + 2, (2 + q) % 4)
                        gate_fns(h, j - 2, n + 2)
                        conv_hi(h, j, (2 + q) % 4)
                        gate_root(h, j - 2)
                        gelu(h, j, n + 6, (2 + q) % 4)
                        decay(h, j - 2)
                        lru_out_hi(h, j - 2)

            def keys(c, C):
                wait_pos(act, qk_done, C)
                own_wait(act)
                for half in range(2):
                    r = slice(64 * half, 64 * half + 64)
                    fn(kd_hi[r, :, half, :], rd(k_hi[r, :, bass.ds(c * CH, 2 * CH)]), ACT.Copy)\
                        .then_inc(kd_hi_made, 1)

            def shift_v(h):
                act.wait_ge(v_hi_made, 4 * h + 2)
                fn(v_hi[CH:P, 0:NCH:2], rd(v_hi[0:CH, 1:NCH + 1:2]), ACT.Copy)\
                    .then_inc(v_hi_made, 1)
                fn(v_hi[0:CH, 2:NCH + 1:2], rd(v_hi[CH:P, 1:NCH + 1:2]), ACT.Copy)\
                    .then_inc(v_hi_made, 1)

            def kvq(h):
                n, n_q = BASE[h]["tail"], BASE[h]["q"]
                if h:
                    act.wait_ge(pv_done, NCH)
                    fn(k_hi[:, :, 0:CH], rd(k_hi[:, :, T:T + CH]), ACT.Copy).then_inc(kept_hi, 1)
                    fn(v_hi[0:CH, 0], rd(v_hi[0:CH, NCH]), ACT.Copy).then_inc(kept_hi, 1)
                    act.wait_ge(kept_hi, 2)
                else:
                    act.wait_ge(zeroed, 6)
                for p in range(PAIRS):
                    act.wait_ge(blocks_done, n + 4 * p + 2)
                    fn(k_hi[:, p, CH:CH + T], ps[:, BK_K[p], :], ACT.Copy).then_inc(k_hi_made, 1)
                    if p:
                        act.wait_ge(kd_zeroed, 4 * (h + 1))
                        act.wait_ge(k_hi_made, PAIRS * (h + 1))
                        keys(0, NCH * h)
                    gate_fns(h, 8 + p, n + 4 * p + 2)
                    gate_root(h, 8 + p)
                    if p:
                        act.wait_ge(blocks_done, BASE[h]["v"] + 4)
                        for a in range(2):
                            fn(v_whole(v_hi, a), v_out(a), ACT.Copy).then_inc(v_hi_made, 1)
                    decay(h, 8 + p)
                    lru_out_hi(h, 8 + p)
                act.wait_ge(lru_lo_made, KR * (h + 1))

                def pair(it, more):
                    for q in range(2):
                        t = it * 2 + q
                        act.wait_ge(blocks_done, t * 2 + (n_q + 2))
                        own_wait(act)
                        fn(q_tile(q_hi, it, q), ps[:, q, :].rearrange("p (c t) -> p c t", t=CH),
                           ACT.Copy).then_inc(q_hi_made, 1)
                        if h:
                            x1_out(0, t)
                        else:
                            act.wait_ge(xs_loaded[q], it * 16 + 16)
                            own_wait(act)
                            square(1, t, xs[:, q, :])
                            act.wait_ge(squared, t + (KD + 1))
                        if more:
                            load_one(x_d[1 - h], t + 2, q)

                with act.Fori(0, KD // 2 - 1) as it:
                    pair(it, True)
                pair(KD // 2 - 1, False)
                if h == 0:
                    act.wait_ge(squared, 2 * KD)

            def attention(h):
                def exps(C):
                    act.wait_ge(maxed, C * 4 + 4)
                    for i in range(8):
                        fn(prob[:, i, :], prob[:, i, :], ACT.Exp, bias=stat[:, 2, i:i + 1],
                           accum_out=stat[:, 3, i:i + 1]).then_inc(exped, 1)
                    fn(stat[:, 4, :], stat[:, 1, :], ACT.Exp).then_inc(exped, 1)

                def gate(c, C):
                    act.wait_ge(blocks_done, c * 8 + (BASE[h]["a"] + 4))
                    wait_pos(act, lru_part, C)
                    own_wait(act)
                    fn(xs[:, 0, :], ps[:, 0, :], ACT.Tanh, bias=half_col("b_gate_lru", c),
                       scale=0.5).then_inc(ga_made, 1)

                def out_hi(c, C):
                    act.wait_ge(pv_done, C + 1)
                    own_wait(act)
                    fn(pv_part[0:HD, :], ps[HD:P, BK_PV, :], ACT.Copy).then_inc(pv_parted, 1)
                    fn(pv_part[HD:P, :], ps[0:HD, BK_PV + 1, :], ACT.Copy).then_inc(pv_parted, 1)
                    act.wait_ge(pv_summed, C * 2 + 2)
                    own_wait(act)
                    fn(q_hi[:, :, bass.ds(c * P, P)], pv_sum.rearrange("p (t q) -> p t q", q=P),
                       ACT.Copy).then_inc(ao_hi_made, 1)

                def turned_hi(C):
                    act.wait_ge(pt_done, C + 1)
                    fn(pt_hi[:, :, :], ps[:, BK_PT:BK_PT + 2, :].rearrange("p b (i k) -> p (b i) k", i=4),
                       ACT.Copy).then_inc(pt_hi_made, 1)

                def chunk(c, C, more=True):
                    if more:
                        keys(c + 1, C + 1)
                    exps(C)
                    gate(c, C)
                    if isinstance(c, int) and c == 0:
                        shift_v(h)
                        acc_hi(1 + 2 * h)
                    if not isinstance(c, int) or c:
                        out_hi(c - 1, C - 1)
                    turned_hi(C)

                chunk(0, NCH * h)
                if h == 0:
                    act.wait_ge(biased, 1)
                    act.dma_start(alibi[:], alibi_d[1]).then_inc(alibi_loaded, 16)
                with act.Fori(1, NCH - 1) as c:
                    chunk(c, c + NCH * h)
                chunk(NCH - 1, NCH * (h + 1) - 1, False)
                out_hi(NCH - 1, NCH * (h + 1) - 1)

            def attn_branch(h):
                def tile(c, C):
                    act.wait_ge(blocks_done, c * 4 + (BASE[h]["b"] + 2))
                    wait_pos(act, attn_part, C) if not isinstance(c, int) else \
                        act.wait_ge(lru_part, NCH * (h + 1))
                    own_wait(act)
                    fn(tmp[:, 0, :], ps[:, 0, :], ACT.Tanh, bias=half_col("b_gate_attn", c),
                       scale=0.5).then_inc(gb_made, 1)
                    act.wait_ge(merged, C + 1)
                    own_wait(act)
                    fn(mg_hi[:, bass.ds(c, 1), :], tmp[:, 1, :], ACT.Copy, scale=0.5)\
                        .then_inc(mg_hi_made, 1)

                tile(0, KD * h)
                deviation(1 + 2 * h)
                with act.Fori(1, KD) as c:
                    tile(c, c + KD * h)

            def row_tile(n, t, done):
                act.wait_ge(blocks_done, done)
                bank = ps[:, bass.ds(t, 1), :]
                act.wait_ge(summed, t + (sum_base(n) + 1))
                own_wait(act)
                fn(sq[:], bank, ACT.Square).then_inc(row_out, 1)
                if n == 7:
                    fn(rows[:, bass.ds(t, 1), :], bank, ACT.Copy, scale=col("g_post_ffn", t))\
                        .then_inc(row_out, 1)
                else:
                    fn(rows[:, bass.ds(t, 1), :], bank, ACT.Copy).then_inc(row_out, 1)

            def rows_out(n, base, size, between):
                for t in range(2):
                    row_tile(n, t, base + size * (t + 1))
                between()
                with act.Fori(2, KD) as t:
                    row_tile(n, t, t * size + (base + size))
                if n != 7:
                    acc_hi(n)

            def normed_stream(k, s, src):
                for t in range(2):
                    load_xs(s, t, src)
                for t in range(KD):
                    norm_hi(k, t)
                    if t + 2 < KD:
                        load_xs(s, t + 2, src)

            def load_one(src, t, q):
                own_wait(act)
                act.dma_start(xs[:, q, :], src[bass.ds(t, 1), :, :]
                              .rearrange("o p t -> (o p) t")).then_inc(xs_loaded[q], 16)

            def x1_out(h, t):
                act.wait_ge(added, t + (KD * h + 1))
                own_wait(act)
                act.dma_start(x1_d[h][bass.ds(t, 1), :, :].rearrange("o p t -> (o p) t"),
                              rows[:, bass.ds(t, 1), :].rearrange("p o t -> p (o t)"))\
                    .then_inc(x1_stored, 16)
                act.wait_ge(summed, t + (sum_base(3 + 2 * h) + 1))
                own_wait(act)
                fn(sq[:], rows[:, bass.ds(t, 1), :], ACT.Square).then_inc(squared, 1)

            one_ap, neg_ap, eps_ap = 1.0, -1.0, EPS
            act.wait_ge(zeroed, 6)
            fn(ones_r[:], ones[:], ACT.Copy).then_inc(acc_hi_made, 1)

            for t in range(KD):
                act.wait_ge(x0_loaded[t], 16)
                fn(x1_all[:, t, :], rows[:, t, :], ACT.Square).then_inc(squared, 1)
            narrow_deviation(0)
            act.dma_start(alibi[:], alibi_d[0]).then_inc(alibi_loaded, 16)
            for t in range(KD):
                norm_hi(0, t)

            for h in range(HALVES):
                recurrent(h)
                kvq(h)
                attention(h)
                attn_branch(h)
                n, o = 2 + 2 * h, BASE[h]["o"]
                if h == 0:
                    rows_out(n, o, 2, lambda: normed_stream(1, 1, x_d[1]))
                else:
                    act.wait_ge(x1_stored, 16 * KD)
                    rows_out(n, o, 2, lambda: normed_stream(2, 3, x1_d[0]))
            for h in range(HALVES):
                def tile(t, F):
                    act.wait_ge(blocks_done, t * 4 + (BASE[h]["f"] + 2))
                    if isinstance(t, int) and t == 0:
                        act.wait_ge(h_lo_made, KD * (3 + h))
                    else:
                        act.wait_ge(f_made, F)
                    fn(tmp[:, 0, :], ps[:, 0, :], ACT.Silu).then_inc(silu_made, 1)
                    act.wait_ge(f_made, F + 1)
                    own_wait(act)
                    fn(f_hi[:, bass.ds(t, 1), :], tmp[:, 1, :], ACT.Copy).then_inc(f_hi_made, 1)

                for t in range(2):
                    tile(t, KF * h + t)
                deviation(4 + 2 * h)
                with act.Fori(0, KD // 2) as it:
                    for q in range(2):
                        load_one(x1_d[0] if h else x_d[1], it * 2 + q, q)
                    for q in range(2):
                        t = it * 2 + (2 + q)
                        tile(t, t + KF * h)
                        c = it * 2 + q
                        if h == 0:
                            x1_out(1, c)
                        else:
                            act.wait_ge(added, c + (2 * KD + 1))
                            own_wait(act)
                            act.dma_start(out_d[0][bass.ds(c, 1), :, :].rearrange("o p t -> (o p) t"),
                                          rows[:, bass.ds(c, 1), :].rearrange("p o t -> p (o t)"))\
                                .then_inc(out_stored, 16)
                if h == 0:
                    acc_hi(5)
                with act.Fori(KD + 2, KF) as t:
                    tile(t, t + KF * h)
                if h == 0:
                    deviation(5)
                    act.wait_ge(x1_stored, 2 * 16 * KD)
                    act.wait_ge(f_lo_made, KF)
                    act.wait_ge(blocks_done, BASE[0]["d"])
                    normed_stream(3, 5, x1_d[1])
                else:
                    act.wait_ge(out_stored, 16 * KD)
                    act.wait_ge(blocks_done, BASE[1]["d"])
                    for t in range(KD):
                        act.dma_start(x1_all[:, t, :], x1_d[1][t]).then_inc(x1_all_loaded, 16)
                    act.wait_ge(rstd_made, 7)
                    fn(dev[:], dev[:], ACT.Sqrt).then_inc(table_in, 1)
                    act.wait_ge(table_in, 1)
                rows_out(6 + h, BASE[h]["d"], len(DOWN), lambda: None)

            narrow_deviation(7)
            act.wait_ge(spread, 2)
            fn(rstd_b[:], ps[:, BK_RSTD, :], ACT.Copy).then_inc(rstd_copied, 1)
            for t in (0, 5, 1, 2, 6, 3, 4, 7):
                if t < DVE_LAST:
                    act.wait_ge(added, 3 * KD + t + 1)
                else:
                    act.wait_ge(pool_added, t - DVE_LAST + 1)
                act.dma_start(out_d[1][t], rows[:, t, :]).then_inc(out_stored, 16)
            act.wait_ge(out_stored, HALVES * 16 * KD)

        @block.vector
        def _(dve):
            tt, ts, stt = nc.vector.tensor_tensor, nc.vector.tensor_scalar, nc.vector.scalar_tensor_tensor

            def open_sum(n):
                wait_pos(dve, stat_mm, n)
                wait_pos(dve, summed, sum_base(n))
                nc.vector.memset(acc[:], 0.0).then_inc(summed, 1)

            def split_acc(n):
                dve.wait_ge(acc_hi_made, n + 1)
                dve.wait_ge(summed, sum_base(n + 1))
                tt(acc_lo[:], acc[:], rd(acc_hi_of(n)[:]), ALU.subtract).then_inc(acc_lo_made, 1)

            def add_square(n, t, sem_value):
                dve.wait_ge(*sem_value)
                dve.wait_ge(summed, t + (sum_base(n) + 1))
                tt(acc[:], acc[:], sq[:], ALU.add).then_inc(summed, 1)

            def invert(n):
                dve.wait_ge(dev_made, n + 1)
                nc.vector.reciprocal(rstd_of(n)[:], rstd_of(n)[:]).then_inc(rstd_made, 1)

            def normalise(k, gain, rstd, src, loaded):
                for t in range(KD):
                    dve.wait_ge(*loaded(t))
                    if t >= 2:
                        dve.wait_ge(h_lo_made, KD * k + t - 1)
                    stt(tmp[:, t % 2, :], src(t), col(gain, t), rstd, ALU.mult, ALU.mult)\
                        .then_inc(normed, 1)
                    if t >= 1:
                        norm_lo(k, t - 1)
                norm_lo(k, KD - 1)

            def norm_lo(k, t):
                dve.wait_ge(normed, KD * k + t + 1)
                dve.wait_ge(h_hi_made, KD * k + t + 1)
                tt(h_lo[:, t, :], tmp[:, t % 2, :], rd(h_hi[:, t, :]), ALU.subtract)\
                    .then_inc(h_lo_made, 1)

            def xs_at(s):
                return lambda t: (xs_loaded[t % 2], 16 * (4 * s + t // 2 + 1))

            def conv(h, j, q):
                J = j + KR * h
                dve.wait_ge(tap0, J + 1)
                for k in range(1, TAPS):
                    if k > 1:
                        dve.wait_ge(taps, J * 3 + (k - 1))
                    stt(uc[:, q, :], u_raw[:, k:k + T], col("conv_w", j + KR * k), uc[:, q, :],
                        ALU.mult, ALU.add).then_inc(taps, 1)

            def conv_lo(h, j, q):
                J = j + KR * h
                dve.wait_ge(uc_hi_made, J + 1)
                tt(uc_lo[:, q, :], uc[:, q, :], rd(uc_hi[:, q, :]), ALU.subtract)\
                    .then_inc(uc_lo_made, 1)

            def recurrence(h, j, q, beside=None):
                J = j + KR * h
                dve.wait_ge(i_made, J + 1)
                stt(g_i[:], g_i[:], 1.0, uc[:, q, :], ALU.add, ALU.mult).then_inc(iu_made, 1)
                dve.wait_ge(th1_made, J + 1)
                nc.vector.reciprocal(g_a[:], g_a[:]).then_inc(recip_made, 1)
                dve.wait_ge(root_made, J + 1)
                dve.wait_ge(recip_made, J + 1)
                tt(g_r[:], g_r[:], g_a[:], ALU.mult).then_inc(amp_made, 1)
                dve.wait_ge(amp_made, J + 1)
                dve.wait_ge(iu_made, J + 1)
                tt(g_i[:], g_i[:], g_r[:], ALU.mult).then_inc(b_made, 1)
                dve.wait_ge(b_made, J + 1)
                dve.wait_ge(a_made, J + 1)
                nc.vector.tensor_tensor_scan(g_h[:], g_a[:], g_i[:], h_carry[:, bass.ds(j, 1)],
                                             ALU.mult, ALU.add).then_inc(scanned, 1)
                dve.wait_ge(scanned, J + 1)
                own_wait(dve)
                nc.vector.tensor_copy(h_carry[:, bass.ds(j, 1)], g_h[:, T - 1:T]).then_inc(h_kept, 1)
                dve.wait_ge(gelu_made, J + 1)
                dve.wait_ge(h_kept, J + 1)
                tt(g_h[:], g_h[:], gy[:, q, :], ALU.mult).then_inc(lru_made, 1)
                if beside:
                    beside()
                dve.wait_ge(lru_hi_made, J + 1)
                dve.wait_ge(lru_made, J + 1)
                tt(lru_lo[:, bass.ds(j, 1), :], g_h[:], rd(lru_hi[:, bass.ds(j, 1), :]), ALU.subtract)\
                    .then_inc(lru_lo_made, 1)

            def recurrent(h):
                for j in range(2):
                    conv(h, j, j)
                    conv_lo(h, j, j)
                if h:
                    invert(2)
                    dve.wait_ge(rstd_made, 3)
                else:
                    prepare()
                open_sum(1 + 2 * h)
                for kd in (kd_hi, kd_lo):
                    for half in range(2):
                        r = slice(64 * half, 64 * half + 64)
                        nc.vector.memset(rd(kd[r, :, 1 - half, :]), 0.0).then_inc(kd_zeroed, 1)
                with dve.Fori(0, 2) as it:
                    for q in range(4):
                        j = it * 4 + (2 + q)
                        conv(h, j, (2 + q) % 4)
                        conv_lo(h, j, (2 + q) % 4)
                        recurrence(h, j - 2, q)

            def keys(c, C):
                wait_pos(dve, qk_done, C)
                own_wait(dve)
                for half in range(2):
                    r = slice(64 * half, 64 * half + 64)
                    nc.vector.tensor_copy(kd_lo[r, :, half, :], rd(k_lo[r, :, bass.ds(c * CH, 2 * CH)]))\
                        .then_inc(kd_lo_made, 1)

            def kvq(h):
                if h:
                    dve.wait_ge(pv_done, NCH)
                    nc.vector.tensor_copy(k_lo[:, :, 0:CH], rd(k_lo[:, :, T:T + CH])).then_inc(kept_lo, 1)
                    nc.vector.tensor_copy(v_lo[0:CH, 0], rd(v_lo[0:CH, NCH])).then_inc(kept_lo, 1)
                    dve.wait_ge(kept_lo, 2)
                else:
                    dve.wait_ge(zeroed, 6)

                def values(a):
                    dve.wait_ge(v_hi_made, 4 * h + a + 1)
                    tt(v_whole(v_lo, a), v_out(a), rd(v_whole(v_hi, a)), ALU.subtract)\
                        .then_inc(v_lo_made, 1)

                for p in range(PAIRS):
                    dve.wait_ge(k_hi_made, PAIRS * h + p + 1)
                    tt(k_lo[:, p, CH:CH + T], ps[:, BK_K[p], :], rd(k_hi[:, p, CH:CH + T]),
                       ALU.subtract).then_inc(k_lo_made, 1)
                    if p:
                        dve.wait_ge(k_lo_made, PAIRS * (h + 1))
                        keys(0, NCH * h)
                    recurrence(h, 8 + p, p, (lambda: values(0)) if p else None)
                values(1)
                with dve.Fori(0, KD // 2) as it:
                    for q in range(2):
                        t = it * 2 + q
                        dve.wait_ge(q_hi_made, t + (KD * h + 1))
                        tt(q_tile(q_lo, it, q), ps[:, q, :].rearrange("p (c t) -> p c t", t=CH),
                           rd(q_tile(q_hi, it, q)), ALU.subtract).then_inc(q_lo_made, 1)
                        if h:
                            add_norm(2, "g_post_mix", 0, 2, it, q)
                        add_square(1 + 2 * h, t, (squared, t + (sq_base(1 + 2 * h) + 1)))

            def attention(h):
                sink = par[:, PARAMS["sink"]:PARAMS["sink"] + 8]
                S = ps[:, BK_S:BK_S + 2, :].rearrange("p b (i k) -> p (b i) k", i=4)
                PT = ps[:, BK_PT:BK_PT + 2, :].rearrange("p b (i k) -> p (b i) k", i=4)

                def softmax_in(C):
                    dve.wait_ge(qk_done, C + 1)
                    wait_pos(dve, pt_done, C)
                    stt(prob[:], S, HD ** -0.5, alibi[:], ALU.mult, ALU.add).then_inc(biased, 1)
                    dve.wait_ge(biased, C + 1)
                    nc.vector.tensor_reduce(stat[:, 0, :], prob[:], AX_X, ALU.max).then_inc(maxed, 1)
                    dve.wait_ge(maxed, C * 4 + 1)
                    tt(stat[:, 0, :], stat[:, 0, :], sink, ALU.max).then_inc(maxed, 1)
                    dve.wait_ge(maxed, C * 4 + 2)
                    tt(stat[:, 1, :], sink, stat[:, 0, :], ALU.subtract).then_inc(maxed, 1)
                    ts(stat[:, 2, :], stat[:, 0, :], -1.0, None, ALU.mult).then_inc(maxed, 1)

                def softmax_out(C):
                    dve.wait_ge(exped, C * 9 + 9)
                    tt(stat[:, 3, :], stat[:, 3, :], stat[:, 4, :], ALU.add).then_inc(probed, 1)
                    dve.wait_ge(probed, C * 3 + 1)
                    nc.vector.reciprocal(stat[:, 5, :], stat[:, 3, :]).then_inc(probed, 1)
                    dve.wait_ge(probed, C * 3 + 2)
                    tt(prob[:], prob[:], stat[:, 5, :].rearrange("p (i o) -> p i o", o=1)
                       .broadcast_to([P, 8, 2 * CH]), ALU.mult).then_inc(probed, 1)

                def out_sum(C):
                    for half in range(2):
                        r = slice(HD * half, HD * half + HD)
                        dve.wait_ge(pv_parted, C * 2 + (half + 1))
                        tt(pv_sum[r, :], ps[r, BK_PV + half, :], pv_part[r, :], ALU.add)\
                            .then_inc(pv_summed, 1)

                def out_lo(c, C):
                    dve.wait_ge(ao_hi_made, C + 1)
                    dve.wait_ge(pv_summed, C * 2 + 2)
                    own_wait(dve)
                    q = (slice(None), slice(None), bass.ds(c * P, P))
                    tt(q_lo[q], pv_sum.rearrange("p (t q) -> p t q", q=P), rd(q_hi[q]), ALU.subtract)\
                        .then_inc(ao_lo_made, 1)

                def chunk(c, C, more=True):
                    softmax_in(C)
                    if more:
                        keys(c + 1, C + 1)
                    if isinstance(c, int) and c == 0:
                        dve.wait_ge(v_lo_made, 4 * h + 2)
                        nc.vector.tensor_copy(v_lo[CH:P, 0:NCH:2], rd(v_lo[0:CH, 1:NCH + 1:2]))\
                            .then_inc(v_lo_made, 1)
                        nc.vector.tensor_copy(v_lo[0:CH, 2:NCH + 1:2], rd(v_lo[CH:P, 1:NCH + 1:2]))\
                            .then_inc(v_lo_made, 1)
                    softmax_out(C)
                    if not isinstance(c, int) or c:
                        out_sum(C - 1)
                        out_lo(c - 1, C - 1)
                    dve.wait_ge(ga_made, C + 1)
                    dve.wait_ge(blocks_done, c * 8 + (BASE[h]["a"] + 8))
                    if h and isinstance(c, int) and c == 0:
                        dve.wait_ge(x1_stored, 16 * KD)
                    stt(rows[:, bass.ds(c, 1), :], xs[:, 0, :], 1.0, ps[:, 1, :], ALU.add, ALU.mult)\
                        .then_inc(lru_part, 1)
                    dve.wait_ge(pt_hi_made, C + 1)
                    tt(pt_lo[:], PT, rd(pt_hi[:]), ALU.subtract).then_inc(pt_lo_made, 1)

                dve.wait_ge(alibi_loaded, 16)
                chunk(0, NCH * h)
                split_acc(1 + 2 * h)
                dve.wait_ge(alibi_loaded, 32)
                with dve.Fori(1, NCH - 1) as c:
                    chunk(c, c + NCH * h)
                chunk(NCH - 1, NCH * (h + 1) - 1, False)
                out_sum(NCH * (h + 1) - 1)
                out_lo(NCH - 1, NCH * (h + 1) - 1)

            def attn_branch(h):
                def tile(c, C):
                    dve.wait_ge(gb_made, C + 1)
                    dve.wait_ge(blocks_done, c * 4 + (BASE[h]["b"] + 4))
                    stt(tmp[:, 1, :], tmp[:, 0, :], 1.0, ps[:, 1, :], ALU.add, ALU.mult)\
                        .then_inc(attn_part, 1)
                    dve.wait_ge(attn_part, C + 1)
                    tt(tmp[:, 1, :], tmp[:, 1, :], rows[:, bass.ds(c, 1), :], ALU.add).then_inc(merged, 1)
                    dve.wait_ge(mg_hi_made, C + 1)
                    stt(mg_lo[:, bass.ds(c, 1), :], tmp[:, 1, :], 0.5, rd(mg_hi[:, bass.ds(c, 1), :]),
                        ALU.mult, ALU.subtract).then_inc(mg_lo_made, 1)

                tile(0, KD * h)
                invert(1 + 2 * h)
                with dve.Fori(1, KD) as c:
                    dve.wait_ge(mg_lo_made, c + KD * h)
                    tile(c, c + KD * h)

            def rows_in(n, r0, between):
                open_sum(n)
                for t in range(2):
                    add_square(n, t, (row_out, 2 * (r0 + t) + 1))
                between()
                with dve.Fori(2, KD - (n == 7)) as t:
                    add_square(n, t, (row_out, t * 2 + (2 * r0 + 1)))
                if n != 7:
                    split_acc(n)

            def add_norm(n, gain, a0, s, it, q):
                c = it * 2 + q
                stt(rows[:, bass.ds(c, 1), :], rows[:, bass.ds(c, 1), :], col(gain, c), rstd_of(n)[:],
                    ALU.mult, ALU.mult).then_inc(scaled, 1)
                dve.wait_ge(scaled, c + (a0 + 1))
                dve.wait_ge(xs_loaded[q], it * 16 + (64 * s + 16))
                tt(rows[:, bass.ds(c, 1), :], rows[:, bass.ds(c, 1), :], xs[:, q, :], ALU.add)\
                    .then_inc(added, 1)

            def sq_base(n):
                return KD * {0: 0, 1: 1, 3: 2, 5: 3}[n]

            def prepare():
                dve.wait_ge(par_loaded, 32)
                done = [0]

                def step(ins):
                    done[0] += 1
                    ins.then_inc(prep_dve, 1)
                    dve.wait_ge(prep_dve, done[0])

                step(ts(half_b[:], par[:, HALVED:N_PARAMS], 0.5, None, ALU.mult))
                dve.wait_ge(prep_act, 2)
                e, s, s2, poly = sp[:, 1, :], sp[:, 0, :], sp[:, 2, :], sp[:, 3, :]
                step(ts(s, e, 2.0, None, ALU.add))
                step(nc.vector.reciprocal(s2, s))
                step(tt(s, e, s2, ALU.mult))
                step(tt(s2, s, s, ALU.mult))
                step(ts(poly, s2, 1.0 / 17, None, ALU.mult))
                for m in (15, 13, 11, 9, 7, 5, 3):
                    step(stt(poly, poly, 1.0 / m, s2, ALU.add, ALU.mult))
                step(stt(poly, poly, 1.0, s, ALU.add, ALU.mult))
                step(ts(s2, par[:, PARAMS["lam"]:PARAMS["lam"] + KR], -2.0, 0.0, ALU.mult, ALU.max))
                step(stt(sp2[:], poly, 4.0, s2, ALU.mult, ALU.add))
                assert done[0] == PREP_STEPS

            def narrow_invert(n):
                dve.wait_ge(dev_made, n + 1)
                nc.vector.reciprocal(dev[:], dev[:]).then_inc(rstd_made, 1)
                dve.wait_ge(rstd_made, n + 1)
                tt(rstd_a.rearrange("p (m t) -> p m t", t=P),
                   dev.rearrange("p (m o) -> p m o", o=1).broadcast_to([P, T // P, P]),
                   eye.rearrange("p (o t) -> p o t", o=1).broadcast_to([P, T // P, P]), ALU.mult)\
                    .then_inc(diag_made, 1)

            for t in range(1, KD):
                dve.wait_ge(squared, t + 1)
                if t > 1:
                    dve.wait_ge(summed_0, t - 1)
                tt(acc[:], acc[:] if t > 1 else x1_all[:, 0, :], x1_all[:, t, :], ALU.add)\
                    .then_inc(summed_0, 1)
            dve.wait_ge(par_loaded, 32)
            narrow_invert(0)
            dve.wait_ge(spread, 1)
            normalise(0, "g_pre_mix", ps[:, BK_RSTD, :], lambda t: rows[:, t, :], lambda t: (x0_loaded[t], 16))

            for h in range(HALVES):
                recurrent(h)
                kvq(h)
                attention(h)
                attn_branch(h)
                dve.wait_ge(mg_lo_made, KD * (h + 1))
                if h == 0:
                    rows_in(2, 0, lambda: normalise(1, "g_pre_mix", rstd_b[:],
                                                    lambda t: xs[:, t % 2, :], xs_at(1)))
                else:
                    rows_in(4, KD, lambda: normalise(2, "g_pre_ffn", rstd_b[:],
                                                     lambda t: xs[:, t % 2, :], xs_at(3)))
            for h in range(HALVES):
                def tile(t, F):
                    dve.wait_ge(silu_made, F + 1)
                    dve.wait_ge(blocks_done, t * 4 + (BASE[h]["f"] + 4))
                    if not isinstance(F, int) or F:
                        dve.wait_ge(f_lo_made, F)
                    tt(tmp[:, 1, :], ps[:, 1, :], tmp[:, 0, :], ALU.mult).then_inc(f_made, 1)
                    dve.wait_ge(f_hi_made, F + 1)
                    dve.wait_ge(f_made, F + 1)
                    tt(f_lo[:, bass.ds(t, 1), :], tmp[:, 1, :], rd(f_hi[:, bass.ds(t, 1), :]),
                       ALU.subtract).then_inc(f_lo_made, 1)

                for t in range(2):
                    tile(t, KF * h + t)
                invert(4 + 2 * h)
                if h == 0:
                    open_sum(5)
                dve.wait_ge(rstd_made, 5 + 2 * h)
                with dve.Fori(0, KD // 2) as it:
                    for q in range(2):
                        t, c = it * 2 + (2 + q), it * 2 + q
                        tile(t, t + KF * h)
                        if h == 0:
                            add_norm(4, "g_post_mix", KD, 4, it, q)
                            add_square(5, c, (squared, c + (sq_base(5) + 1)))
                        else:
                            add_norm(6, "g_post_ffn", 2 * KD, 6, it, q)
                if h == 0:
                    split_acc(5)
                with dve.Fori(KD + 2, KF) as t:
                    tile(t, t + KF * h)
                if h == 0:
                    dve.wait_ge(f_lo_made, KF)
                    invert(5)
                    dve.wait_ge(rstd_made, 6)
                    normalise(3, "g_pre_ffn", rstd_b[:], lambda t: xs[:, t % 2, :], xs_at(5))
                rows_in(6 + h, 16 + KD * h, lambda: None)
            narrow_invert(7)
            dve.wait_ge(rstd_copied, 1)
            for t in range(DVE_LAST):
                tt(rows[:, t, :], rows[:, t, :], rstd_b[:], ALU.mult).then_inc(scaled, 1)
                dve.wait_ge(x1_all_loaded, 16 * KD)
                dve.wait_ge(scaled, 3 * KD + t + 1)
                tt(rows[:, t, :], rows[:, t, :], x1_all[:, t, :], ALU.add).then_inc(added, 1)


def k_tiles(w):
    return w.reshape(-1, P, w.shape[1]).transpose(1, 0, 2)


def cols(w, c):
    return k_tiles(w[:, c * P:(c + 1) * P]).reshape(P, -1)


def weight_streams(w_in, w_rg, w_ig, w_lru_br, w_attn_br, w_out, w_gate, w_up, w_down):
    bounds = np.cumsum([0, D_RNN, D_RNN, HEADS * HD, D_KV, D_KV, D, D])
    u, y, q, k, v, gl, ga = [w_in[:, bounds[i]:bounds[i + 1]] for i in range(7)]
    order = [(2 * p + half) * GRP + a for p in range(PAIRS) for a in range(GRP) for half in range(2)]
    q = q.reshape(D, HEADS, HD)[:, order].reshape(D, -1)
    w_attn_br = w_attn_br.reshape(HEADS, HD, D)[order].reshape(-1, D)

    def gate(w, j):
        full = np.zeros((D_RNN + 2 * P, D_RNN), w.dtype)
        for b in range(N_BLK):
            full[P + b * BLK:P + (b + 1) * BLK, b * BLK:(b + 1) * BLK] = w[b]
        first, last = (1, 3) if j == 0 else (0, 2) if j in (4, 9) else (0, 3)
        part = full[(j + first) * P:(j + last) * P, j * P:(j + 1) * P]
        return k_tiles(part).reshape(P, -1)

    def cat(*parts):
        return np.concatenate(parts, axis=1)

    return {
        "head": np.stack([cat(*[cols(m, j)[:, b * CAP:(b + 1) * CAP] for b in range(2) for m in (u, y)])
                          for j in range(2)]),
        "step": np.stack([cat(*[x for jj in range(j, j + 4)
                                for x in (cols(u, jj), gate(w_rg, jj - 2), gate(w_ig, jj - 2), cols(y, jj))])
                          for j in range(2, KR, 4)]),
        "tail": cat(cols(k, 0), gate(w_rg, 8), gate(w_ig, 8),
                    cols(k, 1), gate(w_rg, 9), gate(w_ig, 9))[None],
        "v": k_tiles(v).reshape(P, -1)[None],
        "q": np.stack([cat(cols(q, t), cols(q, t + 1)) for t in range(0, KD, 2)]),
        "a": np.stack([cat(cols(gl, c), cols(w_lru_br, c)) for c in range(KD)]),
        "b": np.stack([cat(cols(ga, c), cols(w_attn_br, c)) for c in range(KD)]),
        "o": np.stack([cat(cols(w_out, t), cols(w_out, t + 1)) for t in range(0, KD, 2)]),
        "f": np.stack([cat(cols(w_gate, t), cols(w_up, t)) for t in range(KF)]),
        "d": np.stack([cat(cols(w_down, t), cols(w_down, t + 1)) for t in range(0, KD, 2)]),
    }


def by_tile(v):
    return v.reshape(-1, P).T


def score_heads():
    p = np.arange(P)[:, None]
    i = np.arange(8)[None, :]
    pair, b, half = i // 4, i // 2 % 2, i % 2
    return (2 * pair + half) * GRP + 2 * b + p // CH


def alibi_tables():
    slope = np.exp2(-8.0 * (np.arange(HEADS, dtype=np.float32) + 1) / HEADS).astype(np.float32)
    qi = np.arange(P)[:, None] % CH
    dist = np.abs(qi + CH - np.arange(2 * CH)[None, :]).astype(np.float32)
    table = -slope[score_heads()][:, :, None] * dist[:, None, :]
    masked = table.copy()
    masked[:, :, :CH] = MASKED
    return np.stack([masked, table]).astype(np.float32)


def kernel(**inputs):
    import concourse.bacc as bacc
    from concourse.bass_utils import run_bass_kernel_spmd as run

    a = {k: np.asarray(v) for k, v in inputs.items()}
    one = {k: v[0] for k, v in a.items()}
    table = [by_tile(one["norm_pre_mix"]), by_tile(one["norm_post_mix"]),
             by_tile(one["norm_pre_ffn"]), by_tile(one["norm_post_ffn"]),
             np.concatenate([by_tile(one["conv_w"][k]) for k in range(TAPS)], axis=1),
             by_tile(one["conv_b"]), by_tile(one["lru_lambda"]), one["attn_sinks"][score_heads()],
             by_tile(one["b_rg"]), by_tile(one["b_ig"]),
             by_tile(one["b_gate"][:D]), by_tile(one["b_gate"][D:])]
    arrays = {
        "x_t": one["x"].T.reshape(KD, P, HALVES, T).transpose(2, 0, 1, 3),
        "params": np.concatenate(table, axis=1),
        "alibi_in": alibi_tables(),
        "eye_in": np.eye(P, dtype=np.float32),
    }
    streams = weight_streams(one["w_in"], one["w_rg"], one["w_ig"], one["w_lru_br"],
                             one["w_attn_br"], one["w_out"], one["w_ffn_gate"], one["w_ffn_up"],
                             one["w_ffn_down"])
    arrays.update({f"w_{name}": w for name, w in streams.items()})
    arrays = {k: np.ascontiguousarray(v) for k, v in arrays.items()}

    nc = bacc.Bacc("TRN2", target_bir_lowering=False, num_devices=1)
    dram = {k: nc.dram_tensor(k, v.shape, F32, kind="ExternalInput").ap() for k, v in arrays.items()}
    x1 = nc.dram_tensor("x1_scratch", (HALVES, KD, P, T), F32).ap()
    out = nc.dram_tensor("out_t", (HALVES, KD, P, T), F32, kind="ExternalOutput").ap()
    build(nc, dram["x_t"], dram["params"], dram["alibi_in"], dram["eye_in"],
          {name: dram[f"w_{name}"] for name in streams}, x1, out)
    r = run(nc, [arrays], core_ids=[0])
    got = r.results[0]["out_t"]
    return np.ascontiguousarray(got.transpose(0, 3, 1, 2).reshape(1, SEQ, D))
```
